# Optimizing a Trainium2 kernel written in Bass

```python
import jax, jax.numpy as jnp
from jax import lax
import numpy as np

D_MODEL = 2048
BATCH = 1
SEQ = 512
DEPTH = 1
DEC_BATCH = 8
DEC_SEQ = 4
PAST_LEN = 2048
PAGE_SIZE = 128

A_HEADS = 16
A_HEAD_DIM = 64
A_WIDTH = A_HEADS * A_HEAD_DIM
DECAY_RANK = 64
ICLR_RANK = 64
A_COLS = 4 * A_WIDTH + DECAY_RANK + ICLR_RANK
GN_EPS = 64e-5
B_HEADS = 16
B_KV_HEADS = 4
B_GROUP = B_HEADS // B_KV_HEADS
B_HEAD_DIM = 64
B_WIDTH = B_HEADS * B_HEAD_DIM
B_KV_WIDTH = B_KV_HEADS * B_HEAD_DIM
B_COLS = 2 * B_WIDTH + 6 * B_KV_WIDTH + 3 * B_HEADS
CMP_BLOCK = 32
CMP_STRIDE = 16
SEL_BLOCK = 64
N_SELECT = 16
N_LOCAL = 2
WINDOW = 512
Q_BLOCK = 128
SEL_Q_BLOCK = 16
FORCED_SCORE = 1e4
ATTN_SCALE = B_HEAD_DIM ** -0.5
IN_COLS = A_COLS + B_COLS + 2 * D_MODEL
RMS_EPS = 1e-6
NEG = -1e30

kernel_name = 'hybrid_rwkv7_nsa_step'

def rms_norm(x, g):
    xf = x.astype(jnp.float32)
    y = xf * lax.rsqrt(jnp.mean(xf * xf, axis=-1, keepdims=True) + RMS_EPS)
    return (y * g.astype(jnp.float32)).astype(x.dtype)

def masked_softmax(s, mask):
    s = jnp.where(mask, s, NEG)
    m = jnp.max(s, axis=-1, keepdims=True)
    p = jnp.where(mask, jnp.exp(s - m), 0.0)
    return p / jnp.maximum(jnp.sum(p, axis=-1, keepdims=True), 1e-30)

def alibi_slopes():
    h = jnp.arange(1, B_HEADS + 1, dtype=jnp.float32)
    return jnp.exp2(-8.0 * h / B_HEADS).reshape(B_KV_HEADS, B_GROUP)

def rwkv7_mixer(u, u_prev0, S0, mu_shift, w0, w_up, a0, a_up, k_k, k_a, r_k, gn_w, gn_b):
    f32 = jnp.float32
    B, T, _ = u.shape
    H, N = A_HEADS, A_HEAD_DIM
    u_prev = jnp.concatenate([u_prev0[:, None].astype(u.dtype), u[:, :-1]], axis=1)
    us = u + mu_shift * (u_prev - u)
    r, k, v, g, wd, ad = jnp.split(us, [A_WIDTH, 2 * A_WIDTH, 3 * A_WIDTH, 4 * A_WIDTH,
                                        4 * A_WIDTH + DECAY_RANK], axis=-1)
    w_log = -jax.nn.softplus(-(w0 + jnp.tanh(wd) @ w_up).astype(f32)) - 0.5
    decay = jnp.exp(-jnp.exp(w_log))
    a = jax.nn.sigmoid((a0 + ad @ a_up).astype(f32))
    r, k, v = r.astype(f32), k.astype(f32), v.astype(f32)
    kk = (k * k_k).reshape(B, T, H, N)
    kk = kk * lax.rsqrt(jnp.maximum(jnp.sum(kk * kk, axis=-1, keepdims=True), 1e-24))
    k = k * (1.0 + (a - 1.0) * k_a)
    r, k, v, a, decay = (t.reshape(B, T, H, N) for t in (r, k, v, a, decay))

    def step(S, inp):
        r_t, k_t, v_t, kk_t, a_t, w_t = inp
        sa = jnp.einsum('bhij,bhj->bhi', S, kk_t)
        S = (S * w_t[:, :, None, :] - sa[..., None] * (kk_t * a_t)[:, :, None, :]
             + v_t[..., None] * k_t[:, :, None, :])
        return S, jnp.einsum('bhij,bhj->bhi', S, r_t)

    xs = tuple(jnp.moveaxis(t, 1, 0) for t in (r, k, v, kk, a, decay))
    S, o = lax.scan(step, S0.astype(f32), xs)
    o = jnp.moveaxis(o, 0, 1)
    mean = jnp.mean(o, axis=-1, keepdims=True)
    var = jnp.mean(jnp.square(o - mean), axis=-1, keepdims=True)
    o = (o - mean) * lax.rsqrt(var + GN_EPS) * gn_w.reshape(H, N) + gn_b.reshape(H, N)
    o = o + jnp.sum(r * k * r_k, axis=-1, keepdims=True) * v
    o = o.reshape(B, T, A_WIDTH) * jax.nn.silu(g.astype(f32))
    return o.astype(u.dtype), S.astype(u.dtype), u[:, -1]

def compress_blocks(rows, pos_w, w_c):
    B, L, G, D = rows.shape
    ratio = CMP_BLOCK // CMP_STRIDE
    n_ch = L // CMP_STRIDE
    n_cmp = n_ch - ratio + 1
    chunks = rows[:, :n_ch * CMP_STRIDE].reshape(B, n_ch, CMP_STRIDE, G, D)
    pw = pos_w.reshape(ratio, CMP_STRIDE, D)
    pooled = jnp.einsum('bnsgd,sd->bngd', chunks[:, :n_cmp], pw[0])
    for i in range(1, ratio):
        pooled = pooled + jnp.einsum('bnsgd,sd->bngd', chunks[:, i:i + n_cmp], pw[i])
    return jnp.einsum('bngd,de->bnge', pooled, w_c)

def compressed_attention(q, kv, t_pos, slopes, cmp_pos_k, cmp_pos_v, w_cmp_k, w_cmp_v):
    f32 = jnp.float32
    kc = compress_blocks(kv[:, :, 0], cmp_pos_k, w_cmp_k)
    vc = compress_blocks(kv[:, :, 1], cmp_pos_v, w_cmp_v)
    n_cmp = kc.shape[1]
    blk_end = jnp.arange(n_cmp) * CMP_STRIDE + (CMP_BLOCK - 1)
    dist = t_pos[:, None] - blk_end[None, :]
    s = jnp.einsum('btgrd,bngd->btgrn', q, kc, preferred_element_type=f32) * ATTN_SCALE
    s = s - slopes[None, None, :, :, None] * dist[None, :, None, None, :]
    p = masked_softmax(s, (dist >= 0)[None, :, None, None, :])
    o = jnp.einsum('btgrn,bngd->btgrd', p, vc.astype(f32))
    return o, p

def select_blocks(p_cmp, t_pos, L):
    f32 = jnp.float32
    n_cmp = p_cmp.shape[-1]
    n_sel = -(-L // SEL_BLOCK)
    cs = jnp.arange(n_cmp) * CMP_STRIDE
    ss = jnp.arange(n_sel) * SEL_BLOCK
    overlap = jnp.clip(jnp.minimum(cs[:, None] + CMP_BLOCK, ss[None, :] + SEL_BLOCK)
                       - jnp.maximum(cs[:, None], ss[None, :]), 0, None).astype(f32) / CMP_BLOCK
    imp = jnp.einsum('btgrn,nj->btgj', p_cmp, overlap)
    j = jnp.arange(n_sel)
    back = (t_pos // SEL_BLOCK)[:, None] - j[None, :]
    forced = (j[None, :] == 0) | ((back >= 0) & (back < N_LOCAL))
    score = jnp.where(forced[None, :, None], FORCED_SCORE,
                      jnp.where((back >= 0)[None, :, None], imp, -1.0))
    top_s, top_i = lax.top_k(score, min(N_SELECT, n_sel))
    return top_i, top_s >= 0

def selected_attention(q, kv, top_i, top_ok, t_pos, slopes):
    f32 = jnp.float32
    B, T, G, R, D = q.shape
    L = kv.shape[1]
    n_sel = -(-L // SEL_BLOCK)
    kv = jnp.pad(kv, ((0, 0), (0, n_sel * SEL_BLOCK - L), (0, 0), (0, 0), (0, 0)))
    blocks = kv.reshape(B, n_sel, SEL_BLOCK, 2, G, D).transpose(0, 4, 1, 2, 3, 5)
    qb = SEL_Q_BLOCK if T % SEL_Q_BLOCK == 0 else T
    nqb = T // qb
    b_idx = jnp.arange(B)[:, None, None, None]
    g_idx = jnp.arange(G)[None, None, :, None]
    offs = jnp.arange(SEL_BLOCK)

    def to_blocks(a):
        return jnp.moveaxis(a.reshape((B, nqb, qb) + a.shape[2:]), 1, 0)

    def one_block(args):
        q_b, i_b, ok_b, pos_b = args
        nk = i_b.shape[-1] * SEL_BLOCK
        kvg = blocks[b_idx, g_idx, i_b]
        k_pos = i_b[..., None] * SEL_BLOCK + offs
        dist = (pos_b[None, :, None, None, None] - k_pos).reshape(B, qb, G, 1, nk)
        mask = (dist >= 0) & ok_b[..., None].repeat(SEL_BLOCK, axis=-1).reshape(B, qb, G, 1, nk)
        kg = kvg[..., 0, :].reshape(B, qb, G, nk, D)
        vg = kvg[..., 1, :].reshape(B, qb, G, nk, D)
        s = jnp.einsum('bqgrd,bqgnd->bqgrn', q_b, kg, preferred_element_type=f32) * ATTN_SCALE
        s = s - slopes[None, None, :, :, None] * dist
        p = masked_softmax(s, mask)
        return jnp.einsum('bqgrn,bqgnd->bqgrd', p, vg.astype(f32))

    o = lax.map(one_block, (to_blocks(q), to_blocks(top_i), to_blocks(top_ok), t_pos.reshape(nqb, qb)))
    return jnp.moveaxis(o, 0, 1).reshape(B, T, G, R, D)

def window_attention(q, kv, q_pos0, slopes):
    f32 = jnp.float32
    B, T, G, R, D = q.shape
    Lw = kv.shape[1]
    qb = Q_BLOCK if T % Q_BLOCK == 0 else T
    nqb = T // qb
    band = WINDOW + qb
    kvp = jnp.pad(kv, ((0, 0), (WINDOW, 0), (0, 0), (0, 0), (0, 0)))
    k_pos0 = q_pos0 + T - Lw
    q_blocks = jnp.moveaxis(q.reshape(B, nqb, qb, G, R, D), 1, 0)

    def one_block(args):
        i, q_b = args
        start = Lw - T + i * qb
        kv_b = lax.dynamic_slice_in_dim(kvp, start, band, axis=1)
        k_pos = k_pos0 - WINDOW + start + jnp.arange(band)
        q_pos = q_pos0 + i * qb + jnp.arange(qb)
        dist = q_pos[:, None] - k_pos[None, :]
        mask = (dist >= 0) & (dist <= WINDOW) & (k_pos >= k_pos0)[None, :]
        s = jnp.einsum('bqgrd,bkgd->bqgrk', q_b, kv_b[:, :, 0], preferred_element_type=f32) * ATTN_SCALE
        s = s - slopes[None, None, :, :, None] * dist[None, :, None, None, :]
        p = masked_softmax(s, mask[None, :, None, None, :])
        return jnp.einsum('bqgrk,bkgd->bqgrd', p, kv_b[:, :, 1].astype(f32))

    o = lax.map(one_block, (jnp.arange(nqb), q_blocks))
    return jnp.moveaxis(o, 0, 1).reshape(B, T, G, R, D)

def nsa_mixer(q, gates, cmp_kv, sel_kv, win_kv, q_pos0, cmp_pos_k, cmp_pos_v, w_cmp_k, w_cmp_v):
    f32 = jnp.float32
    B, T, _ = q.shape
    q = q.reshape(B, T, B_KV_HEADS, B_GROUP, B_HEAD_DIM)
    t_pos = q_pos0 + jnp.arange(T)
    slopes = alibi_slopes()
    o_cmp, p_cmp = compressed_attention(q, cmp_kv, t_pos, slopes, cmp_pos_k, cmp_pos_v, w_cmp_k, w_cmp_v)
    top_i, top_ok = select_blocks(p_cmp, t_pos, sel_kv.shape[1])
    o_sel = selected_attention(q, sel_kv, top_i, top_ok, t_pos, slopes)
    o_win = window_attention(q, win_kv, q_pos0, slopes)
    g = jax.nn.sigmoid(gates.astype(f32)).reshape(B, T, 3, B_KV_HEADS, B_GROUP, 1)
    o = g[:, :, 0] * o_cmp + g[:, :, 1] * o_sel + g[:, :, 2] * o_win
    return o.reshape(B, T, B_WIDTH)

def hybrid_layer(x, u_prev0, S0, cmp_past, sel_past, win_buf, q_pos0, win_keep,
                 norm_in, w_in, mu_shift, w0, w_up, a0, a_up, k_k, k_a, r_k, gn_w, gn_b,
                 cmp_pos_k, cmp_pos_v, w_cmp_k, w_cmp_v, w_pa, w_pb, w_o):
    f32 = jnp.float32
    B, T, _ = x.shape
    xn = rms_norm(x, norm_in)
    u = jnp.einsum('btd,dc->btc', xn, w_in)
    u_a, u_b, u_m = jnp.split(u, [A_COLS, A_COLS + B_COLS], axis=-1)
    o_a, S_new, shift_new = rwkv7_mixer(u_a, u_prev0, S0, mu_shift, w0, w_up, a0, a_up,
                                        k_k, k_a, r_k, gn_w, gn_b)
    q, g_b, kv_c, kv_s, kv_w, nsa_gates = jnp.split(
        u_b, [B_WIDTH, 2 * B_WIDTH, 2 * B_WIDTH + 2 * B_KV_WIDTH,
              2 * B_WIDTH + 4 * B_KV_WIDTH, 2 * B_WIDTH + 6 * B_KV_WIDTH], axis=-1)
    new_c = kv_c.reshape(B, T, 2, B_KV_HEADS, B_HEAD_DIM)
    new_s = kv_s.reshape(B, T, 2, B_KV_HEADS, B_HEAD_DIM)
    new_w = kv_w.reshape(B, T, 2, B_KV_HEADS, B_HEAD_DIM)
    cmp_all = jnp.concatenate([cmp_past.astype(x.dtype), new_c], axis=1)
    sel_all = jnp.concatenate([sel_past.astype(x.dtype), new_s], axis=1)
    win_all = jnp.concatenate([win_buf.astype(x.dtype), new_w], axis=1)
    o_b = nsa_mixer(q, nsa_gates, cmp_all, sel_all, win_all, q_pos0, cmp_pos_k, cmp_pos_v, w_cmp_k, w_cmp_v)
    o_b = (o_b * jax.nn.silu(g_b.astype(f32))).astype(x.dtype)
    gate_a, gate_b = jnp.split(jax.nn.sigmoid(u_m.astype(f32)), 2, axis=-1)
    merged = gate_a * (o_a @ w_pa) + gate_b * (o_b @ w_pb)
    h = x + merged.astype(x.dtype) @ w_o
    return h, new_c, new_s, win_all[:, win_all.shape[1] - win_keep:], S_new, shift_new

def setup_inputs(seed: int = 0) -> dict:
    key = jax.random.key(seed)
    ks = jax.random.split(key, 32)
    f32 = jnp.float32

    def nrm(k, shape, scale):
        return scale * jax.random.normal(k, shape, f32)

    n_pages = PAST_LEN // PAGE_SIZE
    n_used = DEC_BATCH * n_pages
    n_pool = n_used + n_used // 4
    win_keep = min(WINDOW, PAST_LEN)
    L = DEPTH
    kvs = (2, B_KV_HEADS, B_HEAD_DIM)
    return {
        'x_prompt': nrm(ks[0], (BATCH, SEQ, D_MODEL), 1.0),
        'x_sample': nrm(ks[1], (DEC_BATCH, DEC_SEQ, D_MODEL), 1.0),
        'cache_cmp_kv': nrm(ks[2], (L, n_pool, PAGE_SIZE) + kvs, 1.0),
        'cache_sel_kv': nrm(ks[3], (L, n_pool, PAGE_SIZE) + kvs, 1.0),
        'cache_win_kv': nrm(ks[4], (L, DEC_BATCH, win_keep) + kvs, 1.0),
        'state_rwkv': nrm(ks[5], (L, DEC_BATCH, A_HEADS, A_HEAD_DIM, A_HEAD_DIM), 0.5),
        'state_shift': nrm(ks[6], (L, DEC_BATCH, A_COLS), 1.0),
        'page_table': jax.random.permutation(ks[7], n_pool)[:n_used].reshape(DEC_BATCH, n_pages).astype(jnp.int32),
        'norm_in': 1.0 + nrm(ks[8], (L, D_MODEL), 0.05),
        'w_in': nrm(ks[9], (L, D_MODEL, IN_COLS), D_MODEL ** -0.5),
        'mu_shift': jax.random.uniform(ks[10], (L, A_COLS), f32, 0.1, 0.9),
        'w0': jax.random.uniform(ks[11], (L, A_WIDTH), f32, -6.0, -1.0),
        'w_up': nrm(ks[12], (L, DECAY_RANK, A_WIDTH), 0.1 * DECAY_RANK ** -0.5),
        'a0': nrm(ks[13], (L, A_WIDTH), 0.5),
        'a_up': nrm(ks[14], (L, ICLR_RANK, A_WIDTH), ICLR_RANK ** -0.5),
        'k_k': 0.85 + nrm(ks[15], (L, A_WIDTH), 0.05),
        'k_a': 1.0 + nrm(ks[16], (L, A_WIDTH), 0.05),
        'r_k': nrm(ks[17], (L, A_HEADS, A_HEAD_DIM), 0.1),
        'gn_w': 1.0 + nrm(ks[18], (L, A_WIDTH), 0.05),
        'gn_b': nrm(ks[19], (L, A_WIDTH), 0.02),
        'cmp_pos_k': (1.0 + nrm(ks[20], (L, CMP_BLOCK, B_HEAD_DIM), 0.1)) * CMP_BLOCK ** -0.5,
        'cmp_pos_v': (1.0 + nrm(ks[21], (L, CMP_BLOCK, B_HEAD_DIM), 0.1)) * CMP_BLOCK ** -0.5,
        'w_cmp_k': nrm(ks[22], (L, B_HEAD_DIM, B_HEAD_DIM), B_HEAD_DIM ** -0.5),
        'w_cmp_v': nrm(ks[23], (L, B_HEAD_DIM, B_HEAD_DIM), B_HEAD_DIM ** -0.5),
        'w_pa': nrm(ks[24], (L, A_WIDTH, D_MODEL), A_WIDTH ** -0.5),
        'w_pb': nrm(ks[25], (L, B_WIDTH, D_MODEL), B_WIDTH ** -0.5),
        'w_o': nrm(ks[26], (L, D_MODEL, D_MODEL), D_MODEL ** -0.5),
        'norm_out': 1.0 + nrm(ks[27], (D_MODEL,), 0.05),
    }

def reference(x_prompt, x_sample, cache_cmp_kv, cache_sel_kv, cache_win_kv, state_rwkv, state_shift,
              page_table, norm_in, w_in, mu_shift, w0, w_up, a0, a_up, k_k, k_a, r_k, gn_w, gn_b,
              cmp_pos_k, cmp_pos_v, w_cmp_k, w_cmp_v, w_pa, w_pb, w_o, norm_out):
    f32 = jnp.float32
    B, T, _ = x_prompt.shape
    DB = x_sample.shape[0]
    n_pages = page_table.shape[1]
    past_len = n_pages * PAGE_SIZE
    dt = x_prompt.dtype
    empty = jnp.zeros((B, 0, 2, B_KV_HEADS, B_HEAD_DIM), dt)
    h_p, h_s = x_prompt, x_sample
    outs_p = [[] for _ in range(5)]
    outs_s = [[] for _ in range(5)]
    for l in range(DEPTH):
        lw = (norm_in[l], w_in[l], mu_shift[l], w0[l], w_up[l], a0[l], a_up[l], k_k[l], k_a[l], r_k[l],
              gn_w[l], gn_b[l], cmp_pos_k[l], cmp_pos_v[l], w_cmp_k[l], w_cmp_v[l], w_pa[l], w_pb[l], w_o[l])
        res_p = hybrid_layer(h_p, jnp.zeros((B, A_COLS), dt),
                             jnp.zeros((B, A_HEADS, A_HEAD_DIM, A_HEAD_DIM), f32),
                             empty, empty, empty, 0, min(WINDOW, T), *lw)
        h_p = res_p[0]
        for acc, val in zip(outs_p, res_p[1:]):
            acc.append(val)
        past_c = cache_cmp_kv[l][page_table].reshape(DB, past_len, 2, B_KV_HEADS, B_HEAD_DIM)
        past_s = cache_sel_kv[l][page_table].reshape(DB, past_len, 2, B_KV_HEADS, B_HEAD_DIM)
        res_s = hybrid_layer(h_s, state_shift[l], state_rwkv[l], past_c, past_s, cache_win_kv[l],
                             past_len, cache_win_kv.shape[2], *lw)
        h_s = res_s[0]
        for acc, val in zip(outs_s, res_s[1:]):
            acc.append(val)
    y_prompt = rms_norm(h_p, norm_out)
    y_sample = rms_norm(h_s, norm_out)
    return (y_prompt, y_sample,
            jnp.stack(outs_p[0]), jnp.stack(outs_p[1]), jnp.stack(outs_p[2]), jnp.stack(outs_p[3]), jnp.stack(outs_p[4]),
            jnp.stack(outs_s[0]), jnp.stack(outs_s[1]), jnp.stack(outs_s[2]), jnp.stack(outs_s[3]), jnp.stack(outs_s[4]))


_drawn_inputs = setup_inputs


def setup_inputs(seed=0):
    import zlib

    import numpy as np

    out = dict(_drawn_inputs(seed))
    spreads = {}
    factors = {'w_up': 8.0, 'gn_w': 5.003, 'gn_b': 8.0, 'cmp_pos_k': 8.0, 'cmp_pos_v': 4.456}
    for name, (base, spread) in spreads.items():
        noise = np.random.default_rng([zlib.crc32(name.encode()), seed]).standard_normal(out[name].shape)
        drawn = base * np.exp(spread * noise) if base else spread * noise
        out[name] = __import__('jax').numpy.asarray(drawn.astype(out[name].dtype))
    for name, factor in factors.items():
        out[name] = (out[name] * factor).astype(out[name].dtype)
    return out
```

```python
from contextlib import ExitStack

import numpy as np

import concourse.bass as bass
from concourse import mybir

F32 = mybir.dt.float32
I32 = mybir.dt.int32
ALU = mybir.AluOpType
ACT = mybir.ActivationFunctionType
AX = mybir.AxisListType

P = 128
D_MODEL = 2048
KD = D_MODEL // P
SEQ, DEC_B, DEC_T = 512, 8, 4
NS = DEC_B * DEC_T
NT = SEQ + NS
HALF = NT // 2
PAST, PAGE = 2048, 128
N_PAGES = PAST // PAGE
N_POOL = DEC_B * N_PAGES * 5 // 4
A_WIDTH, A_COLS = 1024, 4224
HD = 64
KVW = 512
COL_Q, COL_GB, COL_C, COL_S, COL_W = 4224, 5248, 6272, 6784, 7296
COL_GATE = 7808
N_GATE = 48
ROW_M = COL_GATE + P
N_ROWS = ROW_M + 2 * D_MODEL
GRP = 256
RMS_EPS, GN_EPS = 1e-6, 64e-5
NEG = -1e30
WINDOW = 512
N_SEL, SEL_BLOCK = 33, 64


def same_engine(eng, sem):
    count = [0]

    def link(ins):
        count[0] += 1
        ins.then_inc(sem, 1)
        eng.wait_ge(sem, count[0])
        return ins

    def restart():
        eng.sem_clear(sem)
        count[0] = 0

    link.restart = restart
    return link


def project(nc, A):
    G_A, G_ALL = 31, 47
    FULL0 = 48
    RING = 4
    with ExitStack() as ctx:
        sb = lambda name, shape: ctx.enter_context(nc.sbuf_tensor(name, shape, F32))
        ps = lambda name, shape: ctx.enter_context(nc.psum_tensor(name, shape, F32))
        sem = nc.alloc_semaphore
        xT = sb("xT", [P, KD, NT])
        sq = sb("sq", [P, 2, NT])
        rs = sb("rs", [P, NT])
        g_in = sb("g_in", [P, KD])
        ones = sb("ones", [P, P])
        ident = sb("ident", [P, P])
        W = [sb(f"W{i}", [P, KD, GRP]) for i in range(2)]
        ub = [sb(f"ub{i}", [P, NT]) for i in range(RING)]
        u_tail = sb("u_tail", [33, 62 * P])
        u_tok = sb("u_tok", [P, 4, 14 * P])
        acc = [ps(f"acc{i}", [P, 2, 512]) for i in range(2)]
        tps = [ps(f"tps{i}", [P, 512]) for i in range(2)]
        tpf = [ps(f"tpf{i}", [P, 512]) for i in range(2)]
        x_in, g_ld, consts = sem("x_in"), sem("g_ld"), sem("consts")
        w_in = [sem(f"w_in{i}") for i in range(2)]
        squared, ssum, sq_free = sem("squared"), sem("ssum"), sem("sq_free")
        rs_ready, xT_ready, eps_ready = sem("rs_ready"), sem("xT_ready"), sem("eps_ready")
        proj_done, evac_done = sem("proj_done"), sem("evac_done")
        stored = [sem(f"stored{i}") for i in range(RING)]
        tail_tp, tail_ev, full_tp, full_ev = sem("tail_tp"), sem("tail_ev"), sem("full_tp"), sem("full_ev")
        rs_chain, act_chain, rows_out = sem("rs_chain"), sem("act_chain"), sem("rows_out")
        eps = sb("eps", [P, 1])
        block = ctx.enter_context(nc.Block())

        def w_src(s):
            if isinstance(s, int) and s == G_A - 1:
                return A["w_tail"]
            if isinstance(s, int) and s >= G_A or not isinstance(s, int) and s_merge[0]:
                return A["w_merge"][bass.ds(s - G_A, 1)].rearrange("a p k n -> (a p) k n")
            return A["w_main"][bass.ds(s, 1)].rearrange("a p k n -> (a p) k n")
        s_merge = [False]

        def plan(eng, group):
            for s in (0, 1):
                group(s, s % 2)
            with eng.Fori(1, 12) as i:
                for j in range(2):
                    group(i * 2 + j, j)
            for s in range(24, 32):
                group(s, s % 2)
            s_merge[0] = True
            with eng.Fori(16, 23) as i:
                for j in range(2):
                    group(i * 2 + j, j)
            s_merge[0] = False
            group(46, 0)

        @block.sync
        def _(sp):
            sp.dma_start(g_in[:, :], A["g_in"]).then_inc(g_ld, 16)
            sp.wait_ge(g_ld, 16)
            sp.dma_start(ident[:, :], A["ident"]).then_inc(g_ld, 16)
            for q in range(4):
                sp.dma_start(xT[:, 4 * q:4 * q + 4, :], A["xT"][:, 4 * q:4 * q + 4, :]).then_inc(x_in, 16)
                sp.wait_ge(x_in, 16 * (q + 1))

            def group(s, slot):
                if not isinstance(s, int) or s >= 2:
                    sp.wait_ge(proj_done, s * 2 - 2)
                src = w_src(s)
                dst = W[slot][:, :, 0:176] if isinstance(s, int) and s == G_A - 1 else W[slot][:, :, :]
                sp.dma_start(dst, src).then_inc(w_in[slot], 16)
            plan(sp, group)

        @block.gpsimd
        def _(pool):
            nc.gpsimd.memset(ones[:, :], 1.0).then_inc(consts, 1)
            pool.wait_ge(tail_ev, 62)
            pool.wait_ge(full_ev, 14)
            pool.dma_start(A["u_tail"], u_tail[:, :]).then_inc(rows_out, 16)
            pool.dma_start(A["p_shift"], u_tail[0:1, 0:A_COLS]).then_inc(rows_out, 16)
            for b in range(DEC_B):
                r = 1 + 4 * b + 3
                pool.dma_start(A["s_shift"][b:b + 1, :], u_tail[r:r + 1, 0:A_COLS]).then_inc(rows_out, 16)
            for name, k in (("s_cmp", 49), ("s_sel", 53)):
                pool.dma_start(A[name], u_tail[1:33, k * P:k * P + KVW]).then_inc(rows_out, 16)
            for b in range(DEC_B):
                pool.dma_start(A["s_win"][b, 508:512, :], u_tail[1 + 4 * b:5 + 4 * b, COL_W:COL_W + KVW])\
                    .then_inc(rows_out, 16)
                pool.dma_start(A["s_win"][b, 0:508, :], A["win_in"][b, 4:512, :]).then_inc(rows_out, 16)
            for name, k in (("p_cmp", 1), ("p_sel", 5), ("p_win", 9)):
                pool.dma_start(A[name].rearrange("(t p) c -> p t c", p=P), u_tok[:, :, k * P:k * P + KVW])\
                    .then_inc(rows_out, 16)
            pool.dma_start(A["u_tok"], u_tok[:, :, :]).then_inc(rows_out, 16)
            pool.wait_ge(rows_out, 16 * (1 + 1 + 8 + 2 + 16 + 3 + 1))

        @block.scalar
        def _(act):
            link = same_engine(act, act_chain)
            for k in range(KD):
                if k % 4 == 0:
                    act.wait_ge(x_in, 16 * (k // 4 + 1))
                if k >= 2:
                    act.wait_ge(ssum, k - 1)
                nc.scalar.activation(sq[:, k % 2, :], xT[:, k, :], ACT.Square).then_inc(squared, 1)
            act.wait_ge(ssum, KD)
            act.wait_ge(eps_ready, 1)
            nc.scalar.activation(rs[:, :].rearrange("p (a n) -> p a n", a=2), acc[0][:, :, 0:HALF], ACT.Sqrt,
                                 bias=eps[:, 0:1], scale=1.0 / D_MODEL).then_inc(rs_ready, 1)

            def group(s, slot):
                for j in range(2):
                    c = s * 2 + j
                    b = 2 * slot + j
                    act.wait_ge(proj_done, c + 1)
                    if not isinstance(s, int) or s >= 2:
                        act.wait_ge(stored[b], (c - b) * 4)
                        if isinstance(s, int):
                            act.wait_ge(tail_tp, min(c - 3, 62))
                            if c - 4 >= FULL0:
                                act.wait_ge(full_tp, min(c - 3 - FULL0, 14))
                        elif not s_merge[0]:
                            act.wait_ge(tail_tp, c - 3)
                    merge = s_merge[0] or isinstance(s, int) and s >= G_A
                    m = N_GATE if isinstance(s, int) and s == G_A - 1 and j == 1 else P
                    out = ub[b][0:m, :].rearrange("p (a n) -> p a n", a=2)
                    nc.scalar.activation(out, acc[j][0:m, :, 0:HALF], ACT.Sigmoid if merge else ACT.Copy)\
                        .then_inc(evac_done, 1)
                    act.wait_ge(evac_done, c + 1)
                    if isinstance(c, int):
                        dst = A["uT"][c * P:c * P + m, :]
                    else:
                        dst = A["uT"][bass.ds(c * P, P), :]
                    act.dma_start(dst, ub[b][0:m, :]).then_inc(stored[b], 16)
            plan(act, group)
            for b in range(RING):
                act.wait_ge(stored[b], 16 * (24 if b < 2 else 23))

        @block.vector
        def _(dve):
            link = same_engine(dve, rs_chain)
            nc.vector.memset(eps[:, :], RMS_EPS).then_inc(eps_ready, 1)
            dve.wait_ge(rs_ready, 1)
            link(nc.vector.reciprocal(rs[:, :], rs[:, :]))
            dve.wait_ge(g_ld, 32)
            for k in range(KD):
                nc.vector.scalar_tensor_tensor(out=xT[:, k, :], in0=xT[:, k, :], scalar=g_in[:, k:k + 1],
                                               in1=rs[:, :], op0=ALU.mult, op1=ALU.mult).then_inc(xT_ready, 1)

            def copies(c):
                dve.wait_ge(tail_tp, c + 1)
                if isinstance(c, int):
                    m = N_GATE if c == 61 else P
                    dst = u_tail[:, c * P:c * P + m]
                else:
                    m = P
                    dst = u_tail[:, bass.ds(c * P, P)]
                slot = c % 2 if isinstance(c, int) else parity[0]
                nc.vector.tensor_copy(dst, tps[slot][0:33, 0:m]).then_inc(tail_ev, 1)
                if isinstance(c, int) and c >= FULL0:
                    f = c - FULL0
                    dve.wait_ge(full_tp, f + 1)
                    nc.vector.tensor_copy(u_tok[:, :, f * P:f * P + m],
                                          tpf[f % 2][:, :].rearrange("p (t n) -> p t n", t=4)[:, :, 0:m])\
                        .then_inc(full_ev, 1)
            parity = [0]

            def group(s, slot):
                for j in range(2):
                    c = s * 2 + j - 1
                    parity[0] = (j + 1) % 2
                    if isinstance(s, int) and (c < 0 or c > 61):
                        continue
                    if s_merge[0]:
                        continue
                    copies(c)
            nc.vector.memset(u_tail[:, 61 * P + N_GATE:62 * P], 0.0)
            nc.vector.memset(u_tok[:, :, 13 * P + N_GATE:14 * P], 0.0).then_inc(eps_ready, 1)
            dve.wait_ge(eps_ready, 2)
            for s in (0, 1):
                group(s, s % 2)
            with dve.Fori(1, 12) as i:
                for j in range(2):
                    group(i * 2 + j, j)
            for s in range(24, 32):
                group(s, s % 2)

        @block.tensor
        def _(pe):
            pe.wait_ge(consts, 1)
            for k in range(KD):
                pe.wait_ge(squared, k + 1)
                for h in range(2):
                    ins = nc.tensor.matmul(acc[0][:, h, 0:HALF], ones[:, :], sq[:, k % 2, h * HALF:(h + 1) * HALF],
                                           start=(k == 0), stop=(k == KD - 1))
                ins.then_inc(ssum, 1)
            pe.wait_ge(xT_ready, 1)

            def copies(c, b):
                m = N_GATE if isinstance(c, int) and c == 61 else P
                pe.wait_ge(evac_done, c + 1)
                if not isinstance(c, int) or c >= 2:
                    pe.wait_ge(tail_ev, c - 1)
                nc.tensor.matmul(tps[b % 2][0:33, 0:m], ub[b][0:m, SEQ - 1:NT], ident[0:m, 0:m],
                                 start=True, stop=True).then_inc(tail_tp, 1)
                if isinstance(c, int) and c >= FULL0:
                    f = c - FULL0
                    if f >= 2:
                        pe.wait_ge(full_ev, f - 1)
                    for t in range(4):
                        ins = nc.tensor.transpose(tpf[f % 2][:, t * P:t * P + m],
                                                  ub[b][0:m, t * P:(t + 1) * P], ident[0:m, 0:m])
                    ins.then_inc(full_tp, 1)

            pe.wait_ge(g_ld, 32)

            def group(s, slot):
                if isinstance(s, int):
                    pe.wait_ge(w_in[slot], 16 * (s // 2 + 1))
                else:
                    pe.wait_ge(w_in[slot], (s - slot) * 8 + 16)
                for j in range(2):
                    c = s * 2 + j
                    if not isinstance(c, int) or c >= 2:
                        pe.wait_ge(evac_done, c - 1)
                    m = N_GATE if isinstance(s, int) and s == G_A - 1 and j == 1 else P
                    for k in range(KD):
                        if isinstance(c, int) and c == 0:
                            pe.wait_ge(xT_ready, k + 1)
                        for h in range(2):
                            ins = nc.tensor.matmul(acc[j][0:m, h, 0:HALF], W[slot][:, k, j * P:j * P + m],
                                                   xT[:, k, h * HALF:(h + 1) * HALF],
                                                   start=(k == 0), stop=(k == KD - 1))
                    ins.then_inc(proj_done, 1)
                    p = c - 1
                    if isinstance(p, int) and (p < 0 or p > 61) or s_merge[0]:
                        continue
                    copies(p, (2 * slot + j - 1) % 4)
            plan(pe, group)


CH = 64
NCH = SEQ // CH
DECAY_SCALE = -float(np.exp(-0.5))
R_, K_, V_, G_ = range(4)
(MU, W0, A0, KK_K, KA, RK, GNW, GNB, OMKA) = (0, 4, 5, 6, 7, 8, 9, 10, 11)
N_PAR = 12

RWKV_JOBS = [
    ("zw", 0, 2, "act"), ("za", 2, 2, "act"), ("tok_a", 0, 1, "act"), ("tok_b", 1, 1, "act"),
    ("knorm", 2, 1, "dve"), ("bonus", 3, 1, "dve"),
    ("bk_tok0", 0, 1, "act"), ("bk_tok1", 1, 1, "act"), ("v_tok0", 2, 1, "act"), ("v_tok1", 3, 1, "act"),
    ("N", 0, 1, "dve"), ("NT", 1, 1, "dve"), ("kk_tok", 2, 1, "act"),
    ("D2", 3, 1, "act"), ("DT2", 0, 1, "dve"),
    ("G0", 1, 1, "dve"), ("G1", 2, 1, "dve"),
    ("D4", 3, 1, "act"), ("DT4", 0, 1, "dve"),
    ("G2", 1, 1, "dve"), ("G3", 2, 1, "dve"),
    ("Q1T", 3, 1, "act"), ("D8", 0, 1, "dve"),
    ("X2", 1, 1, "act"), ("Q2", 2, 1, "act"),
    ("Di", 3, 1, "act"), ("DiT", 0, 1, "dve"),
    ("E", 1, 1, "dve"), ("ET", 2, 1, "dve"), ("E2", 3, 1, "dve"), ("M1T", 0, 1, "dve"),
    ("Tt", 1, 1, "act"), ("W1T", 2, 1, "act"), ("W2a", 3, 1, "act"), ("W2b", 0, 1, "act"),
]
for _n in range(NCH):
    RWKV_JOBS += [(f"U{_n}", 1 + _n % 2, 1, "dve"), (f"O{_n}", 3, 1, "act"), (f"S{_n}", 0, 1, "dve")]
RWKV_JOBS += [("S_out", 1, 1, "act"), ("mean", 2, 1, "dve"), ("var", 3, 1, "act")]


def job_counts():
    n = {"act": 0, "dve": 0}
    out = {}
    for at, (name, _, _, eng) in enumerate(RWKV_JOBS):
        for e in ("act", "dve"):
            if eng in (e, "both"):
                n[e] += 1
                out[name, e] = n[e]
        out[name] = at + 1
    return out, n


def rwkv(nc, A):
    at, per_pair = job_counts()
    NJ = len(RWKV_JOBS)
    last_user = {}
    before = {}
    for name, b0, nb, _ in RWKV_JOBS:
        before[name] = {last_user[b] for b in range(b0, b0 + nb) if b in last_user}
        for b in range(b0, b0 + nb):
            last_user[b] = name
    bank_of = {name: b0 for name, b0, _, _ in RWKV_JOBS}
    engine_of = {name: e for name, _, _, e in RWKV_JOBS}
    with ExitStack() as ctx:
        sb = lambda name, shape: ctx.enter_context(nc.sbuf_tensor(name, shape, F32))
        sem = nc.alloc_semaphore
        bank = ctx.enter_context(nc.psum_tensor("rbank", [P, 4, 512], F32))
        in4, d4, u4 = sb("in4", [P, 4, NT]), sb("d4", [P, 4, NT]), sb("u4", [P, 4, NT])
        par, wup, shift = sb("par", [P, N_PAR]), sb("wup", [P, P]), sb("shift", [P, 4, DEC_B])
        lora_in, lora_d, lora = sb("lora_in", [P, NT]), sb("lora_d", [P, NT]), sb("lora", [P, NT])
        lora_mu, lora_shift = sb("lora_mu", [P, 1]), sb("lora_shift", [P, DEC_B])
        sw, a = sb("sw", [P, NT]), sb("a", [P, NT])
        ident, headsum, headmean = (sb(n, [P, P]) for n in ("r_ident", "headsum", "headmean"))
        mask = sb("mask", [P, 512 + P + 5 * CH])
        m_scan, m_G = mask[:, 0:512], mask[:, 512:512 + P]
        m_D, m_F, m_DT, m_I = (mask[:, 512 + P + k * CH:512 + P + (k + 1) * CH] for k in range(4))
        L, cum, cumL = sb("L", [P, SEQ]), sb("cum", [P, SEQ]), sb("cumL", [P, SEQ])
        E1, Ei, E0 = sb("E1", [P, SEQ]), sb("Ei", [P, SEQ]), sb("E0", [P, SEQ])
        sqk, rn, kk, kb, k2, rk = (sb(n, [P, SEQ]) for n in ("sqk", "rn", "kk", "kb", "k2", "rk"))
        bonus = sb("bonus", [P, SEQ])
        BK, KR, VZ = (sb(n, [P, NCH, 2, CH]) for n in ("BK", "KR", "VZ"))
        tok6 = sb("tok6", [NS, 6, P])
        BKtok, UV = sb("BKtok", [P, NCH, P]), sb("UV", [P, NCH, P])
        G = sb("G", [P, 2, NCH, P])
        mats = {n: sb("m_" + n, [P, NCH, CH]) for n in (
            "D", "ImD", "F", "DT", "kk_tok", "D2", "DT2", "IpDT2", "IpD2", "D4", "DT4", "IpDT4", "IpD8", "Q1T",
            "Q2", "Di", "DiT", "E", "ImE", "ET", "ImET", "IpE2", "M1T", "Tt", "X2", "W1T")}
        W2 = sb("W2", [CH, 2, NCH, CH])
        S, Sd, S_nat = sb("S", [P, P]), sb("Sd", [P, P]), sb("S_nat", [P, P])
        oT, oc, osq, osd = sb("oT", [P, SEQ]), sb("oc", [P, SEQ]), sb("osq", [P, SEQ]), sb("osd", [P, SEQ])
        gate = sb("gate", [P, SEQ])
        epsg = sb("epsg", [P, 1])

        loaded, consts, in_free = sem("r_loaded"), sem("r_consts"), sem("r_in_free")
        pe_jobs, ev_act, ev_dve = sem("pe_jobs"), sem("ev_act"), sem("ev_dve")
        mixed, lora_ready, tanh_done = sem("mixed"), sem("lora_ready"), sem("tanh_done")
        cum_ready, exps_ready, sqk_ready, knorm2 = sem("cum_ready"), sem("exps_ready"), sem("sqk_ready"), sem("knorm2")
        knorm_sqrt, operands, tok_sent, rk_ready = sem("knorm_sqrt"), sem("operands"), sem("tok_sent"), sem("rk_ready")
        centered, sq_ready, std_ready, gate_ready = sem("centered"), sem("sq_ready"), sem("std_ready"), sem("gate_ready")
        o_ready, o_sent, s_ready, s_sent = sem("r_o_ready"), sem("r_o_sent"), sem("r_s_ready"), sem("r_s_sent")
        pair_pe, pair_act, pair_dve, pre = sem("pair_pe"), sem("pair_act"), sem("pair_dve"), sem("r_pre")
        dve_chain, settled = sem("r_dve_chain"), sem("settled")
        state_ready = sem("state_ready")
        block = ctx.enter_context(nc.Block())
        NA, ND = per_pair["act"], per_pair["dve"]

        def taken(eng, i, *names):
            for e, s, n in (("act", ev_act, NA), ("dve", ev_dve, ND)):
                places = [at[name, e] for name in names if engine_of[name] in (e, "both")]
                if places:
                    eng.wait_ge(s, i * n + max(places))

        N_CONST = 6

        @block.sync
        def _(sp):
            for dst, src in ((ident, "ident"), (headsum, "headsum"), (headmean, "headmean"), (mask, "rmask"),
                             (lora_mu, "lora_mu"), (lora_shift, "lora_shift")):
                sp.dma_start(dst[:, :], A[src]).then_inc(consts, 16)
            sp.dma_start(lora_in[:, :], A["uT"][4 * A_WIDTH:4 * A_WIDTH + P, :]).then_inc(consts, 16)
            with sp.Fori(0, 8) as i:
                sp.wait_ge(in_free, i + 1)
                u = A["uT"][0:4 * A_WIDTH, :].rearrange("(f c p) n -> c p f n", f=4, p=P)
                sp.dma_start(in4[:, :, :], u[bass.ds(i, 1)].rearrange("a p f n -> (a p) f n")).then_inc(loaded, 16)
                for dst, src in ((par, "par"), (wup, "wup")):
                    sp.dma_start(dst[:, :], A[src][bass.ds(i, 1)].rearrange("a p n -> (a p) n")).then_inc(loaded, 16)
                sp.dma_start(shift[:, :, :], A["shift"][bass.ds(i, 1)].rearrange("a p f n -> (a p) f n"))\
                    .then_inc(loaded, 16)
                sp.wait_ge(ev_act, i * NA + at["tok_b", "act"])
                for h in range(2):
                    dst = A["smp"][bass.ds(i * 2 + h, 1)].rearrange("a t (f d) -> (a t) f d", f=6)
                    sp.dma_start(dst, tok6[:, :, h * HD:(h + 1) * HD]).then_inc(tok_sent, 16)
                sp.wait_ge(ev_act, i * NA + at["S_out", "act"])
                for h in range(2):
                    dst = A["p_rwkv"][bass.ds(i * 2 + h, 1)].rearrange("a t d -> (a t) d")
                    sp.dma_start(dst, S_nat[h * HD:(h + 1) * HD, h * HD:(h + 1) * HD]).then_inc(s_sent, 16)
                sp.wait_ge(o_ready, i + 1)
                sp.dma_start(A["oaT"][bass.ds(i, 1)].rearrange("a p n -> (a p) n"), oT[:, :]).then_inc(o_sent, 16)
            sp.wait_ge(tok_sent, 16 * 16)
            sp.wait_ge(s_sent, 16 * 16)
            sp.wait_ge(o_sent, 8 * 16)

        @block.vector
        def _(dve):
            link = same_engine(dve, dve_chain)
            v = nc.vector
            tt, ts, stt = v.tensor_tensor, v.tensor_scalar, v.scalar_tensor_tensor
            v.memset(epsg[:, :], GN_EPS)
            v.memset(VZ[:, :, 0, :], 0.0)
            v.memset(L[:, :], 0.0).then_inc(in_free, 1)
            dve.wait_ge(consts, 16 * (N_CONST + 1))

            def shift_mix(x, d, u, mu, prev, f):
                four = lambda t: t[:, :, SEQ:NT].rearrange("p f (b t) -> p f b t", t=DEC_T)
                tt(d[:, :, 1:SEQ], x[:, :, 0:SEQ - 1], x[:, :, 1:SEQ], ALU.subtract)
                ts(d[:, :, 0:1], x[:, :, 0:1], -1.0, None, ALU.mult)
                for k in range(f):
                    xf, df = four(x)[:, k], four(d)[:, k]
                    tt(df[:, :, 1:DEC_T], xf[:, :, 0:DEC_T - 1], xf[:, :, 1:DEC_T], ALU.subtract)
                    last = tt(df[:, :, 0:1], prev[:, k, :, None], xf[:, :, 0:1], ALU.subtract)
                link(last)
                for k in range(f):
                    last = stt(out=u[:, k, :], in0=d[:, k, :], scalar=mu[:, k:k + 1], in1=x[:, k, :],
                               op0=ALU.mult, op1=ALU.add)
                return last
            shift_mix(lora_in[:, None, :], lora_d[:, None, :], lora[:, None, :], lora_mu,
                      lora_shift[:, None, :], 1).then_inc(lora_ready, 1)
            link.restart()
            with dve.Fori(0, 8) as i:
                def got(name):
                    dve.wait_ge(pe_jobs, i * NJ + at[name])
                dve.wait_ge(pair_pe, i + 1)
                dve.wait_ge(pair_act, i + 1)
                dve.wait_ge(loaded, (i + 1) * 64)
                shift_mix(in4, d4, u4, par, shift, 4).then_inc(mixed, 1)
                dve.wait_ge(mixed, i + 1)
                link(ts(par[:, OMKA:OMKA + 1], par[:, KA:KA + 1], -1.0, 1.0, ALU.mult, ALU.add))
                dve.wait_ge(ev_act, i * NA + at["za", "act"])
                link(ts(L[:, :], sw[:, 0:SEQ], DECAY_SCALE, None, ALU.mult))
                link(v.tensor_tensor_scan(out=cum[:, :], data0=m_scan, data1=L[:, :], initial=0.0,
                                          op0=ALU.mult, op1=ALU.add))
                tt(cumL[:, :], cum[:, :], L[:, :], ALU.subtract).then_inc(cum_ready, 1)
                link(ts(kb[:, :], a[:, 0:SEQ], par[:, KA:KA + 1], par[:, OMKA:OMKA + 1], ALU.mult, ALU.add))
                link(tt(k2[:, :], u4[:, K_, 0:SEQ], kb[:, :], ALU.mult))
                stt(out=rk[:, :], in0=u4[:, R_, 0:SEQ], scalar=par[:, RK:RK + 1], in1=k2[:, :],
                    op0=ALU.mult, op1=ALU.mult).then_inc(rk_ready, 1)
                got("knorm")
                ts(rn[:, :], bank[:, bank_of["knorm"], :], 1e-24, None, ALU.max).then_inc(ev_dve, 1)
                dve.wait_ge(knorm_sqrt, i + 1)
                link(v.reciprocal(rn[:, :], rn[:, :]))
                link(stt(out=kk[:, :], in0=u4[:, K_, 0:SEQ], scalar=par[:, KK_K:KK_K + 1], in1=rn[:, :],
                         op0=ALU.mult, op1=ALU.mult))
                link(tt(kb[:, :], kk[:, :], a[:, 0:SEQ], ALU.mult))
                dve.wait_ge(exps_ready, (i + 1) * 3)
                by = lambda t: t[:, :].rearrange("p (n c) -> p n c", c=CH)
                tt(BK[:, :, 0, :], by(kb), by(Ei), ALU.mult)
                tt(BK[:, :, 1, :], by(k2), by(Ei), ALU.mult)
                tt(KR[:, :, 0, :], by(kk), by(E0), ALU.mult)
                tt(KR[:, :, 1, :], u4[:, R_, 0:SEQ].rearrange("p (n c) -> p n c", c=CH), by(E1), ALU.mult)
                v.tensor_copy(VZ[:, :, 1, :], u4[:, V_, 0:SEQ].rearrange("p (n c) -> p n c", c=CH))
                v.memset(S[:, :], 0.0).then_inc(operands, 1)
                got("bonus")
                tt(bonus[:, :], bank[:, bank_of["bonus"], :], u4[:, V_, 0:SEQ], ALU.mult).then_inc(ev_dve, 1)
                m = mats
                pb = lambda name: bank[:, bank_of[name], :].rearrange("p (n c) -> p n c", c=CH)
                over = lambda t: t[:, None, :].to_broadcast([P, NCH, CH])
                got("N")
                tt(m["D"][:, :, :], pb("N"), over(m_D), ALU.mult)
                link(tt(m["F"][:, :, :], pb("N"), over(m_F), ALU.mult))
                tt(m["ImD"][:, :, :], over(m_I), m["D"][:, :, :], ALU.subtract).then_inc(ev_dve, 1)
                got("NT")
                tt(m["DT"][:, :, :], pb("NT"), over(m_DT), ALU.mult).then_inc(ev_dve, 1)
                got("DT2")
                tt(m["IpDT2"][:, :, :], pb("DT2"), over(m_I), ALU.add)
                v.tensor_copy(m["DT2"][:, :, :], pb("DT2")).then_inc(ev_dve, 1)

                def g_quarter(q):
                    got(f"G{q}")
                    src = bank[:, bank_of[f"G{q}"], :].rearrange("p (n c) -> p n c", c=P)
                    tt(G[:, q // 2, 4 * (q % 2):4 * (q % 2) + 4, :], src,
                       m_G[:, None, :].to_broadcast([P, 4, P]), ALU.mult).then_inc(ev_dve, 1)
                g_quarter(0)
                g_quarter(1)
                got("DT4")
                tt(m["IpDT4"][:, :, :], pb("DT4"), over(m_I), ALU.add)
                v.tensor_copy(m["DT4"][:, :, :], pb("DT4")).then_inc(ev_dve, 1)
                g_quarter(2)
                g_quarter(3)
                got("D8")
                tt(m["IpD8"][:, :, :], pb("D8"), over(m_I), ALU.add).then_inc(ev_dve, 1)
                got("DiT")
                v.tensor_copy(m["DiT"][:, :, :], pb("DiT")).then_inc(ev_dve, 1)
                got("E")
                v.tensor_copy(m["E"][:, :, :], pb("E"))
                tt(m["ImE"][:, :, :], over(m_I), pb("E"), ALU.subtract).then_inc(ev_dve, 1)
                got("ET")
                v.tensor_copy(m["ET"][:, :, :], pb("ET"))
                tt(m["ImET"][:, :, :], over(m_I), pb("ET"), ALU.subtract).then_inc(ev_dve, 1)
                got("E2")
                tt(m["IpE2"][:, :, :], pb("E2"), over(m_I), ALU.add).then_inc(ev_dve, 1)
                got("M1T")
                v.tensor_copy(m["M1T"][:, :, :], pb("M1T")).then_inc(ev_dve, 1)
                for n in range(NCH):
                    last_p = E1[:, (n + 1) * CH - 1:(n + 1) * CH]
                    link(ts(Sd[:, :], S[:, :], last_p, None, ALU.mult))
                    dve.wait_ge(ev_act, i * NA + at["W2b", "act"])
                    got(f"U{n}")
                    stt(out=UV[0:CH, n, :].rearrange("p (h i) -> p h i", h=2),
                        in0=bank[0:CH, bank_of[f"U{n}"], 0:P].rearrange("p (h i) -> p h i", h=2), scalar=-1.0,
                        in1=W2[:, :, n, :], op0=ALU.mult, op1=ALU.subtract).then_inc(ev_dve, 1)
                    got(f"S{n}")
                    for h, hp in enumerate((slice(0, CH), slice(CH, P))):
                        last = stt(out=S[hp, h * CH:(h + 1) * CH], in0=bank[hp, bank_of[f"S{n}"], 0:CH],
                                   scalar=last_p[hp], in1=Sd[hp, h * CH:(h + 1) * CH], op0=ALU.mult, op1=ALU.add)
                    last.then_inc(ev_dve, 1)
                    dve.wait_ge(ev_dve, i * ND + at[f"S{n}", "dve"])
                got("mean")
                tt(oc[:, :], oT[:, :], bank[:, bank_of["mean"], :], ALU.subtract).then_inc(ev_dve, 1)
                dve.wait_ge(std_ready, i + 1)
                link(v.reciprocal(osd[:, :], osd[:, :]))
                link(stt(out=oc[:, :], in0=oc[:, :], scalar=par[:, GNW:GNW + 1], in1=osd[:, :],
                         op0=ALU.mult, op1=ALU.mult))
                link(stt(out=oc[:, :], in0=oc[:, :], scalar=par[:, GNB:GNB + 1], in1=bonus[:, :],
                         op0=ALU.add, op1=ALU.add))
                dve.wait_ge(gate_ready, i + 1)
                link(tt(gate[:, :], gate[:, :], u4[:, G_, 0:SEQ], ALU.mult))
                tt(oT[:, :], oc[:, :], gate[:, :], ALU.mult).then_inc(o_ready, 1)
                dve.wait_ge(o_ready, i + 1)
                v.memset(Sd[:, 0:1], 0.0).then_inc(in_free, 1)
                link.restart()

        @block.scalar
        def _(act):
            act.wait_ge(lora_ready, 1)
            nc.scalar.activation(lora[0:HD, :], lora[0:HD, :], ACT.Tanh).then_inc(tanh_done, 1)
            f = nc.scalar.activation
            act.wait_ge(tanh_done, 1)
            act.sem_inc(pair_act, 1)
            with act.Fori(0, 8) as i:
                def got(name):
                    act.wait_ge(pe_jobs, i * NJ + at[name])

                def out(name, dst, src=None, func=ACT.Copy, **kw):
                    got(name)
                    f(dst, bank[:, bank_of[name], :] if src is None else src, func, **kw).then_inc(ev_act, 1)
                act.wait_ge(pair_pe, i + 1)
                act.wait_ge(mixed, i + 1)
                f(sqk[:, :], u4[:, K_, 0:SEQ], ACT.Square, scale=par[:, KK_K:KK_K + 1]).then_inc(sqk_ready, 1)
                two = lambda t: t[:, :].rearrange("p (a n) -> p a n", a=2)
                out("zw", two(sw), bank[:, 0:2, 0:HALF], ACT.Sigmoid, bias=par[:, W0:W0 + 1])
                out("za", two(a), bank[:, 2:4, 0:HALF], ACT.Sigmoid, bias=par[:, A0:A0 + 1])
                f(gate[:, :], u4[:, G_, 0:SEQ], ACT.Sigmoid).then_inc(gate_ready, 1)
                out("tok_a", tok6[:, 0:4, :], bank[0:NS, bank_of["tok_a"], :].rearrange("p (f d) -> p f d", f=4))
                out("tok_b", tok6[:, 4:6, :], bank[0:NS, bank_of["tok_b"], 0:2 * P].rearrange("p (f d) -> p f d", f=2))
                act.wait_ge(cum_ready, i + 1)
                f(E1[:, :], cum[:, :], ACT.Exp).then_inc(exps_ready, 1)
                f(Ei[:, :], cum[:, :], ACT.Exp, scale=-1.0).then_inc(exps_ready, 1)
                f(E0[:, :], cumL[:, :], ACT.Exp).then_inc(exps_ready, 1)
                act.wait_ge(ev_dve, i * ND + at["knorm", "dve"])
                f(rn[:, :], rn[:, :], ACT.Sqrt).then_inc(knorm_sqrt, 1)
                m = mats
                pb = lambda name: bank[:, bank_of[name], :].rearrange("p (n c) -> p n c", c=CH)
                pw = lambda name: bank[:, bank_of[name], :].rearrange("p (n c) -> p n c", c=P)
                out("bk_tok0", BKtok[:, 0:4, :], pw("bk_tok0"))
                out("bk_tok1", BKtok[:, 4:8, :], pw("bk_tok1"))
                out("v_tok0", UV[CH:P, 0:4, :], pw("v_tok0")[CH:P])
                out("v_tok1", UV[CH:P, 4:8, :], pw("v_tok1")[CH:P])
                out("kk_tok", m["kk_tok"][:, :, :], pb("kk_tok"))
                for name in ("D2", "D4", "Q1T", "X2", "Q2", "Di", "Tt", "W1T"):
                    out(name, m[name][:, :, :], pb(name))
                for h, name in enumerate(("W2a", "W2b")):
                    out(name, W2[:, h, :, :], pb(name)[0:CH])
                for n in range(NCH):
                    out(f"O{n}", oT[:, n * CH:(n + 1) * CH], bank[:, bank_of[f"O{n}"], 0:CH])
                out("S_out", S_nat[:, :], bank[:, bank_of["S_out"], 0:P])
                act.wait_ge(ev_dve, i * ND + at["mean", "dve"])
                f(osq[:, :], oc[:, :], ACT.Square).then_inc(sq_ready, 1)
                got("var")
                f(osd[:, :], bank[:, bank_of["var"], :], ACT.Sqrt, bias=epsg[:, 0:1]).then_inc(std_ready, 1)
                act.wait_ge(std_ready, i + 1)
                act.sem_inc(ev_act, 1)
                act.wait_ge(o_sent, (i + 1) * 16)
                act.wait_ge(tok_sent, (i + 1) * 32)
                act.wait_ge(s_sent, (i + 1) * 32)
                act.sem_inc(pair_act, 1)

        @block.tensor
        def _(pe):
            mm = nc.tensor.matmul
            pe.wait_ge(consts, 16 * (N_CONST + 1))
            pe.wait_ge(tanh_done, 1)
            pe.sem_inc(pair_pe, 1)

            def settle():
                pe.sem_inc(settled, 1)
            with pe.Fori(0, 8) as i:
                def job(name, *needs):
                    taken(pe, i, *before[name], *needs)
                    settle()

                def done(ins):
                    ins.then_inc(pe_jobs, 1)
                pe.wait_ge(mixed, i + 1)
                for name, rows in (("zw", slice(0, HD)), ("za", slice(HD, P))):
                    job(name)
                    for h in range(2):
                        ins = mm(bank[:, bank_of[name] + h, 0:HALF], wup[rows, :],
                                 lora[rows, h * HALF:(h + 1) * HALF], start=True, stop=True)
                    done(ins)
                job("tok_a", "za")
                for f in range(4):
                    ins = mm(bank[0:NS, 0, f * P:(f + 1) * P], u4[:, f, SEQ:NT], ident[:, :], start=True, stop=True)
                done(ins)
                job("tok_b")
                for f, t in enumerate((sw, a)):
                    ins = mm(bank[0:NS, 1, f * P:(f + 1) * P], t[:, SEQ:NT], ident[:, :], start=True, stop=True)
                done(ins)
                pe.wait_ge(sqk_ready, i + 1)
                job("knorm")
                done(mm(bank[:, 2, :], headsum[:, :], sqk[:, :], start=True, stop=True))
                pe.wait_ge(rk_ready, i + 1)
                job("bonus")
                done(mm(bank[:, 3, :], headsum[:, :], rk[:, :], start=True, stop=True))
                pe.wait_ge(operands, i + 1)
                for name, src, n0 in (("bk_tok0", BK, 0), ("bk_tok1", BK, 4), ("v_tok0", VZ, 0), ("v_tok1", VZ, 4)):
                    job(name)
                    for n in range(4):
                        ins = mm(bank[:, bank_of[name], n * P:(n + 1) * P],
                                 src[:, n0 + n, :, :].rearrange("p a c -> p (a c)"), ident[:, :],
                                 start=True, stop=True)
                    done(ins)
                H = (slice(0, CH), slice(CH, P))

                def both(name, lhsT, rhs, *needs):
                    job(name, *needs)
                    for n in range(NCH):
                        for hp in H:
                            ins = mm(bank[hp, bank_of[name], n * CH:(n + 1) * CH], lhsT(hp, n), rhs(hp, n),
                                     start=True, stop=True)
                    done(ins)
                B = lambda hp, n: BK[hp, n, 0, :]
                KK = lambda hp, n: KR[hp, n, 0, :]
                M = lambda name: (lambda hp, n: mats[name][hp, n, :])
                both("N", B, KK)
                both("NT", KK, B)
                both("kk_tok", KK, lambda hp, n: ident[hp, hp])
                both("D2", M("DT"), M("D"), "N", "NT")
                both("DT2", M("D"), M("DT"))

                def g_quarter(q):
                    job(f"G{q}")
                    hp = H[q // 2]
                    for n in range(4):
                        nn = 4 * (q % 2) + n
                        ins = mm(bank[:, bank_of[f"G{q}"], n * P:(n + 1) * P],
                                 BK[hp, nn, :, :].rearrange("p a c -> p (a c)"),
                                 KR[hp, nn, :, :].rearrange("p a c -> p (a c)"), start=True, stop=True)
                    done(ins)
                g_quarter(0)
                g_quarter(1)
                both("D4", M("DT2"), M("D2"), "D2", "DT2")
                both("DT4", M("D2"), M("DT2"))
                g_quarter(2)
                g_quarter(3)
                both("Q1T", M("ImD"), M("IpDT2"))
                both("D8", M("DT4"), M("D4"), "D4", "DT4")
                job("X2", "G0", "G1", "G2", "G3", "v_tok0", "v_tok1")
                for n in range(NCH):
                    for h, hp in enumerate(H):
                        ins = mm(bank[hp, bank_of["X2"], n * CH:(n + 1) * CH], G[CH:P, h, n, 0:CH],
                                 UV[CH:P, n, h * CH:(h + 1) * CH], start=True, stop=True)
                done(ins)
                both("Q2", M("IpDT4"), M("IpD8"), "D8")
                both("Di", M("Q1T"), M("Q2"), "Q1T", "Q2")
                both("DiT", M("Q2"), M("Q1T"))
                both("E", M("DiT"), M("F"), "DiT")
                both("ET", M("F"), M("DiT"))
                both("E2", M("ET"), M("E"), "E", "ET")
                both("M1T", M("IpE2"), M("ImET"), "E2")
                both("Tt", M("M1T"), M("Di"), "M1T", "Di")
                both("W1T", M("kk_tok"), M("Tt"), "Tt", "kk_tok", "X2")
                for h, name in enumerate(("W2a", "W2b")):
                    job(name)
                    for n in range(NCH):
                        ins = mm(bank[0:CH, bank_of[name], n * CH:(n + 1) * CH], mats["Tt"][H[h], n, :],
                                 mats["X2"][H[h], n, :], start=True, stop=True)
                    done(ins)
                for n in range(NCH):
                    job(f"U{n}", "W1T", *([f"S{n - 1}"] if n else []))
                    done(mm(bank[0:CH, bank_of[f"U{n}"], 0:P], mats["W1T"][:, n, :], S[:, :], start=True, stop=True))
                    job(f"O{n}", f"U{n}", "bk_tok1")
                    mm(bank[:, bank_of[f"O{n}"], 0:CH], S[:, :], KR[:, n, 1, :], start=True, stop=False)
                    for h, hp in enumerate(H):
                        ins = mm(bank[hp, bank_of[f"O{n}"], 0:CH], UV[:, n, h * CH:(h + 1) * CH],
                                 G[:, h, n, CH:P], start=False, stop=True)
                    done(ins)
                    job(f"S{n}")
                    for h, hp in enumerate(H):
                        ins = mm(bank[hp, bank_of[f"S{n}"], 0:CH], BKtok[:, n, h * CH:(h + 1) * CH],
                                 UV[:, n, h * CH:(h + 1) * CH], start=True, stop=True)
                    done(ins)
                job("S_out", f"S{NCH - 1}", f"O{NCH - 1}")
                done(mm(bank[:, bank_of["S_out"], 0:P], S[:, :], ident[:, :], start=True, stop=True))
                job("mean")
                done(mm(bank[:, bank_of["mean"], :], headmean[:, :], oT[:, :], start=True, stop=True))
                pe.wait_ge(sq_ready, i + 1)
                job("var")
                done(mm(bank[:, bank_of["var"], :], headmean[:, :], osq[:, :], start=True, stop=True))
                taken(pe, i, "S_out", "mean", "var", f"S{NCH - 1}")
                pe.sem_inc(pair_pe, 1)


def rwkv_samples(nc, A):
    with ExitStack() as ctx:
        sb = lambda name, shape: ctx.enter_context(nc.sbuf_tensor(name, shape, F32))
        sem = nc.alloc_semaphore
        X = sb("sx", [P, DEC_T, 6, HD])
        tab = sb("stab", [P, 5, HD])
        S, Sw, outer, prod = (sb(n, [P, HD, HD]) for n in ("sS", "sSw", "s_outer", "s_prod"))
        w, kraw, sq, kk, b, k2, rk, o, oc, gate = (
            sb("s_" + n, [P, DEC_T, HD]) for n in ("w", "kraw", "sq", "kk", "b", "k2", "rk", "o", "oc", "gate"))
        ss, mean, var, bonus = (sb("s_" + n, [P, DEC_T]) for n in ("ss", "mean", "var", "bonus"))
        sa, eps = sb("s_sa", [P, HD]), sb("s_eps", [P, 1])
        loaded, chain, act_done, ready = sem("s_loaded"), sem("s_chain"), sem("s_act_done"), sem("s_ready_in")
        norm_in, var_in, state_new, pool_chain, decayed = (
            sem(n) for n in ("s_norm_in", "s_var_in", "s_state_new", "s_pool_chain", "s_decayed"))
        o_done, sent = sem("s_o_done"), sem("s_sent")
        block = ctx.enter_context(nc.Block())
        last_dim = lambda t, i: t[:, i, None, :].to_broadcast([P, HD, HD])
        over_j = lambda t: t[:, :, None].to_broadcast([P, HD, HD])
        over_d = lambda t: t[:, :, None].to_broadcast([P, DEC_T, HD])
        over_t = lambda k: tab[:, None, k, :].to_broadcast([P, DEC_T, HD])
        r, k, v, g, sw, a = (X[:, :, f, :] for f in range(6))

        @block.sync
        def _(sp):
            sp.dma_start(X[:, :, :, :], A["smp"].rearrange("h (b t) f -> (h b) (t f)", t=DEC_T)
                         .rearrange("p (t f d) -> p t f d", t=DEC_T, f=6)).then_inc(loaded, 16)
            sp.dma_start(tab[:, :, :], A["stab"]).then_inc(loaded, 16)
            sp.dma_start(S[:, :, :], A["state"]).then_inc(loaded, 16)
            sp.wait_ge(o_done, 1)
            sp.dma_start(A["s_rwkv"], S[:, :, :]).then_inc(sent, 16)
            sp.dma_start(A["oS"].rearrange("h n d -> (h n d)").rearrange("(p n) -> p n", p=P),
                         o[:, :, :].rearrange("p t d -> p (t d)")).then_inc(sent, 16)
            sp.wait_ge(sent, 32)

        @block.scalar
        def _(act):
            f = nc.scalar.activation
            act.wait_ge(loaded, 48)
            f(w[:, :, :], sw, ACT.Exp, scale=DECAY_SCALE).then_inc(act_done, 1)
            f(gate[:, :, :], g, ACT.Sigmoid).then_inc(act_done, 1)
            act.wait_ge(norm_in, 1)
            f(ss[:, :], ss[:, :], ACT.Sqrt).then_inc(act_done, 1)
            act.wait_ge(var_in, 1)
            f(var[:, :], var[:, :], ACT.Sqrt, bias=eps[:, 0:1], scale=1.0 / HD).then_inc(act_done, 1)

        @block.gpsimd
        def _(pool):
            tt = nc.gpsimd.tensor_tensor
            link = same_engine(pool, pool_chain)
            pool.wait_ge(ready, 1)
            pool.wait_ge(act_done, 2)
            for t in range(DEC_T):
                if t:
                    pool.wait_ge(decayed, t)
                link(tt(outer[:, :, :], over_j(v[:, t, :]), last_dim(k2, t), ALU.mult))
                if t:
                    pool.wait_ge(state_new, t)
                link(tt(Sw[:, :, :], S[:, :, :], last_dim(w, t), ALU.mult))
                tt(Sw[:, :, :], Sw[:, :, :], outer[:, :, :], ALU.add).then_inc(decayed, 1)

        @block.vector
        def _(dve):
            link = same_engine(dve, chain)
            vv = nc.vector
            tt, ts, stt = vv.tensor_tensor, vv.tensor_scalar, vv.scalar_tensor_tensor
            red = lambda out, x: vv.reduce_sum(out, x, axis=AX.X)
            vv.memset(eps[:, :], GN_EPS)
            dve.wait_ge(loaded, 48)
            link(tt(kraw[:, :, :], k, over_t(0), ALU.mult))
            link(tt(sq[:, :, :], kraw[:, :, :], kraw[:, :, :], ALU.mult))
            link(red(ss[:, :], sq[:, :, :]))
            ts(ss[:, :], ss[:, :], 1e-24, None, ALU.max).then_inc(norm_in, 1)
            link(ts(k2[:, :, :], a, 1.0, None, ALU.subtract))
            link(tt(k2[:, :, :], k2[:, :, :], over_t(1), ALU.mult))
            link(stt(out=k2[:, :, :], in0=k2[:, :, :], scalar=1.0, in1=k, op0=ALU.add, op1=ALU.mult))
            dve.wait_ge(act_done, 3)
            link(vv.reciprocal(ss[:, :], ss[:, :]))
            link(tt(kk[:, :, :], kraw[:, :, :], over_d(ss), ALU.mult))
            tt(b[:, :, :], kk[:, :, :], a, ALU.mult).then_inc(ready, 1)
            dve.wait_ge(ready, 1)
            for t in range(DEC_T):
                link(tt(prod[:, :, :], S[:, :, :], last_dim(kk, t), ALU.mult))
                link(red(sa[:, :], prod[:, :, :]))
                link(tt(prod[:, :, :], over_j(sa), last_dim(b, t), ALU.mult))
                dve.wait_ge(decayed, t + 1)
                tt(S[:, :, :], Sw[:, :, :], prod[:, :, :], ALU.subtract).then_inc(state_new, 1)
                dve.wait_ge(state_new, t + 1)
                link(tt(prod[:, :, :], S[:, :, :], last_dim(X[:, t], 0), ALU.mult))
                link(red(o[:, t, :], prod[:, :, :]))
            link(red(mean[:, :], o[:, :, :]))
            link(ts(mean[:, :], mean[:, :], 1.0 / HD, None, ALU.mult))
            link(tt(oc[:, :, :], o[:, :, :], over_d(mean), ALU.subtract))
            link(tt(sq[:, :, :], oc[:, :, :], oc[:, :, :], ALU.mult))
            red(var[:, :], sq[:, :, :]).then_inc(var_in, 1)
            link(tt(rk[:, :, :], r, k2[:, :, :], ALU.mult))
            link(tt(rk[:, :, :], rk[:, :, :], over_t(2), ALU.mult))
            link(red(bonus[:, :], rk[:, :, :]))
            link(tt(rk[:, :, :], v, over_d(bonus), ALU.mult))
            dve.wait_ge(act_done, 4)
            link(vv.reciprocal(var[:, :], var[:, :]))
            link(tt(oc[:, :, :], oc[:, :, :], over_d(var), ALU.mult))
            link(tt(oc[:, :, :], oc[:, :, :], over_t(3), ALU.mult))
            link(tt(oc[:, :, :], oc[:, :, :], over_t(4), ALU.add))
            link(tt(oc[:, :, :], oc[:, :, :], rk[:, :, :], ALU.add))
            link(tt(gate[:, :, :], gate[:, :, :], g, ALU.mult))
            tt(o[:, :, :], oc[:, :, :], gate[:, :, :], ALU.mult).then_inc(o_done, 1)


STRIDE = 16
N_CHUNK = PAST // STRIDE


def compress(nc, A):
    with ExitStack() as ctx:
        sb = lambda name, shape: ctx.enter_context(nc.sbuf_tensor(name, shape, F32))
        sem = nc.alloc_semaphore
        table = ctx.enter_context(nc.sbuf_tensor("table", [1, DEC_B * N_PAGES], I32))
        X = [sb(f"rows{i}", [P, STRIDE, KVW]) for i in range(2)]
        pw = sb("pos_w", [P, 4, STRIDE, HD])
        prod = [sb(f"prod{i}", [P, STRIDE, 2 * P]) for i in range(4)]
        C = sb("C", [P, 4, 2 * P])
        pooled, kv = sb("pooled", [P, 4, P]), sb("kv", [P, 4, P])
        ident, shift = sb("c_ident", [P, P]), sb("c_shift", [P, P])
        wbd = sb("wbd", [P, 2, P])
        ps_pool = ctx.enter_context(nc.psum_tensor("ps_pool", [P, 4, P], F32))
        ps_proj = ctx.enter_context(nc.psum_tensor("ps_proj", [P, 4, P], F32))
        consts, wts, zeroed = sem("c_consts"), sem("c_wts"), sem("c_zeroed")
        rows = [sem(f"c_rows{i}") for i in range(2)]
        pool_mul, dve_mul, C_ready, C_free = sem("c_pool_mul"), sem("c_dve_mul"), sem("c_C_ready"), sem("c_C_free")
        prod_free, used_pool, used_dve = sem("c_prod_free"), sem("c_used_pool"), sem("c_used_dve")
        pool_mm, pooled_ready, proj_mm, kv_ready, kv_sent = (
            sem("c_" + n) for n in ("pool_mm", "pooled_ready", "proj_mm", "kv_ready", "kv_sent"))
        x_zero, table_in = sem("c_x_zero"), sem("c_table")
        block = ctx.enter_context(nc.Block())
        NB = DEC_B + 1

        @block.sync
        def _(sp):
            sp.dma_start(table[:, :], A["page_table"]).then_inc(table_in, 16)
            sp.wait_ge(table_in, 16)

            def load_rows(b, slot):
                for p in range(N_PAGES):
                    page = sp.value_load(table[0:1, bass.ds(b * N_PAGES + p, 1)], min_val=0, max_val=N_POOL - 1)
                    sp.dma_start(X[slot][8 * p:8 * p + 8, :, :].rearrange("p s c -> p (s c)"),
                                 A["cmp_rows"][bass.ds(page, 1)].rearrange("a n x -> (a n) x"),
                                 max_dma_last_dim=8192).then_inc(rows[slot], 16)
            load_rows(0, 0)
            load_rows(1, 1)
            for dst, src in ((pw, "pos_w"), (ident, "ident"), (shift, "shift1")):
                sp.dma_start(dst[:], A[src]).then_inc(consts, 16)
            sp.wait_ge(zeroed, 1)
            for k, src in enumerate(("w_cmp_k", "w_cmp_v")):
                for h in range(2):
                    sp.dma_start(wbd[h * HD:(h + 1) * HD, k, h * HD:(h + 1) * HD], A[src]).then_inc(wts, 16)
            with sp.Fori(1, 4) as i:
                for j in range(2):
                    sp.wait_ge(used_pool, i * 2 + j - 1)
                    sp.wait_ge(used_dve, i * 2 + j - 1)
                    load_rows(i * 2 + j, j)
            sp.wait_ge(x_zero, 1)
            for t in range(4):
                src = A["u_tok"][:, t, P:P + KVW].rearrange("(n s) c -> n s c", s=STRIDE)
                sp.dma_start(X[0][8 * t:8 * t + 8, :, :], src).then_inc(rows[0], 16)

        def loop(eng, body, chain=None):
            with eng.Fori(0, 4) as i:
                for j in range(2):
                    body(i * 2 + j, j)
            body(8, 0)

        def rows_in(eng, b, slot):
            if isinstance(b, int):
                eng.wait_ge(rows[0], 16 * (4 * N_PAGES + 4))
            else:
                eng.wait_ge(rows[slot], (b - slot) * 8 * N_PAGES + 16 * N_PAGES)

        def multiply(eng, slot, kvr):
            x = X[slot][:, :, (kvr // 2) * 2 * P:(kvr // 2 + 1) * 2 * P].rearrange("p s (g d) -> p s g d", d=HD)
            w = pw[:, kvr, :, None, :].to_broadcast([P, STRIDE, 4, HD])
            out = prod[kvr][:, :, :].rearrange("p s (g d) -> p s g d", d=HD)
            return eng.tensor_tensor(out, x, w, ALU.mult)

        @block.gpsimd
        def _(pool):
            nc.gpsimd.memset(wbd[:, :, :], 0.0).then_inc(zeroed, 1)
            pool.wait_ge(consts, 48)

            def body(b, slot):
                rows_in(pool, b, slot)
                pool.wait_ge(prod_free, b * 1 + 1)
                multiply(nc.gpsimd, slot, 2).then_inc(pool_mul, 1)
                multiply(nc.gpsimd, slot, 3).then_inc(pool_mul, 1)
                pool.wait_ge(pool_mul, b * 2 + 2)
                pool.sem_inc(used_pool, 1)
            loop(pool, body)

        @block.vector
        def _(dve):
            dve.sem_inc(prod_free, 1)
            dve.wait_ge(consts, 48)

            def body(b, slot):
                if isinstance(b, int):
                    dve.wait_ge(used_pool, 7)
                    nc.vector.memset(X[0][:, :, :], 0.0).then_inc(x_zero, 1)
                rows_in(dve, b, slot)
                multiply(nc.vector, slot, 0).then_inc(dve_mul, 1)
                multiply(nc.vector, slot, 1).then_inc(dve_mul, 1)
                dve.wait_ge(dve_mul, b * 2 + 2)
                dve.sem_inc(used_dve, 1)
                dve.wait_ge(C_free, b * 1 + 1)
                for kvr in range(4):
                    if kvr == 2:
                        dve.wait_ge(pool_mul, b * 2 + 2)
                    ins = nc.vector.reduce_sum(C[:, kvr, :], prod[kvr][:, :, :].rearrange("p s c -> p c s"),
                                               axis=AX.X)
                ins.then_inc(C_ready, 1)
                dve.wait_ge(C_ready, b * 1 + 1)
                dve.sem_inc(prod_free, 1)
            loop(dve, body)

        @block.tensor
        def _(pe):
            pe.wait_ge(consts, 48)
            pe.wait_ge(wts, 64)

            def body(b, slot):
                pe.wait_ge(C_ready, b * 1 + 1)
                for kv_ in range(2):
                    for gp in range(2):
                        c = slice(gp * P, (gp + 1) * P)
                        nc.tensor.matmul(ps_pool[:, 2 * kv_ + gp, :], C[:, 2 * kv_, c], ident[:, :],
                                         start=True, stop=False)
                        ins = nc.tensor.matmul(ps_pool[:, 2 * kv_ + gp, :], C[:, 2 * kv_ + 1, c], shift[:, :],
                                               start=False, stop=True)
                ins.then_inc(pool_mm, 1)
                pe.wait_ge(pooled_ready, b * 1 + 1)
                for gp in range(2):
                    nc.tensor.matmul(ps_proj[:, gp, :], wbd[:, 0, :], pooled[:, gp, :], start=True, stop=True)
                for gp in range(2):
                    ins = nc.tensor.matmul(ps_proj[:, 2 + gp, :], pooled[:, 2 + gp, :], wbd[:, 1, :],
                                           start=True, stop=True)
                ins.then_inc(proj_mm, 1)
            loop(pe, body)

        @block.scalar
        def _(act):
            act.sem_inc(kv_sent, 32)
            act.sem_inc(C_free, 1)

            def body(b, slot):
                act.wait_ge(pool_mm, b * 1 + 1)
                nc.scalar.activation(pooled[:, :, :], ps_pool[:, :, :], ACT.Copy).then_inc(pooled_ready, 1)
                act.wait_ge(pooled_ready, b * 1 + 1)
                act.sem_inc(C_free, 1)
                act.wait_ge(proj_mm, b * 1 + 1)
                act.wait_ge(kv_sent, b * 32 + 32)
                nc.scalar.activation(kv[:, :, :], ps_proj[:, :, :], ACT.Copy).then_inc(kv_ready, 1)
                act.wait_ge(kv_ready, b * 1 + 1)
                act.dma_start(A["kcT"][bass.ds(b, 1)].rearrange("a k p n -> (a p) k n"), kv[:, 0:2, :])\
                    .then_inc(kv_sent, 16)
                act.dma_start(A["vc"][bass.ds(b, 1)].rearrange("a p k n -> (a p) k n"), kv[:, 2:4, :])\
                    .then_inc(kv_sent, 16)
            loop(act, body)
            act.wait_ge(kv_sent, 32 * (NB + 1))


N_TILE = SEQ // P
G_KV = 4
REP = 4
N_CMP_PAD = 32


def attend_prompt(nc, A):
    UNITS = [(r, t) for r in range(REP) for t in range(N_TILE)]
    NU = len(UNITS)
    with ExitStack() as ctx:
        sb = lambda name, shape: ctx.enter_context(nc.sbuf_tensor(name, shape, F32))
        sem = nc.alloc_semaphore
        psum = lambda name: ctx.enter_context(nc.psum_tensor(name, [P, 512], F32))
        q = [sb(f"a_q{j}", [HD, REP, SEQ]) for j in range(2)]
        kT = [sb(f"a_kT{j}", [HD, 2, SEQ]) for j in range(2)]
        vv = [sb(f"a_v{j}", [P, 2, N_TILE, HD]) for j in range(2)]
        kcT = [sb(f"a_kcT{j}", [HD, N_CMP_PAD]) for j in range(2)]
        vc = [sb(f"a_vc{j}", [N_CMP_PAD, HD]) for j in range(2)]
        bias = [sb(f"a_bias{j}", [P, REP, SEQ]) for j in range(2)]
        cbias = [sb(f"a_cbias{j}", [P, NU, N_CMP_PAD]) for j in range(2)]
        gates = [sb(f"a_gates{j}", [P, N_TILE, 3, REP]) for j in range(2)]
        ident, cmask = sb("a_ident", [P, P]), sb("a_cmask", [P, N_TILE, N_CMP_PAD])
        S = [sb(f"a_S{j}", [P, 2, SEQ]) for j in range(2)]
        Pm = [sb(f"a_P{j}", [P, 2, SEQ]) for j in range(2)]
        PT = [sb(f"a_PT{j}", [P, 2, SEQ]) for j in range(2)]
        Sc, Pc = sb("a_Sc", [P, NU, N_CMP_PAD]), sb("a_Pc", [P, NU, N_CMP_PAD])
        PTc = [sb(f"a_PTc{j}", [N_CMP_PAD, P]) for j in range(2)]
        cmax, csum, coef_c = sb("a_cmax", [P, NU]), sb("a_csum", [P, NU]), sb("a_coef_c", [P, NU])
        mx, sums, coef = sb("a_mx", [P, 2, 2]), sb("a_sums", [P, 4, 2]), sb("a_coef", [P, 2, 2])
        acc = sb("a_acc", [P, HD])
        out = [sb(f"a_out{j}", [P, N_TILE, REP, HD]) for j in range(2)]
        s_bank = [[psum(f"s_{n}{j}") for n in ("sel", "win")] for j in range(2)]
        pt_bank = [psum("pt_sel"), psum("pt_win")]
        c_bank, o_bank = psum("c_bank"), psum("o_bank")

        consts, g_in = sem("a_consts"), [sem(f"a_in{j}") for j in range(2)]
        q_scaled, c_scores, c_sub, c_exp, c_ready, gate_done = (
            sem("a_" + n) for n in ("q_scaled", "c_scores", "c_sub", "c_exp", "c_ready", "gate_done"))
        scores, max_ready, exp_done, t_done, evA, evB, pv_done, out_done = (
            sem("a_" + n) for n in ("scores", "max_ready", "exp_done", "t_done", "evA", "evB", "pv_done", "out_done"))
        chain, sent, cmax_ready = sem("a_chain"), sem("a_sent"), sem("a_cmax_ready")
        freed = sem("a_freed")
        settled, settled_dve = sem("a_settled"), sem("a_settled_dve")
        block = ctx.enter_context(nc.Block())
        N_IN = 13

        def keys(t):
            return (t + 1) * P

        @block.sync
        def _(sp):
            sp.dma_start(ident[:, :], A["ident"]).then_inc(consts, 16)
            sp.dma_start(cmask[:, :, :], A["cmask"]).then_inc(consts, 16)
            with sp.Fori(0, 2) as i:
                for j in range(2):
                    g = i * 2 + j
                    sp.wait_ge(freed, g + 1)
                    rows = lambda base: A["uT"][bass.ds(g * HD + base, HD), 0:SEQ]
                    dma = lambda dst, src: sp.dma_start(dst, src).then_inc(g_in[j], 16)
                    dma(q[j][:, :, :], A["uT"][bass.ds(g * (REP * HD) + COL_Q, REP * HD), 0:SEQ]
                        .rearrange("(r d) n -> d r n", r=REP))
                    dma(kT[j][:, 0, :], rows(COL_S))
                    dma(kT[j][:, 1, :], rows(COL_W))
                    for k, col in enumerate((COL_S, COL_W)):
                        c0 = col + 2 * P - 48 * P
                        dma(vv[j][:, k, :, :], A["u_tok"][:, :, bass.ds(g * HD + c0, HD)])
                    dma(kcT[j][:, :], A["kcT"][DEC_B, i, j * HD:(j + 1) * HD, 0:N_CMP_PAD]
                        if isinstance(i, int) else
                        A["kcT"][DEC_B][bass.ds(i, 1)].rearrange("a p n -> (a p) n")[j * HD:(j + 1) * HD, 0:N_CMP_PAD])
                    dma(vc[j][:, :], A["vc"][DEC_B, 0:N_CMP_PAD, :, :].rearrange("p k n -> p (k n)")
                        [:, bass.ds(g * HD, HD)])
                    for t in range(N_TILE):
                        dma(gates[j][:, t, :, :], A["u_tok"][:, t, COL_GATE - 48 * P:COL_GATE - 48 * P + N_GATE]
                            .rearrange("p (b g r) -> g p b r", b=3, g=G_KV)[bass.ds(g, 1)]
                            .rearrange("a p b r -> (a p) b r"))
                    dma(bias[j][:, :, :], A["bias_p"][bass.ds(g, 1)].rearrange("a p r n -> (a p) r n"))
                    dma(cbias[j][:, :, :], A["cbias_p"][bass.ds(g, 1)].rearrange("a p u n -> (a p) u n"))

        @block.scalar
        def _(act):
            f = nc.scalar.activation
            act.sem_inc(freed, 2)
            with act.Fori(0, 2) as i:
                for j in range(2):
                    g = i * 2 + j
                    act.wait_ge(g_in[j], i * 16 * N_IN + 16 * N_IN)
                    f(q[j][:, :, :], q[j][:, :, :], ACT.Copy, scale=HD ** -0.5).then_inc(q_scaled, 1)
                    f(gates[j][:, :, :, :], gates[j][:, :, :, :], ACT.Sigmoid).then_inc(gate_done, 1)

                    def exps(u):
                        r, t = UNITS[u]
                        act.wait_ge(max_ready, g * NU + u + 1)
                        for k in range(2):
                            ins = f(Pm[u % 2][:, k, 0:keys(t)], S[u % 2][:, k, 0:keys(t)], ACT.Exp,
                                    bias=mx[:, u % 2, k:k + 1], accum_out=sums[:, u % 4, k:k + 1])
                        ins.then_inc(exp_done, 1)
                    act.wait_ge(c_sub, g + 1)
                    f(Pc[:, :, :], Sc[:, :, :], ACT.Exp).then_inc(c_exp, 1)
                    exps(0)
                    for u, (r, t) in enumerate(UNITS):
                        if u + 1 < NU:
                            exps(u + 1)
                        act.wait_ge(t_done, g * NU + u + 1)
                        f(PT[u % 2][:, 0, 0:keys(t)], pt_bank[0][:, 0:keys(t)], ACT.Copy)
                        f(PTc[u % 2][:, :], c_bank[0:N_CMP_PAD, 0:P], ACT.Copy).then_inc(evA, 1)
                    act.wait_ge(out_done, g * NU + NU)
                    act.dma_start(A["obN"][:, :, bass.ds(g * (REP * HD), REP * HD)],
                                  out[j][:, :, :, :].rearrange("p t r d -> p t (r d)")).then_inc(sent, 16)
                    act.wait_ge(sent, g * 16 + 16)
                    act.sem_inc(freed, 1)

        @block.vector
        def _(dve):
            v = nc.vector
            link = same_engine(dve, chain)
            dve.wait_ge(consts, 32)
            with dve.Fori(0, 2) as i:
                for j in range(2):
                    g = i * 2 + j

                    def maxes(u):
                        r, t = UNITS[u]
                        dve.wait_ge(scores, g * NU + u + 1)
                        dve.sem_inc(settled_dve, 1)
                        for k in range(2):
                            last = v.tensor_tensor_reduce(
                                out=S[u % 2][:, k, 0:keys(t)], in0=s_bank[u % 2][k][:, 0:keys(t)],
                                in1=bias[j][:, r, SEQ - keys(t):SEQ], scale=1.0, scalar=-3e38,
                                op0=ALU.add, op1=ALU.max, accum_out=mx[:, u % 2, k:k + 1])
                        link(last)
                        v.tensor_scalar(mx[:, u % 2, :], mx[:, u % 2, :], -1.0, None, ALU.mult).then_inc(max_ready, 1)
                    dve.wait_ge(c_scores, g + 1)
                    link(v.tensor_tensor(Sc[:, :, :], c_bank[:, :].rearrange("p (u n) -> p u n", n=N_CMP_PAD),
                                         cbias[j][:, :, :], ALU.add))
                    link(v.tensor_reduce(cmax[:, :], Sc[:, :, :], axis=AX.X, op=ALU.max))
                    v.tensor_tensor(Sc[:, :, :], Sc[:, :, :], cmax[:, :, None].to_broadcast([P, NU, N_CMP_PAD]),
                                    ALU.subtract).then_inc(c_sub, 1)
                    maxes(0)
                    dve.wait_ge(c_exp, g + 1)
                    for r in range(REP):
                        last = v.tensor_tensor(Pc[:, 4 * r:4 * r + 4, :], Pc[:, 4 * r:4 * r + 4, :], cmask[:, :, :],
                                               ALU.mult)
                    last.then_inc(c_ready, 1)
                    dve.wait_ge(c_ready, g + 1)
                    link(v.reduce_sum(csum[:, :], Pc[:, :, :], axis=AX.X))
                    link(v.tensor_scalar(csum[:, :], csum[:, :], 1e-30, None, ALU.max))
                    link(v.reciprocal(csum[:, :], csum[:, :]))
                    dve.wait_ge(gate_done, g + 1)
                    link(v.tensor_tensor(coef_c[:, :].rearrange("p (r t) -> p r t", t=N_TILE),
                                         csum[:, :].rearrange("p (r t) -> p r t", t=N_TILE),
                                         gates[j][:, :, 0, :].rearrange("p t r -> p r t"), ALU.mult))

                    def outs(u):
                        r, t = UNITS[u]
                        link(v.reciprocal(coef[:, u % 2, :], sums[:, u % 4, :]))
                        link(v.tensor_tensor(coef[:, u % 2, :], coef[:, u % 2, :], gates[j][:, t, 1:3, r], ALU.mult))
                        dve.wait_ge(pv_done, g * NU + u + 1)
                        o = lambda k: o_bank[:, k * HD:(k + 1) * HD]
                        dst = out[j][:, t, r, :]
                        link(v.tensor_scalar(acc[:, :], o(0), coef[:, u % 2, 0:1], None, ALU.mult))
                        link(v.scalar_tensor_tensor(out=acc[:, :], in0=o(1), scalar=coef[:, u % 2, 1:2], in1=acc[:, :],
                                                    op0=ALU.mult, op1=ALU.add))
                        v.scalar_tensor_tensor(out=dst, in0=o(2), scalar=coef_c[:, u:u + 1],
                                               in1=acc[:, :], op0=ALU.mult, op1=ALU.add).then_inc(out_done, 1)
                    for u, (r, t) in enumerate(UNITS):
                        if u + 1 < NU:
                            maxes(u + 1)
                        dve.wait_ge(t_done, g * NU + u + 1)
                        v.tensor_copy(PT[u % 2][:, 1, 0:keys(t)], pt_bank[1][:, 0:keys(t)]).then_inc(evB, 1)
                        if u:
                            outs(u - 1)
                    outs(NU - 1)
                link.restart()

        @block.tensor
        def _(pe):
            mm = nc.tensor.matmul
            settle = lambda: pe.sem_inc(settled, 1)
            pe.wait_ge(consts, 32)
            with pe.Fori(0, 2) as i:
                for j in range(2):
                    g = i * 2 + j

                    def score(u):
                        r, t = UNITS[u]
                        if u >= 2:
                            pe.wait_ge(max_ready, g * NU + u - 1)
                            settle()
                        for k in range(2):
                            ins = mm(s_bank[u % 2][k][:, 0:keys(t)], q[j][:, r, t * P:(t + 1) * P],
                                     kT[j][:, k, 0:keys(t)], start=True, stop=True)
                        ins.then_inc(scores, 1)
                    pe.wait_ge(q_scaled, g + 1)
                    settle()
                    for u, (r, t) in enumerate(UNITS):
                        ins = mm(c_bank[:, u * N_CMP_PAD:(u + 1) * N_CMP_PAD], q[j][:, r, t * P:(t + 1) * P],
                                 kcT[j][:, :], start=True, stop=True)
                    ins.then_inc(c_scores, 1)
                    score(0)

                    def values(u):
                        r, t = UNITS[u]
                        pe.wait_ge(evA, g * NU + u + 1)
                        pe.wait_ge(evB, g * NU + u + 1)
                        if u:
                            pe.wait_ge(out_done, g * NU + u)
                        settle()
                        for k in range(2):
                            for b in range(t + 1):
                                mm(o_bank[:, k * HD:(k + 1) * HD], PT[u % 2][:, k, b * P:(b + 1) * P],
                                   vv[j][:, k, b, :], start=(b == 0), stop=(b == t))
                        mm(o_bank[:, 2 * HD:3 * HD], PTc[u % 2][:, :], vc[j][:, :], start=True, stop=True)\
                            .then_inc(pv_done, 1)
                    for u, (r, t) in enumerate(UNITS):
                        if u + 1 < NU:
                            score(u + 1)
                        pe.wait_ge(exp_done, g * NU + u + 1)
                        if u == 0:
                            pe.wait_ge(c_ready, g + 1)
                        else:
                            pe.wait_ge(evA, g * NU + u)
                            pe.wait_ge(evB, g * NU + u)
                        settle()
                        for k in range(2):
                            for b in range(t + 1):
                                nc.tensor.transpose(pt_bank[k][:, b * P:(b + 1) * P],
                                                    Pm[u % 2][:, k, b * P:(b + 1) * P], ident[:, :])
                        nc.tensor.transpose(c_bank[0:N_CMP_PAD, 0:P], Pc[:, u, :], ident[:, :]).then_inc(t_done, 1)
                        if u:
                            values(u - 1)
                    values(NU - 1)
                    pe.wait_ge(out_done, g * NU + NU)
                    settle()


S_SEL, S_SNEW, S_WIN, S_WNEW, S_CMP, S_END = 0, 2048, 2052, 2564, 2568, 2696
N_SELECT = 16


def attend_samples(nc, A):
    with ExitStack() as ctx:
        sb = lambda name, shape: ctx.enter_context(nc.sbuf_tensor(name, shape, F32))
        sem = nc.alloc_semaphore
        table = ctx.enter_context(nc.sbuf_tensor("d_table", [1, DEC_B * N_PAGES], I32))
        kT = [[sb(f"d_kT{j}{b}", [P, 2, PAST]) for b in range(2)] for j in range(2)]
        vS = [[sb(f"d_v{j}{b}", [P, N_PAGES, 2 * P]) for b in range(2)] for j in range(2)]
        kW, vW = ([sb(f"d_{n}{b}", [P, 2, WINDOW]) for b in range(2)] for n in ("kW", "vW"))
        kC, vC = ([sb(f"d_{n}{b}", [P, 2, P]) for b in range(2)] for n in ("kC", "vC"))
        vN = [sb(f"d_vN{b}", [DEC_T, 2, 2 * P]) for b in range(2)]
        q_raw, q_all = sb("d_q_raw", [P, 2, REP, NS]), sb("d_q_all", [P, DEC_B, 2, 32])
        q = sb("d_q", [P, 2, 2, 32])
        kN_all, kN = sb("d_kN_all", [P, 2, 2, NS]), sb("d_kN", [P, 2, 2, 2, DEC_T])
        bias, S, PT = sb("d_bias", [P, S_END]), sb("d_S", [P, S_END]), sb("d_PT", [P, N_PAGES, P])
        PTc, PTw, PTn = sb("d_PTc", [P, P]), sb("d_PTw", [P, 4, P]), sb("d_PTn", [DEC_T, 2, P])
        ident, gsum, overlap = sb("d_ident", [P, P]), sb("d_gsum", [P, P]), sb("d_overlap", [P, N_SEL])
        selc = sb("d_selc", [P, 2, N_SEL])
        lower = sb("d_lower", [P, N_SEL, N_SEL])
        gmask = sb("d_gmask", [P, G_KV])
        imp, score, rank, mb = (sb("d_" + n, [P, N_SEL]) for n in ("imp", "score", "rank", "mb"))
        gt, eq = sb("d_gt", [P, N_SEL, N_SEL]), sb("d_eq", [P, N_SEL, N_SEL])
        mx, nmx, sums, coef = sb("d_mx", [P, 3]), sb("d_nmx", [P, 3]), sb("d_sums", [P, 3]), sb("d_coef", [P, 3])
        gates = sb("d_gates", [P, 4, 3])
        gates_now = sb("d_gates_now", [P, 3])
        acc, o = sb("d_acc", [P, G_KV, HD]), sb("d_o", [P, HD])
        psum = lambda name: ctx.enter_context(nc.psum_tensor(name, [P, 512], F32))
        sc = [psum("d_sc0"), psum("d_sc1")]
        small, pt, ob, oc, ps_imp = psum("d_small"), [psum("d_pt0"), psum("d_pt1")], psum("d_ob"), psum("d_oc"), psum("d_ps_imp")

        names = ("consts", "table_in", "q_in", "zeroed", "q_ready", "set_up", "small_done", "small_out", "win_sc",
                 "c_exp", "c_norm", "c_max", "ptc_done", "ptc_out", "imp_done", "imp_out", "imp2_done", "w_max", "w_exp",
                 "s_max", "s_exp", "o_done", "freed", "sent", "settled", "chain", "o_ready", "sel_sc", "sel_out",
                 "pt_done", "pt_out", "gates_ready", "pv_c", "win_out", "ptn_done")
        s = {n: sem("d_" + n) for n in names}
        pages_in = [sem(f"d_pages_in{j}") for j in range(2)]
        rest_in = sem("d_rest_in")
        block = ctx.enter_context(nc.Block())
        N_REST = 10
        GROUPS = [(kind, n) for kind in ("w", "s") for n in range(1 if kind == "w" else 4)]

        @block.sync
        def _(sp):
            sp.dma_start(table[:, :], A["page_table"]).then_inc(s["table_in"], 16)
            for dst, src in ((ident, "ident"), (gsum, "gsum"), (overlap, "overlap"), (selc, "selc"), (lower, "lower"),
                             (gmask, "gmask"), (bias, "bias_s")):
                sp.dma_start(dst[:], A[src]).then_inc(s["consts"], 16)
            for g2 in range(2):
                for gp in range(2):
                    row = COL_Q + (2 * gp + g2) * REP * HD
                    sp.dma_start(q_raw[g2 * HD:(g2 + 1) * HD, gp, :, :],
                                 A["uT"][row:row + REP * HD, SEQ:NT].rearrange("(r d) n -> d r n", r=REP))\
                        .then_inc(s["q_in"], 16)
            for k, col in enumerate((COL_S, COL_W)):
                sp.dma_start(kN_all[:, k, :, :], A["uT"][col:col + 2 * P, SEQ:NT].rearrange("(g p) n -> p g n", g=2))\
                    .then_inc(s["q_in"], 16)
            with nc.allow_non_contiguous_dma(reason="gates: 1536 values in all"):
                for b in range(DEC_B):
                    for g in range(G_KV):
                        p0 = (b % 2) * HD + g * 16
                        for br in range(3):
                            c = COL_GATE + br * 16 + g * REP
                            sp.dma_start(gates[p0:p0 + 16, b // 2, br:br + 1],
                                         A["u_tail"][1 + 4 * b:5 + 4 * b, c:c + REP][:, :, None]).then_inc(s["q_in"], 16)
            sp.wait_ge(s["table_in"], 16)
            with sp.Fori(0, 2) as i:
                for j in range(2):
                    bp = i * 2 + j
                    sp.wait_ge(s["freed"], bp + 2)
                    for b2 in range(2):
                        for p in range(N_PAGES):
                            page = sp.value_load(table[0:1, bass.ds(bp * (2 * N_PAGES) + b2 * N_PAGES + p, 1)],
                                                 min_val=0, max_val=N_POOL - 1)
                            sp.dma_start(kT[j][b2][:, :, p * P:(p + 1) * P],
                                         A["sel_k"][bass.ds(page, 1)].rearrange("a k p n -> p (a k) n"))\
                                .then_inc(pages_in[j], 16)
                            sp.dma_start(vS[j][b2][:, p, :], A["sel_v"][bass.ds(page, 1)]
                                         .rearrange("a p n -> (a p) n")).then_inc(pages_in[j], 16)
                    sp.wait_ge(s["freed"], bp + 3)
                    for b2 in range(2):
                        b = bp * 2 + b2
                        one = lambda name: A[name][bass.ds(b, 1)]
                        for dst, src in ((kW[b2][:, :, :], one("win_k").rearrange("a k p n -> p (a k) n")),
                                         (vW[b2][:, :, :].rearrange("p a (c n) -> p (a c) n", n=2 * P),
                                          one("win_v").rearrange("a p t n -> (a p) t n")),
                                         (kC[b2][:, :, :], one("kcT").rearrange("a k p n -> p (a k) n")),
                                         (vC[b2][:, :, :], one("vc").rearrange("a p k n -> (a p) k n")),
                                         (vN[b2][:, :, :], A["u_tail"][bass.ds(b * DEC_T + 1, DEC_T), COL_S + 2 * P:COL_W + 4 * P]
                                          .rearrange("p (k n) -> p k n", n=2 * P)[:, 0:3:2, :])):
                            sp.dma_start(dst, src).then_inc(rest_in, 16)

        @block.scalar
        def _(act):
            f = nc.scalar.activation
            act.sem_inc(s["freed"], 3)
            act.wait_ge(s["q_in"], 16 * (6 + 96))
            act.wait_ge(s["zeroed"], 1)
            for g2 in range(2):
                rows = slice(g2 * HD, (g2 + 1) * HD)
                for gp in range(2):
                    ins = f(q_all[rows, :, gp, g2 * 16:(g2 + 1) * 16].rearrange("p b (t r) -> p b t r", r=REP),
                            q_raw[rows, gp, :, :].rearrange("p r (b t) -> p b t r", t=DEC_T), ACT.Copy, scale=HD ** -0.5)
            ins.then_inc(s["q_ready"], 1)
            f(gates[:, :, :], gates[:, :, :], ACT.Sigmoid).then_inc(s["gates_ready"], 1)
            with act.Fori(0, 2) as i:
                for j in range(2):
                    bp = i * 2 + j
                    w = lambda name, n=1, k=1: act.wait_ge(s[name], bp * n + k)

                    def soft(name, a, b, k):
                        f(S[:, a:b], S[:, a:b], ACT.Exp, bias=nmx[:, k:k + 1], accum_out=sums[:, k:k + 1])\
                            .then_inc(s[name], 1)
                    w("c_max")
                    soft("c_exp", S_CMP, S_END, 2)
                    w("ptc_done")
                    f(PTc[:, :], pt[0][:, 0:P], ACT.Copy).then_inc(s["ptc_out"], 1)
                    w("imp_done")
                    f(imp[:, :], ps_imp[:, 0:N_SEL], ACT.Copy).then_inc(s["imp_out"], 1)
                    w("w_max")
                    soft("w_exp", S_WIN, S_CMP, 1)
                    w("pt_done", 5, 1)
                    f(PTw[:, :, :], pt[1][:, :].rearrange("p (k n) -> p k n", k=4), ACT.Copy).then_inc(s["pt_out"], 1)
                    w("s_max")
                    soft("s_exp", S_SEL, S_WIN, 0)
                    w("ptn_done")
                    f(PTn[:, :, :], ps_imp[0:DEC_T, 0:2 * P].rearrange("p (k n) -> p k n", k=2), ACT.Copy)\
                        .then_inc(s["pt_out"], 1)
                    for n in range(4):
                        w("pt_done", 5, n + 2)
                        f(PT[:, 4 * n:4 * n + 4, :], pt[n % 2][:, :].rearrange("p (k n) -> p k n", k=4), ACT.Copy)\
                            .then_inc(s["pt_out"], 1)
                    w("o_ready")
                    act.dma_start(A["obS"][bass.ds(bp, 1)].rearrange("a p n -> (a p) n"), o[:, :]).then_inc(s["sent"], 16)
                    w("sent", 16, 16)
                    act.sem_inc(s["freed"], 1)

        @block.vector
        def _(dve):
            v = nc.vector
            tt, ts, stt = v.tensor_tensor, v.tensor_scalar, v.scalar_tensor_tensor
            link = same_engine(dve, s["chain"])
            v.memset(q_all[:, :, :, :], 0.0).then_inc(s["zeroed"], 1)
            dve.wait_ge(s["consts"], 16 * 7)
            dve.wait_ge(s["q_ready"], 1)
            dve.wait_ge(s["gates_ready"], 1)
            with dve.Fori(0, 2) as i:
                for j in range(2):
                    bp = i * 2 + j
                    w = lambda name, n=1, k=1: dve.wait_ge(s[name], bp * n + k)
                    w("freed", 1, 3)
                    v.tensor_copy(q[:, :, :, :], q_all[:, bass.ds(bp * 2, 2), :, :])
                    v.tensor_copy(gates_now[:, :], gates[:, bass.ds(bp, 1), :].rearrange("p a c -> p (a c)"))
                    for b2 in range(2):
                        last = v.tensor_copy(kN[:, b2, :, :, :], kN_all[:, :, :, bass.ds(bp * (2 * DEC_T) + b2 * DEC_T, DEC_T)])
                    last.then_inc(s["set_up"], 1)
                    w("small_done")
                    tt(S[:, S_CMP:S_END], small[:, 0:P], bias[:, S_CMP:S_END], ALU.add)
                    tt(S[:, S_SNEW:S_WIN], small[:, P:P + DEC_T], bias[:, S_SNEW:S_WIN], ALU.add)
                    link(tt(S[:, S_WNEW:S_CMP], small[:, P + DEC_T:P + 2 * DEC_T], bias[:, S_WNEW:S_CMP], ALU.add))

                    def neg_max(a, b, k, name):
                        link(v.reduce_max(mx[:, k:k + 1], S[:, a:b], axis=AX.X))
                        ts(nmx[:, k:k + 1], mx[:, k:k + 1], -1.0, None, ALU.mult).then_inc(s[name], 1)
                    neg_max(S_CMP, S_END, 2, "c_max")
                    for n in range(5):
                        w("sel_sc", 5, n + 1)
                        a = S_WIN if n == 0 else 512 * (n - 1)
                        tt(S[:, a:a + 512], sc[n % 2][:, :], bias[:, a:a + 512], ALU.add).then_inc(s["sel_out"], 1)
                        if n == 0:
                            w("sel_out", 5, 1)
                            neg_max(S_WIN, S_CMP, 1, "w_max")
                        if n == 1:
                            w("c_exp")
                            link(v.reciprocal(coef[:, 2:3], sums[:, 2:3]))
                            ts(S[:, S_CMP:S_END], S[:, S_CMP:S_END], coef[:, 2:3], None, ALU.mult).then_inc(s["c_norm"], 1)
                    w("sel_out", 5, 5)
                    w("imp2_done")
                    link(tt(score[:, :], ps_imp[:, 64:64 + N_SEL], selc[:, 0, :], ALU.mult))
                    link(tt(score[:, :], score[:, :], selc[:, 1, :], ALU.add))
                    si = score[:, None, :].to_broadcast([P, N_SEL, N_SEL])
                    sj = score[:, :, None].to_broadcast([P, N_SEL, N_SEL])
                    tt(gt[:, :, :], si, sj, ALU.is_gt)
                    link(tt(eq[:, :, :], si, sj, ALU.is_equal))
                    link(tt(eq[:, :, :], eq[:, :, :], lower[:, :, :], ALU.mult))
                    link(tt(gt[:, :, :], gt[:, :, :], eq[:, :, :], ALU.add))
                    link(v.reduce_sum(rank[:, :], gt[:, :, :], axis=AX.X))
                    link(ts(mb[:, :], rank[:, :], N_SELECT - 0.5, NEG, ALU.is_gt, ALU.mult))
                    link(tt(S[:, 0:PAST].rearrange("p (j k) -> p j k", k=SEL_BLOCK),
                            S[:, 0:PAST].rearrange("p (j k) -> p j k", k=SEL_BLOCK),
                            mb[:, 0:N_SEL - 1, None].to_broadcast([P, N_SEL - 1, SEL_BLOCK]), ALU.add))
                    link(ts(S[:, S_SNEW:S_WIN], S[:, S_SNEW:S_WIN], mb[:, N_SEL - 1:N_SEL], None, ALU.add))
                    neg_max(S_SEL, S_WIN, 0, "s_max")
                    w("s_exp")
                    w("w_exp")
                    link(v.reciprocal(coef[:, 0:2], sums[:, 0:2]))
                    link(tt(coef[:, 0:2], coef[:, 0:2], gates_now[:, 1:3], ALU.mult))
                    w("o_done")
                    flat = acc[:, :, :].rearrange("p g d -> p (g d)")
                    link(ts(flat, ob[:, 0:2 * P], coef[:, 0:1], None, ALU.mult))
                    link(stt(out=flat, in0=ob[:, 2 * P:4 * P], scalar=coef[:, 1:2], in1=flat, op0=ALU.mult, op1=ALU.add))
                    link(stt(out=flat, in0=oc[:, 0:2 * P], scalar=gates_now[:, 0:1], in1=flat, op0=ALU.mult, op1=ALU.add))
                    link(tt(acc[:, :, :], acc[:, :, :], gmask[:, :, None].to_broadcast([P, G_KV, HD]), ALU.mult))
                    v.reduce_sum(o[:, :], acc[:, :, :].rearrange("p g d -> p d g"), axis=AX.X).then_inc(s["o_ready"], 1)
                link.restart()

        @block.tensor
        def _(pe):
            mm = nc.tensor.matmul
            pe.wait_ge(s["consts"], 16 * 7)
            with pe.Fori(0, 2) as i:
                for j in range(2):
                    bp = i * 2 + j

                    def w(*conditions):
                        for name, n, k in conditions:
                            pe.wait_ge(s[name], bp * n + k)
                        pe.sem_inc(s["settled"], 1)
                    rows = lambda b2, gp: slice(b2 * HD + gp * 32, b2 * HD + gp * 32 + 32)
                    PAIRS = [(b2, gp) for b2 in range(2) for gp in range(2)]
                    pe.wait_ge(rest_in, bp * (16 * N_REST) + 16 * N_REST)
                    w(("set_up", 1, 1))
                    for b2, gp in PAIRS:
                        mm(small[rows(b2, gp), 0:P], q[:, b2, gp, :], kC[b2][:, gp, :], start=True, stop=True)
                        for k in range(2):
                            c = P + k * DEC_T
                            ins = mm(small[rows(b2, gp), c:c + DEC_T], q[:, b2, gp, :], kN[:, b2, k, gp, :],
                                     start=True, stop=True)
                    ins.then_inc(s["small_done"], 1)
                    for n in range(5):
                        if n >= 2:
                            w(("sel_out", 5, n - 1))
                        if n == 1:
                            pe.wait_ge(pages_in[j], i * (64 * 16) + 64 * 16)
                            pe.sem_inc(s["settled"], 1)
                        for b2, gp in PAIRS:
                            rhs = kW[b2][:, gp, :] if n == 0 else kT[j][b2][:, gp, 512 * (n - 1):512 * n]
                            ins = mm(sc[n % 2][rows(b2, gp), :], q[:, b2, gp, :], rhs, start=True, stop=True)
                        ins.then_inc(s["sel_sc"], 1)
                    w(("c_norm", 1, 1))
                    nc.tensor.transpose(pt[0][:, 0:P], S[:, S_CMP:S_END], ident[:, :]).then_inc(s["ptc_done"], 1)
                    w(("ptc_out", 1, 1))
                    mm(ps_imp[:, 0:N_SEL], PTc[:, :], overlap[:, :], start=True, stop=True).then_inc(s["imp_done"], 1)
                    w(("imp_out", 1, 1))
                    mm(ps_imp[:, 64:64 + N_SEL], gsum[:, :], imp[:, :], start=True, stop=True).then_inc(s["imp2_done"], 1)
                    halves = [slice(b2 * HD, (b2 + 1) * HD) for b2 in range(2)]
                    for b2, h in enumerate(halves):
                        mm(oc[h, 0:2 * P], PTc[:, h], vC[b2][:, :, :].rearrange("p a n -> p (a n)"), start=True, stop=True)
                    w(("w_exp", 1, 1))
                    for n in range(4):
                        ins = nc.tensor.transpose(pt[1][:, n * P:(n + 1) * P], S[:, S_WIN + n * P:S_WIN + (n + 1) * P],
                                                  ident[:, :])
                    ins.then_inc(s["pt_done"], 1)
                    w(("s_exp", 1, 1))
                    for k, c in enumerate((S_SNEW, S_WNEW)):
                        ins = nc.tensor.transpose(ps_imp[0:DEC_T, k * P:(k + 1) * P], S[:, c:c + DEC_T], ident[:, :])
                    ins.then_inc(s["ptn_done"], 1)
                    for n in range(4):
                        w(("pt_out", 6, 1 if n < 2 else n + 1))
                        for k in range(4):
                            c = (4 * n + k) * P
                            ins = nc.tensor.transpose(pt[n % 2][:, k * P:(k + 1) * P], S[:, c:c + P], ident[:, :])
                        ins.then_inc(s["pt_done"], 1)
                    w(("pt_out", 6, 6))
                    for b2, h in enumerate(halves):
                        for kind, tiles, pts, vals in ((0, N_PAGES, PT, vS[j][b2]),
                                                       (1, 4, PTw, vW[b2][:, :, :].rearrange("p a (c n) -> p (a c) n", n=2 * P))):
                            out = ob[h, kind * 2 * P:(kind + 1) * 2 * P]
                            for n in range(tiles):
                                mm(out, pts[:, n, h], vals[:, n, :], start=(n == 0), stop=False)
                            ins = mm(out, PTn[:, kind, h], vN[b2][:, kind, :], start=False, stop=True)
                    ins.then_inc(s["o_done"], 1)


KW = A_WIDTH // P


def merge(nc, A):
    with ExitStack() as ctx:
        sb = lambda name, shape: ctx.enter_context(nc.sbuf_tensor(name, shape, F32))
        sem = nc.alloc_semaphore
        oaT, obT, gT, sg = (sb("m_" + n, [P, KW, NT]) for n in ("oaT", "obT", "gT", "sg"))
        ob_tok, oa_s, ob_s = sb("m_ob_tok", [P, 4, 1024]), sb("m_oa_s", [NS, 1024]), sb("m_ob_s", [NS, 1024])
        ident = sb("m_ident", [P, P])
        w = [[sb(f"m_w{j}{k}", [P, KW, GRP]) for k in range(2)] for j in range(2)]
        gates = [sb(f"m_gates{j}", [P, 2, NT]) for j in range(2)]
        prod = [[sb(f"m_prod{j}{k}", [P, NT]) for k in range(2)] for j in range(2)]
        out = [sb(f"m_out{j}", [P, NT]) for j in range(2)]
        ps = [[ctx.enter_context(nc.psum_tensor(f"m_ps{j}{k}", [P, 2, 512], F32)) for k in range(2)] for j in range(2)]
        first, tps, taken_out = sem("m_first"), sem("m_tps"), sem("m_taken")
        sig, silu, w_in, g_in = sem("m_sig"), sem("m_silu"), [sem(f"m_w_in{j}") for j in range(2)], [sem(f"m_g_in{j}") for j in range(2)]
        mm_done, prods, summed, sent = sem("m_mm"), sem("m_prods"), sem("m_summed"), [sem(f"m_sent{j}") for j in range(2)]
        freed, settled = sem("m_freed"), sem("m_settled")
        block = ctx.enter_context(nc.Block())
        N_FIRST = 1 + 1 + 1 + 1 + 1 + 8

        @block.sync
        def _(sp):
            d = lambda dst, src: sp.dma_start(dst, src).then_inc(first, 16)
            d(ident[:, :], A["ident"])
            d(ob_tok[:, :, :], A["obN"])
            d(gT[:, :, :], A["uT"][COL_GB:COL_GB + 1024, :].rearrange("(c p) n -> p c n", p=P))
            d(oaT[:, :, 0:SEQ], A["oaT"].rearrange("c p n -> p c n"))
            d(oa_s[:, :].rearrange("n (h d) -> n h d", h=16), A["oS"].rearrange("h n d -> n h d"))
            for b in range(DEC_B):
                src = A["obS"][b // 2, (b % 2) * HD:(b % 2 + 1) * HD, :].rearrange("(g t r) d -> t g (r d)", g=G_KV, t=DEC_T)
                d(ob_s[b * DEC_T:(b + 1) * DEC_T, :].rearrange("n (g x) -> n g x", g=G_KV), src)
            with sp.Fori(0, 4) as i:
                for j in range(2):
                    c2 = i * 2 + j
                    sp.wait_ge(prods, c2 * 2 + 1)
                    for k, name in enumerate(("w_pa", "w_pb")):
                        sp.dma_start(w[j][k][:, :, :], A[name][bass.ds(c2, 1)].rearrange("a p k n -> (a p) k n"))\
                            .then_inc(w_in[j], 16)

        @block.scalar
        def _(act):
            f = nc.scalar.activation
            act.sem_inc(freed, 3)
            act.wait_ge(first, 16 * N_FIRST)
            f(sg[:, :, :], gT[:, :, :], ACT.Sigmoid).then_inc(sig, 1)
            with act.Fori(0, 8) as i:
                for j in range(2):
                    c = i * 2 + j
                    src = A["uT"][ROW_M:N_ROWS, :].rearrange("(k c p) n -> c p k n", k=2, p=P)[bass.ds(c, 1)]
                    act.wait_ge(freed, c + 2)
                    act.dma_start(gates[j][:, :, :], src.rearrange("a p k n -> (a p) k n")).then_inc(g_in[j], 16)
                    act.wait_ge(summed, c + 1)
                    act.dma_start(A["mT"][bass.ds(c, 1)].rearrange("a p n -> (a p) n"), out[j][:, :]).then_inc(sent[j], 16)
                    act.wait_ge(sent[j], i * 16 + 16)
                    act.sem_inc(freed, 1)

        @block.vector
        def _(dve):
            v = nc.vector
            dve.wait_ge(sig, 1)
            v.tensor_tensor(gT[:, :, :], gT[:, :, :], sg[:, :, :], ALU.mult).then_inc(silu, 1)
            dve.wait_ge(silu, 1)
            for c in range(KW):
                dve.wait_ge(tps, c + 1)
                p = ps[c % 2]
                v.tensor_tensor(obT[:, c, 0:SEQ], p[0][:, 0, :], gT[:, c, 0:SEQ], ALU.mult)
                v.tensor_tensor(obT[:, c, SEQ:NT], p[1][:, 0, 0:NS], gT[:, c, SEQ:NT], ALU.mult)
                v.tensor_copy(oaT[:, c, SEQ:NT], p[1][:, 0, NS:2 * NS]).then_inc(taken_out, 1)
            dve.sem_inc(prods, 3)
            with dve.Fori(0, 8) as i:
                for j in range(2):
                    c = i * 2 + j
                    dve.wait_ge(mm_done, c + 1)
                    dve.wait_ge(g_in[j], i * 16 + 16)
                    two = lambda t: t.rearrange("p (a n) -> p a n", a=2)
                    for k in range(2):
                        ins = v.tensor_tensor(two(prod[j][k][:, :]), ps[j][k][:, :, 0:HALF], two(gates[j][:, k, :]), ALU.mult)
                    ins.then_inc(prods, 1)
                    dve.wait_ge(prods, c + 4)
                    v.tensor_tensor(out[j][:, :], prod[j][0][:, :], prod[j][1][:, :], ALU.add).then_inc(summed, 1)

        @block.tensor
        def _(pe):
            mm = nc.tensor.matmul
            pe.wait_ge(first, 16 * N_FIRST)
            for c in range(KW):
                if c >= 2:
                    pe.wait_ge(taken_out, c - 1)
                p = ps[c % 2]
                cols = slice(c * P, (c + 1) * P)
                for t in range(4):
                    nc.tensor.transpose(p[0][:, 0, t * P:(t + 1) * P], ob_tok[:, t, cols], ident[:, :])
                mm(p[1][:, 0, 0:NS], ob_s[:, cols], ident[0:NS, 0:NS], start=True, stop=True)
                mm(p[1][:, 0, NS:2 * NS], oa_s[:, cols], ident[0:NS, 0:NS], start=True, stop=True).then_inc(tps, 1)
            pe.wait_ge(taken_out, KW)
            with pe.Fori(0, 4) as i:
                for j in range(2):
                    pe.wait_ge(w_in[j], i * 32 + 32)
                    for jj in range(2):
                        c = i * 4 + j * 2 + jj
                        pe.wait_ge(prods, c + 2)
                        pe.sem_inc(settled, 1)
                        for k, x in enumerate((oaT, obT)):
                            for kk in range(KW):
                                for h in range(2):
                                    ins = mm(ps[jj][k][:, h, 0:HALF], w[j][k][:, kk, jj * P:(jj + 1) * P],
                                             x[:, kk, h * HALF:(h + 1) * HALF], start=(kk == 0), stop=(kk == KW - 1))
                        ins.then_inc(mm_done, 1)


def project_out(nc, A):
    TILES = 5
    with ExitStack() as ctx:
        sb = lambda name, shape: ctx.enter_context(nc.sbuf_tensor(name, shape, F32))
        sem = nc.alloc_semaphore
        mT, wo = sb("o_mT", [P, KD, NT]), sb("o_wo", [P, KD, D_MODEL])
        g_out = sb("o_g", [P, D_MODEL])
        h = [sb(f"o_h{j}", [P, D_MODEL]) for j in range(2)]
        sq = sb("o_sq", [P, 512])
        ss, tot, rs = sb("o_ss", [P, 2, 4]), sb("o_tot", [P, 2]), sb("o_rs", [P, 2])
        eps = sb("o_eps", [P, 1])
        ps = [ctx.enter_context(nc.psum_tensor(f"o_ps{j}", [P, 4, 512], F32)) for j in range(2)]
        m_in, g_in, k_in = sem("o_m_in"), sem("o_g_in"), [sem(f"o_k_in{k}") for k in range(KD)]
        x_in, mm_done, added, squared, summed, rooted, scaled, sent = (
            sem("o_" + n) for n in ("x_in", "mm_done", "added", "squared", "summed", "rooted", "scaled", "sent"))
        chain = sem("o_chain")
        block = ctx.enter_context(nc.Block())
        size = lambda t: P if t < 4 else NS

        @block.sync
        def _(sp):
            for q in range(4):
                sp.dma_start(mT[:, 4 * q:4 * q + 4, :], A["mT"][4 * q:4 * q + 4].rearrange("c p n -> p c n")).then_inc(m_in, 16)
                for k in range(4 * q, 4 * q + 4):
                    sp.dma_start(wo[:, k, :], A["w_o"][k * P:(k + 1) * P, :]).then_inc(k_in[k], 16)
                sp.wait_ge(m_in, 16 * (q + 1))
            sp.dma_start(g_out[:, :], A["g_out"]).then_inc(g_in, 16)
            for t in range(TILES):
                sp.wait_ge(scaled, t + 1)
                dst = A["y_prompt"][t * P:(t + 1) * P, :] if t < 4 else A["y_sample"]
                sp.dma_start(dst, h[t % 2][0:size(t), :]).then_inc(sent, 16)
                sp.wait_ge(sent, 16 * (t + 1))

        @block.scalar
        def _(act):
            for t in range(TILES):
                m = size(t)
                if t >= 2:
                    act.wait_ge(sent, 16 * (t - 1))
                act.dma_start(h[t % 2][0:m, :], A["x"][t * P:t * P + m, :]).then_inc(x_in, 16)
                act.wait_ge(x_in, 16 * (t + 1))
                for n in range(4):
                    act.wait_ge(added, 4 * t + n + 1)
                    if n or t:
                        act.wait_ge(squared, 4 * t + n)
                    nc.scalar.activation(sq[0:m, :], h[t % 2][0:m, n * 512:(n + 1) * 512], ACT.Square,
                                         accum_out=ss[0:m, t % 2, n:n + 1]).then_inc(squared, 1)
                act.wait_ge(summed, t + 1)
                nc.scalar.activation(rs[0:m, t % 2:t % 2 + 1], tot[0:m, t % 2:t % 2 + 1], ACT.Sqrt, bias=eps[0:m, 0:1],
                                     scale=1.0 / D_MODEL).then_inc(rooted, 1)

        @block.vector
        def _(dve):
            v = nc.vector
            link = same_engine(dve, chain)
            link(v.memset(eps[:, :], RMS_EPS))
            for t in range(TILES):
                m = size(t)
                dve.wait_ge(x_in, 16 * (t + 1))
                dve.wait_ge(mm_done, t + 1)
                for n in range(4):
                    c = slice(n * 512, (n + 1) * 512)
                    v.tensor_tensor(h[t % 2][0:m, c], h[t % 2][0:m, c], ps[t % 2][0:m, n, :], ALU.add).then_inc(added, 1)
                dve.wait_ge(squared, 4 * t + 4)
                v.reduce_sum(tot[0:m, t % 2:t % 2 + 1], ss[0:m, t % 2, :], axis=AX.X).then_inc(summed, 1)
                dve.wait_ge(rooted, t + 1)
                link(v.reciprocal(rs[0:m, t % 2:t % 2 + 1], rs[0:m, t % 2:t % 2 + 1]))
                dve.wait_ge(g_in, 16)
                v.scalar_tensor_tensor(out=h[t % 2][0:m, :], in0=h[t % 2][0:m, :], scalar=rs[0:m, t % 2:t % 2 + 1],
                                       in1=g_out[0:m, :], op0=ALU.mult, op1=ALU.mult).then_inc(scaled, 1)

        @block.tensor
        def _(pe):
            for t in range(TILES):
                m = size(t)
                if t >= 2:
                    pe.wait_ge(added, 4 * (t - 1))
                for k in range(KD):
                    if t == 0:
                        if k % 4 == 0:
                            pe.wait_ge(m_in, 16 * (k // 4 + 1))
                        pe.wait_ge(k_in[k], 16)
                    for n in range(4):
                        ins = nc.tensor.matmul(ps[t % 2][0:m, n, :], mT[:, k, t * P:t * P + m],
                                               wo[:, k, n * 512:(n + 1) * 512], start=(k == 0), stop=(k == KD - 1))
                ins.then_inc(mm_done, 1)


def program(nc, A):
    for phase in (project, rwkv, rwkv_samples, compress, attend_prompt, attend_samples, merge, project_out):
        before = nc.snapshot_sems()
        phase(nc, A)
        nc.clear_and_free_semaphores(nc.allocated_since(before))
        nc.all_engine_barrier()


def laid_out(i):
    w = i["w_in"][0].reshape(KD, P, -1).transpose(1, 0, 2)

    def groups(a, b):
        return w[:, :, a:b].reshape(P, KD, (b - a) // GRP, GRP).transpose(2, 0, 1, 3)
    x = np.concatenate([i["x_prompt"].reshape(SEQ, D_MODEL), i["x_sample"].reshape(NS, D_MODEL)])
    per_channel = lambda v: v.reshape(-1, P).T
    out = {
        "x": x,
        "xT": x.T.reshape(KD, P, NT).transpose(1, 0, 2),
        "g_in": per_channel(i["norm_in"][0]),
        "w_main": groups(0, 30 * GRP),
        "w_tail": w[:, :, 30 * GRP:COL_GATE + N_GATE],
        "w_merge": groups(COL_GATE + N_GATE, COL_GATE + N_GATE + 2 * D_MODEL),
        "par": np.concatenate([i["mu_shift"][0][:4 * A_WIDTH].reshape(4, 8, P).transpose(1, 2, 0)]
                              + [i[n][0].reshape(8, P, 1) for n in ("w0", "a0", "k_k", "k_a", "r_k", "gn_w", "gn_b")]
                              + [np.zeros((8, P, 1), np.float32)], axis=2),
        "wup": np.concatenate([i["w_up"][0], i["a_up"][0]]).reshape(P, 8, P).transpose(1, 0, 2),
        "lora_mu": i["mu_shift"][0][4 * A_WIDTH:].reshape(P, 1),
        "shift": i["state_shift"][0][:, :4 * A_WIDTH].reshape(DEC_B, 4, 8, P).transpose(2, 3, 1, 0),
        "lora_shift": i["state_shift"][0][:, 4 * A_WIDTH:].T,
        "stab": np.stack([np.repeat(i[n][0].reshape(16, HD), DEC_B, axis=0)
                          for n in ("k_k", "k_a", "r_k", "gn_w", "gn_b")], axis=1),
        "state": i["state_rwkv"][0].transpose(1, 0, 2, 3).reshape(P, HD, HD),
        "cmp_rows": i["cache_cmp_kv"][0].reshape(N_POOL, 8, STRIDE * KVW),
        "pos_w": np.broadcast_to(np.stack([i["cmp_pos_k"][0].reshape(2, STRIDE, HD),
                                           i["cmp_pos_v"][0].reshape(2, STRIDE, HD)]).reshape(1, 4, STRIDE, HD),
                                 (P, 4, STRIDE, HD)),
        "w_cmp_k": i["w_cmp_k"][0], "w_cmp_v": i["w_cmp_v"][0],
        "page_table": i["page_table"].reshape(1, DEC_B * N_PAGES),
        "sel_k": i["cache_sel_kv"][0][:, :, 0].reshape(N_POOL, PAGE, 2, P).transpose(0, 2, 3, 1),
        "sel_v": i["cache_sel_kv"][0][:, :, 1].reshape(N_POOL, PAGE, 2 * P),
        "win_k": i["cache_win_kv"][0][:, :, 0].reshape(DEC_B, WINDOW, 2, P).transpose(0, 2, 3, 1),
        "win_v": i["cache_win_kv"][0][:, :, 1].reshape(DEC_B, 4, P, 2 * P).transpose(0, 2, 1, 3),
        "w_pa": i["w_pa"][0].reshape(8, P, 8, GRP).transpose(2, 1, 0, 3),
        "w_pb": i["w_pb"][0].reshape(8, P, 8, GRP).transpose(2, 1, 0, 3),
        "w_o": i["w_o"][0],
        "g_out": np.broadcast_to(i["norm_out"], (P, D_MODEL)),
        "win_in": i["cache_win_kv"][0].reshape(DEC_B, WINDOW, KVW),
    }
    return out


def constants():
    f = lambda a: np.asarray(a, np.float32)
    s, t = np.arange(CH)[:, None], np.arange(CH)[None, :]
    same16 = s // 16 == t // 16
    two = lambda m: np.concatenate([m, m])
    head = np.arange(P) // HD
    rmask = np.concatenate([
        np.broadcast_to(np.arange(SEQ) % CH != 0, (P, SEQ)),
        np.concatenate([two(s < t), two(s <= t)], axis=1),
        two((s < t) & same16), two((s < t) & ~same16), two((s > t) & same16), two(s == t), two(s == t)], axis=1)
    slope = np.exp2(-8.0 * np.arange(1, 17, dtype=np.float32) / 16).astype(np.float32).reshape(4, 4)
    q, key = np.arange(P)[:, None], np.arange(SEQ)[None, :]
    dist = q + SEQ - P - key
    bias_p = np.where(dist[None, :, None, :] >= 0, -slope[:, None, :, None] * f(dist)[None, :, None, :], NEG)
    tok = (np.arange(4)[:, None] * P + np.arange(P)[None, :])[:, :, None]
    n = np.arange(32)[None, None, :]
    cdist = tok - (n * STRIDE + 2 * STRIDE - 1)
    cmp_ok = (cdist >= 0) & (n < 31)
    cbias_p = np.where(cmp_ok[None, :, :, None, :], -slope[:, None, None, :, None] * f(cdist)[None, :, :, None, :], NEG)
    cbias_p = cbias_p.transpose(0, 2, 3, 1, 4).reshape(4, P, 16, 32)
    row = np.arange(P)
    rg, rt, rr = row // 16 % 4, row // 4 % 4, row % 4
    pos = PAST + rt[:, None]

    def alibi(key, seen):
        d = pos - key[None, :]
        return np.where(seen(d), -slope[rg, rr][:, None] * f(d), NEG)
    new = PAST + np.arange(DEC_T)
    causal = lambda d: d >= 0
    window = lambda d: (d >= 0) & (d <= WINDOW)
    n128 = np.arange(P)
    bias_s = np.concatenate([alibi(np.arange(PAST), causal), alibi(new, causal),
                             alibi(PAST - WINDOW + np.arange(WINDOW), window), alibi(new, window),
                             np.where(n128 < 127, alibi(n128 * STRIDE + 2 * STRIDE - 1, causal), NEG)], axis=1)
    same_group = (row[:, None] // 4) == (row[None, :] // 4)
    cs, bs = n128[:, None] * STRIDE, np.arange(N_SEL)[None, :] * SEL_BLOCK
    overlap = np.clip(np.minimum(cs + 2 * STRIDE, bs + SEL_BLOCK) - np.maximum(cs, bs), 0, None) / (2 * STRIDE)
    forced = np.isin(np.arange(N_SEL), (0, N_SEL - 2, N_SEL - 1))
    selc = np.broadcast_to(np.stack([~forced, forced * 1e4]), (P, 2, N_SEL))
    jj = np.arange(N_SEL)
    same_head = f(head[:, None] == head[None, :])
    return {
        "ident": np.eye(P, dtype=np.float32),
        "headsum": same_head, "headmean": same_head / HD, "rmask": f(rmask),
        "bias_p": f(bias_p), "cbias_p": f(cbias_p), "cmask": f(np.broadcast_to(cmp_ok.transpose(1, 0, 2), (P, 4, 32))),
        "bias_s": f(bias_s), "gsum": f(same_group), "overlap": f(overlap), "selc": f(selc),
        "lower": f(np.broadcast_to(jj[None, None, :] < jj[None, :, None], (P, N_SEL, N_SEL))),
        "gmask": f(rg[:, None] == np.arange(4)[None, :]),
        "shift1": np.eye(P, k=-1, dtype=np.float32),
    }


_SCRATCH = [("uT", (N_ROWS, NT)), ("u_tail", (33, 62 * P)), ("u_tok", (P, 4, 14 * P)),
            ("smp", (16, NS, 6 * HD)), ("oaT", (8, P, SEQ)),
            ("oS", (16, NS, HD)), ("obN", (P, 4, 1024)), ("obS", (4, P, HD)), ("mT", (16, P, NT)), ("kcT", (DEC_B + 1, 2, P, P)), ("vc", (DEC_B + 1, P, 2, P))]


_OUTS = [
    ("y_prompt", (SEQ, D_MODEL)), ("y_sample", (NS, D_MODEL)),
    ("p_cmp", (SEQ, KVW)), ("p_sel", (SEQ, KVW)), ("p_win", (SEQ, KVW)),
    ("p_rwkv", (16, HD, HD)), ("p_shift", (1, A_COLS)),
    ("s_cmp", (NS, KVW)), ("s_sel", (NS, KVW)), ("s_win", (DEC_B, WINDOW, KVW)),
    ("s_rwkv", (P, HD, HD)), ("s_shift", (DEC_B, A_COLS)),
]
_SHAPES = [
    (1, SEQ, D_MODEL), (DEC_B, DEC_T, D_MODEL),
    (1, 1, SEQ, 2, 4, HD), (1, 1, SEQ, 2, 4, HD), (1, 1, SEQ, 2, 4, HD), (1, 1, 16, HD, HD), (1, 1, A_COLS),
    (1, DEC_B, DEC_T, 2, 4, HD), (1, DEC_B, DEC_T, 2, 4, HD), (1, DEC_B, WINDOW, 2, 4, HD),
    (1, DEC_B, 16, HD, HD), (1, DEC_B, A_COLS),
]


def kernel(**inputs):
    import concourse.bacc as bacc
    from concourse.bass_utils import run_bass_kernel_spmd

    arrays = laid_out({k: np.asarray(v) for k, v in inputs.items()})
    arrays.update(constants())
    nc = bacc.Bacc("TRN2", target_bir_lowering=False, num_devices=1)
    A = {}
    for name, a in arrays.items():
        arrays[name] = a = np.ascontiguousarray(a)
        A[name] = nc.dram_tensor(f"in_{name}", a.shape, mybir.dt.from_np(a.dtype), kind="ExternalInput").ap()
    for name, shape in _OUTS:
        A[name] = nc.dram_tensor(f"out_{name}", shape, F32, kind="ExternalOutput").ap()
    for name, shape in _SCRATCH:
        A[name] = nc.dram_tensor(f"tmp_{name}", shape, F32, kind="Internal").ap()
    program(nc, A)
    r = run_bass_kernel_spmd(nc, [{f"in_{n}": a for n, a in arrays.items()}], core_ids=[0])
    out = {n: np.asarray(r.results[0][f"out_{n}"]) for n, _ in _OUTS}
    out["s_rwkv"] = out["s_rwkv"].reshape(16, DEC_B, HD, HD).transpose(1, 0, 2, 3)
    return tuple(out[n].reshape(s) for (n, _), s in zip(_OUTS, _SHAPES))
```

```python
from contextlib import ExitStack

import numpy as np

import concourse.bass as bass
from concourse import mybir

F32 = mybir.dt.float32
F32R = mybir.dt.float32r
I32 = mybir.dt.int32
ALU = mybir.AluOpType
ACT = mybir.ActivationFunctionType
AX = mybir.AxisListType

P = 128
D_MODEL = 2048
KD = D_MODEL // P
SEQ, DEC_B, DEC_T = 512, 8, 4
NS = DEC_B * DEC_T
NT = SEQ + NS
HALF = NT // 2
PAST, PAGE = 2048, 128
N_PAGES = PAST // PAGE
N_POOL = DEC_B * N_PAGES * 5 // 4
A_WIDTH, A_COLS = 1024, 4224
HD = 64
KVW = 512
COL_Q, COL_GB, COL_C, COL_S, COL_W = 4224, 5248, 6272, 6784, 7296
COL_GATE = 7808
N_GATE = 48
ROW_M = COL_GATE + P
N_ROWS = ROW_M + 2 * D_MODEL
GRP = 256
RMS_EPS, GN_EPS = 1e-6, 64e-5
NEG = -1e30
WINDOW = 512
N_SEL, SEL_BLOCK = 33, 64


def same_engine(eng, sem):
    count = [0]

    def link(ins):
        count[0] += 1
        ins.then_inc(sem, 1)
        eng.wait_ge(sem, count[0])
        return ins

    def restart():
        eng.sem_clear(sem)
        count[0] = 0

    link.restart = restart
    return link


def project(nc, A):
    G_A, G_ALL = 31, 47
    FULL0 = 48
    RING = 4
    with ExitStack() as ctx:
        sb = lambda name, shape: ctx.enter_context(nc.sbuf_tensor(name, shape, F32))
        ps = lambda name, shape: ctx.enter_context(nc.psum_tensor(name, shape, F32))
        sem = nc.alloc_semaphore
        sbr = lambda name, shape: ctx.enter_context(nc.sbuf_tensor(name, shape, F32R))
        late = sb("late", [P, KD * NT])
        xT = late[:, :].rearrange("p (k n) -> p k n", n=NT)
        u_tok = late[:, 0:4 * 14 * P].rearrange("p (t n) -> p t n", t=4)
        xh, xl = sbr("xh", [P, KD, NT]), sbr("xl", [P, KD, NT])
        Wh, Wl = ([sbr(f"W{n}{j}", [P, KD, P]) for j in range(2)] for n in "hl")
        g_in = sb("g_in", [P, KD])
        ones = sb("ones", [P, P])
        ident = sb("ident", [P, P])
        W = [sb(f"W{i}", [P, KD, GRP]) for i in range(2)]
        ub = [sb(f"ub{i}", [P, NT]) for i in range(RING)]
        rs, sq = ub[0], ub[2:4]
        u_tail = sb("u_tail", [33, 62 * P])
        acc = [ps(f"acc{i}", [P, 2, 512]) for i in range(2)]
        tps = [ps(f"tps{i}", [P, 512]) for i in range(2)]
        tpf = [ps(f"tpf{i}", [P, 512]) for i in range(2)]
        x_in, g_ld, consts = sem("x_in"), sem("g_ld"), sem("consts")
        w_in = [sem(f"w_in{i}") for i in range(2)]
        squared, ssum, sq_free = sem("squared"), sem("ssum"), sem("sq_free")
        rs_ready, xT_ready, eps_ready = sem("rs_ready"), sem("xT_ready"), sem("eps_ready")
        xh_ready, xl_ready, w_hi, w_lo = sem("xh_ready"), sem("xl_ready"), sem("w_hi"), sem("w_lo")
        proj_done, evac_done = sem("proj_done"), sem("evac_done")
        stored = [sem(f"stored{i}") for i in range(RING)]
        tail_tp, tail_ev, full_tp, full_ev = sem("tail_tp"), sem("tail_ev"), sem("full_tp"), sem("full_ev")
        rs_chain, act_chain, rows_out = sem("rs_chain"), sem("act_chain"), sem("rows_out")
        eps = sb("eps", [P, 1])
        block = ctx.enter_context(nc.Block())

        def w_src(s):
            if isinstance(s, int) and s == G_A - 1:
                return A["w_tail"]
            if isinstance(s, int) and s >= G_A or not isinstance(s, int) and s_merge[0]:
                return A["w_merge"][bass.ds(s - G_A, 1)].rearrange("a p k n -> (a p) k n")
            return A["w_main"][bass.ds(s, 1)].rearrange("a p k n -> (a p) k n")
        s_merge = [False]

        def plan(eng, group):
            for s in (0, 1):
                group(s, s % 2)
            with eng.Fori(1, 12) as i:
                for j in range(2):
                    group(i * 2 + j, j)
            for s in range(24, 32):
                group(s, s % 2)
            s_merge[0] = True
            with eng.Fori(16, 23) as i:
                for j in range(2):
                    group(i * 2 + j, j)
            s_merge[0] = False
            group(46, 0)

        @block.sync
        def _(sp):
            sp.dma_start(g_in[:, :], A["g_in"]).then_inc(g_ld, 16)
            sp.wait_ge(g_ld, 16)
            sp.dma_start(ident[:, :], A["ident"]).then_inc(g_ld, 16)
            for q in range(4):
                sp.dma_start(xT[:, 4 * q:4 * q + 4, :], A["xT"][:, 4 * q:4 * q + 4, :]).then_inc(x_in, 16)
                sp.wait_ge(x_in, 16 * (q + 1))

            def group(s, slot):
                if not isinstance(s, int) or s >= 2:
                    sp.wait_ge(w_lo, s * 2 - 2)
                src = w_src(s)
                dst = W[slot][:, :, 0:176] if isinstance(s, int) and s == G_A - 1 else W[slot][:, :, :]
                sp.dma_start(dst, src).then_inc(w_in[slot], 16)
            plan(sp, group)

        @block.gpsimd
        def _(pool):
            nc.gpsimd.memset(ones[:, :], 1.0).then_inc(consts, 1)
            pool.wait_ge(tail_ev, 62)
            pool.wait_ge(full_ev, 14)
            pool.dma_start(A["u_tail"], u_tail[:, :]).then_inc(rows_out, 16)
            pool.dma_start(A["p_shift"], u_tail[0:1, 0:A_COLS]).then_inc(rows_out, 16)
            for b in range(DEC_B):
                r = 1 + 4 * b + 3
                pool.dma_start(A["s_shift"][b:b + 1, :], u_tail[r:r + 1, 0:A_COLS]).then_inc(rows_out, 16)
            for name, k in (("s_cmp", 49), ("s_sel", 53)):
                pool.dma_start(A[name], u_tail[1:33, k * P:k * P + KVW]).then_inc(rows_out, 16)
            for b in range(DEC_B):
                pool.dma_start(A["s_win"][b, 508:512, :], u_tail[1 + 4 * b:5 + 4 * b, COL_W:COL_W + KVW])\
                    .then_inc(rows_out, 16)
                pool.dma_start(A["s_win"][b, 0:508, :], A["win_in"][b, 4:512, :]).then_inc(rows_out, 16)
            for name, k in (("p_cmp", 1), ("p_sel", 5), ("p_win", 9)):
                pool.dma_start(A[name].rearrange("(t p) c -> p t c", p=P), u_tok[:, :, k * P:k * P + KVW])\
                    .then_inc(rows_out, 16)
            pool.dma_start(A["u_tok"], u_tok[:, :, :]).then_inc(rows_out, 16)
            pool.wait_ge(rows_out, 16 * (1 + 1 + 8 + 2 + 16 + 3 + 1))

        @block.scalar
        def _(act):
            link = same_engine(act, act_chain)
            for k in range(KD):
                if k % 4 == 0:
                    act.wait_ge(x_in, 16 * (k // 4 + 1))
                if k >= 2:
                    act.wait_ge(ssum, k - 1)
                nc.scalar.activation(sq[k % 2][:, :], xT[:, k, :], ACT.Square).then_inc(squared, 1)
            act.wait_ge(ssum, KD)
            act.wait_ge(eps_ready, 1)
            nc.scalar.activation(rs[:, :].rearrange("p (a n) -> p a n", a=2), acc[0][:, :, 0:HALF], ACT.Sqrt,
                                 bias=eps[:, 0:1], scale=1.0 / D_MODEL).then_inc(rs_ready, 1)
            act.wait_ge(w_in[0], 16)
            nc.scalar.activation(Wh[0][:, :, :], W[0][:, :, 0:P], ACT.Copy).then_inc(w_hi, 1)
            for k in range(KD):
                act.wait_ge(xT_ready, k + 1)
                nc.scalar.activation(xh[:, k, :], xT[:, k, :], ACT.Copy).then_inc(xh_ready, 1)

            def high_part(s, slot, j):
                c = s * 2 + j
                if isinstance(c, int) and c == 2 * G_ALL - 1:
                    return
                if j == 1:
                    act.wait_ge(w_in[1 - slot], 16 * ((s + 1) // 2 + 1) if isinstance(s, int)
                                else (s - slot) * 8 + 16 * (slot + 1))
                if not isinstance(c, int) or c >= 1:
                    act.wait_ge(proj_done, c)
                src = W[slot][:, :, P:2 * P] if j == 0 else W[1 - slot][:, :, 0:P]
                nc.scalar.activation(Wh[1 - j][:, :, :], src, ACT.Copy).then_inc(w_hi, 1)

            def group(s, slot):
                for j in range(2):
                    c = s * 2 + j
                    b = 2 * slot + j
                    high_part(s, slot, j)
                    act.wait_ge(proj_done, c + 1)
                    if not isinstance(s, int) or s >= 2:
                        act.wait_ge(stored[b], (c - b) * 4)
                        if isinstance(s, int):
                            act.wait_ge(tail_tp, min(c - 3, 62))
                            if c - 4 >= FULL0:
                                act.wait_ge(full_tp, min(c - 3 - FULL0, 14))
                        elif not s_merge[0]:
                            act.wait_ge(tail_tp, c - 3)
                    merge = s_merge[0] or isinstance(s, int) and s >= G_A
                    m = N_GATE if isinstance(s, int) and s == G_A - 1 and j == 1 else P
                    out = ub[b][0:m, :].rearrange("p (a n) -> p a n", a=2)
                    nc.scalar.activation(out, acc[j][0:m, :, 0:HALF], ACT.Sigmoid if merge else ACT.Copy)\
                        .then_inc(evac_done, 1)
                    act.wait_ge(evac_done, c + 1)
                    if isinstance(c, int):
                        dst = A["uT"][c * P:c * P + m, :]
                    else:
                        dst = A["uT"][bass.ds(c * P, P), :]
                    act.dma_start(dst, ub[b][0:m, :]).then_inc(stored[b], 16)
            plan(act, group)
            for b in range(RING):
                act.wait_ge(stored[b], 16 * (24 if b < 2 else 23))

        @block.vector
        def _(dve):
            link = same_engine(dve, rs_chain)
            nc.vector.memset(eps[:, :], RMS_EPS).then_inc(eps_ready, 1)
            dve.wait_ge(rs_ready, 1)
            link(nc.vector.reciprocal(rs[:, :], rs[:, :]))
            dve.wait_ge(g_ld, 32)
            dve.wait_ge(w_hi, 1)
            nc.vector.tensor_tensor(Wl[0][:, :, :], W[0][:, :, 0:P], Wh[0][:, :, :].bitcast(F32), ALU.subtract)\
                .then_inc(w_lo, 1)
            for k in range(KD + 1):
                if k < KD:
                    nc.vector.scalar_tensor_tensor(out=xT[:, k, :], in0=xT[:, k, :], scalar=g_in[:, k:k + 1],
                                                   in1=rs[:, :], op0=ALU.mult, op1=ALU.mult).then_inc(xT_ready, 1)
                if k:
                    dve.wait_ge(xh_ready, k)
                    nc.vector.tensor_tensor(xl[:, k - 1, :], xT[:, k - 1, :], xh[:, k - 1, :].bitcast(F32),
                                            ALU.subtract).then_inc(xl_ready, 1)
            dve.wait_ge(xl_ready, KD)

            def low_part(s, slot, j):
                c = s * 2 + j
                if isinstance(c, int) and c == 2 * G_ALL - 1:
                    return
                dve.wait_ge(w_hi, c + 2)
                src = W[slot][:, :, P:2 * P] if j == 0 else W[1 - slot][:, :, 0:P]
                nc.vector.tensor_tensor(Wl[1 - j][:, :, :], src, Wh[1 - j][:, :, :].bitcast(F32), ALU.subtract)\
                    .then_inc(w_lo, 1)

            def copies(c):
                dve.wait_ge(tail_tp, c + 1)
                if isinstance(c, int):
                    m = N_GATE if c == 61 else P
                    dst = u_tail[:, c * P:c * P + m]
                else:
                    m = P
                    dst = u_tail[:, bass.ds(c * P, P)]
                slot = c % 2 if isinstance(c, int) else parity[0]
                nc.vector.tensor_copy(dst, tps[slot][0:33, 0:m]).then_inc(tail_ev, 1)
                if isinstance(c, int) and c >= FULL0:
                    f = c - FULL0
                    dve.wait_ge(full_tp, f + 1)
                    nc.vector.tensor_copy(u_tok[:, :, f * P:f * P + m],
                                          tpf[f % 2][:, :].rearrange("p (t n) -> p t n", t=4)[:, :, 0:m])\
                        .then_inc(full_ev, 1)
            parity = [0]

            def group(s, slot):
                for j in range(2):
                    low_part(s, slot, j)
                    c = s * 2 + j - 1
                    parity[0] = (j + 1) % 2
                    if isinstance(s, int) and (c < 0 or c > 61):
                        continue
                    if s_merge[0]:
                        continue
                    copies(c)
            nc.vector.memset(u_tail[:, 61 * P + N_GATE:62 * P], 0.0)
            nc.vector.memset(u_tok[:, :, 13 * P + N_GATE:14 * P], 0.0).then_inc(eps_ready, 1)
            dve.wait_ge(eps_ready, 2)
            plan(dve, group)

        @block.tensor
        def _(pe):
            pe.wait_ge(consts, 1)
            for k in range(KD):
                pe.wait_ge(squared, k + 1)
                for h in range(2):
                    ins = nc.tensor.matmul(acc[0][:, h, 0:HALF], ones[:, :], sq[k % 2][:, h * HALF:(h + 1) * HALF],
                                           start=(k == 0), stop=(k == KD - 1))
                ins.then_inc(ssum, 1)
            pe.wait_ge(xT_ready, 1)

            def copies(c, b):
                m = N_GATE if isinstance(c, int) and c == 61 else P
                pe.wait_ge(evac_done, c + 1)
                if not isinstance(c, int) or c >= 2:
                    pe.wait_ge(tail_ev, c - 1)
                nc.tensor.matmul(tps[b % 2][0:33, 0:m], ub[b][0:m, SEQ - 1:NT], ident[0:m, 0:m],
                                 start=True, stop=True).then_inc(tail_tp, 1)
                if isinstance(c, int) and c >= FULL0:
                    f = c - FULL0
                    if f >= 2:
                        pe.wait_ge(full_ev, f - 1)
                    for t in range(4):
                        ins = nc.tensor.transpose(tpf[f % 2][:, t * P:t * P + m],
                                                  ub[b][0:m, t * P:(t + 1) * P], ident[0:m, 0:m])
                    ins.then_inc(full_tp, 1)

            pe.wait_ge(g_ld, 32)

            def group(s, slot):
                for j in range(2):
                    c = s * 2 + j
                    pe.wait_ge(w_lo, c + 1)
                    if not isinstance(c, int) or c >= 2:
                        pe.wait_ge(evac_done, c - 1)
                    parts = ((Wh[j], xh), (Wh[j], xl), (Wl[j], xh))
                    for k in range(KD):
                        if isinstance(c, int) and c == 0:
                            pe.wait_ge(xl_ready, k + 1)
                        for n, (w, x) in enumerate(parts):
                            for h in range(2):
                                ins = nc.tensor.matmul(acc[j][:, h, 0:HALF], w[:, k, :],
                                                       x[:, k, h * HALF:(h + 1) * HALF],
                                                       start=(k == 0 and n == 0), stop=(k == KD - 1 and n == 2))
                    ins.then_inc(proj_done, 1)
                    p = c - 1
                    if isinstance(p, int) and (p < 0 or p > 61) or s_merge[0]:
                        continue
                    copies(p, (2 * slot + j - 1) % 4)
            plan(pe, group)


CH = 64
NCH = SEQ // CH
DECAY_SCALE = -float(np.exp(-0.5))
R_, K_, V_, G_ = range(4)
(MU, W0, A0, KK_K, KA, RK, GNW, GNB, OMKA) = (0, 4, 5, 6, 7, 8, 9, 10, 11)
N_PAR = 12

RWKV_JOBS = [
    ("zw", 0, 2, "act"), ("za", 2, 2, "act"), ("tok_a", 0, 1, "act"), ("tok_b", 1, 1, "act"),
    ("knorm", 2, 1, "dve"), ("bonus", 3, 1, "dve"),
    ("bk_tok0", 0, 1, "act"), ("bk_tok1", 1, 1, "act"), ("v_tok0", 2, 1, "act"), ("v_tok1", 3, 1, "act"),
    ("N", 0, 1, "dve"), ("NT", 1, 1, "dve"), ("kk_tok", 2, 1, "act"),
    ("D2", 3, 1, "act"), ("DT2", 0, 1, "dve"),
    ("G0", 1, 1, "dve"), ("G1", 2, 1, "dve"),
    ("D4", 3, 1, "act"), ("DT4", 0, 1, "dve"),
    ("G2", 1, 1, "dve"), ("G3", 2, 1, "dve"),
    ("Q1T", 3, 1, "act"), ("D8", 0, 1, "dve"),
    ("X2", 1, 1, "act"), ("Q2", 2, 1, "act"),
    ("Di", 3, 1, "act"), ("DiT", 0, 1, "dve"),
    ("E", 1, 1, "dve"), ("ET", 2, 1, "dve"), ("E2", 3, 1, "dve"), ("M1T", 0, 1, "dve"),
    ("Tt", 1, 1, "act"), ("W1T", 2, 1, "act"), ("W2a", 3, 1, "act"), ("W2b", 0, 1, "act"),
]
for _n in range(NCH):
    RWKV_JOBS += [(f"U{_n}", 1 + _n % 2, 1, "dve"), (f"O{_n}", 3, 1, "act"), (f"S{_n}", 0, 1, "dve")]
RWKV_JOBS += [("S_out", 1, 1, "act"), ("mean", 2, 1, "dve"), ("var", 3, 1, "act")]


def job_counts():
    n = {"act": 0, "dve": 0}
    out = {}
    for at, (name, _, _, eng) in enumerate(RWKV_JOBS):
        for e in ("act", "dve"):
            if eng in (e, "both"):
                n[e] += 1
                out[name, e] = n[e]
        out[name] = at + 1
    return out, n


def rwkv(nc, A):
    at, per_pair = job_counts()
    NJ = len(RWKV_JOBS)
    last_user = {}
    before = {}
    for name, b0, nb, _ in RWKV_JOBS:
        before[name] = {last_user[b] for b in range(b0, b0 + nb) if b in last_user}
        for b in range(b0, b0 + nb):
            last_user[b] = name
    bank_of = {name: b0 for name, b0, _, _ in RWKV_JOBS}
    engine_of = {name: e for name, _, _, e in RWKV_JOBS}
    with ExitStack() as ctx:
        sb = lambda name, shape: ctx.enter_context(nc.sbuf_tensor(name, shape, F32))
        sem = nc.alloc_semaphore
        bank = ctx.enter_context(nc.psum_tensor("rbank", [P, 4, 512], F32))
        in4, d4, u4 = sb("in4", [P, 4, NT]), sb("d4", [P, 4, NT]), sb("u4", [P, 4, NT])
        par, wup, shift = sb("par", [P, N_PAR]), sb("wup", [P, P]), sb("shift", [P, 4, DEC_B])
        lora_in, lora_d, lora = sb("lora_in", [P, NT]), sb("lora_d", [P, NT]), sb("lora", [P, NT])
        lora_mu, lora_shift = sb("lora_mu", [P, 1]), sb("lora_shift", [P, DEC_B])
        sw, a = sb("sw", [P, NT]), sb("a", [P, NT])
        ident, headsum, headmean = (sb(n, [P, P]) for n in ("r_ident", "headsum", "headmean"))
        mask = sb("mask", [P, 512 + P + 5 * CH])
        m_scan, m_G = mask[:, 0:512], mask[:, 512:512 + P]
        m_D, m_F, m_DT, m_I = (mask[:, 512 + P + k * CH:512 + P + (k + 1) * CH] for k in range(4))
        L, cum, cumL = sb("L", [P, SEQ]), sb("cum", [P, SEQ]), sb("cumL", [P, SEQ])
        E1, Ei, E0 = sb("E1", [P, SEQ]), sb("Ei", [P, SEQ]), sb("E0", [P, SEQ])
        sqk, rn, kk, kb, k2, rk = (sb(n, [P, SEQ]) for n in ("sqk", "rn", "kk", "kb", "k2", "rk"))
        bonus = sb("bonus", [P, SEQ])
        BK, KR, VZ = (sb(n, [P, NCH, 2, CH]) for n in ("BK", "KR", "VZ"))
        tok6 = sb("tok6", [NS, 6, P])
        BKtok, UV = sb("BKtok", [P, NCH, P]), sb("UV", [P, NCH, P])
        G = sb("G", [P, 2, NCH, P])
        mats = {n: sb("m_" + n, [P, NCH, CH]) for n in (
            "D", "ImD", "F", "DT", "kk_tok", "D2", "DT2", "IpDT2", "IpD2", "D4", "DT4", "IpDT4", "IpD8", "Q1T",
            "Q2", "Di", "DiT", "E", "ImE", "ET", "ImET", "IpE2", "M1T", "Tt", "X2", "W1T")}
        W2 = sb("W2", [CH, 2, NCH, CH])
        S, Sd, S_nat = sb("S", [P, P]), sb("Sd", [P, P]), sb("S_nat", [P, P])
        oT, oc, osq, osd = sb("oT", [P, SEQ]), sb("oc", [P, SEQ]), sb("osq", [P, SEQ]), sb("osd", [P, SEQ])
        gate = sb("gate", [P, SEQ])
        epsg = sb("epsg", [P, 1])

        loaded, consts, in_free = sem("r_loaded"), sem("r_consts"), sem("r_in_free")
        pe_jobs, ev_act, ev_dve = sem("pe_jobs"), sem("ev_act"), sem("ev_dve")
        mixed, lora_ready, tanh_done = sem("mixed"), sem("lora_ready"), sem("tanh_done")
        cum_ready, exps_ready, sqk_ready, knorm2 = sem("cum_ready"), sem("exps_ready"), sem("sqk_ready"), sem("knorm2")
        knorm_sqrt, operands, tok_sent, rk_ready = sem("knorm_sqrt"), sem("operands"), sem("tok_sent"), sem("rk_ready")
        centered, sq_ready, std_ready, gate_ready = sem("centered"), sem("sq_ready"), sem("std_ready"), sem("gate_ready")
        o_ready, o_sent, s_ready, s_sent = sem("r_o_ready"), sem("r_o_sent"), sem("r_s_ready"), sem("r_s_sent")
        pair_pe, pair_act, pair_dve, pre = sem("pair_pe"), sem("pair_act"), sem("pair_dve"), sem("r_pre")
        dve_chain, settled = sem("r_dve_chain"), sem("settled")
        state_ready = sem("state_ready")
        block = ctx.enter_context(nc.Block())
        NA, ND = per_pair["act"], per_pair["dve"]

        def taken(eng, i, *names):
            for e, s, n in (("act", ev_act, NA), ("dve", ev_dve, ND)):
                places = [at[name, e] for name in names if engine_of[name] in (e, "both")]
                if places:
                    eng.wait_ge(s, i * n + max(places))

        N_CONST = 6

        @block.sync
        def _(sp):
            for dst, src in ((ident, "ident"), (headsum, "headsum"), (headmean, "headmean"), (mask, "rmask"),
                             (lora_mu, "lora_mu"), (lora_shift, "lora_shift")):
                sp.dma_start(dst[:, :], A[src]).then_inc(consts, 16)
            sp.dma_start(lora_in[:, :], A["uT"][4 * A_WIDTH:4 * A_WIDTH + P, :]).then_inc(consts, 16)
            with sp.Fori(0, 8) as i:
                sp.wait_ge(in_free, i + 1)
                u = A["uT"][0:4 * A_WIDTH, :].rearrange("(f c p) n -> c p f n", f=4, p=P)
                sp.dma_start(in4[:, :, :], u[bass.ds(i, 1)].rearrange("a p f n -> (a p) f n")).then_inc(loaded, 16)
                for dst, src in ((par, "par"), (wup, "wup")):
                    sp.dma_start(dst[:, :], A[src][bass.ds(i, 1)].rearrange("a p n -> (a p) n")).then_inc(loaded, 16)
                sp.dma_start(shift[:, :, :], A["shift"][bass.ds(i, 1)].rearrange("a p f n -> (a p) f n"))\
                    .then_inc(loaded, 16)
                sp.wait_ge(ev_act, i * NA + at["tok_b", "act"])
                for h in range(2):
                    dst = A["smp"][bass.ds(i * 2 + h, 1)].rearrange("a t (f d) -> (a t) f d", f=6)
                    sp.dma_start(dst, tok6[:, :, h * HD:(h + 1) * HD]).then_inc(tok_sent, 16)
                sp.wait_ge(ev_act, i * NA + at["S_out", "act"])
                for h in range(2):
                    dst = A["p_rwkv"][bass.ds(i * 2 + h, 1)].rearrange("a t d -> (a t) d")
                    sp.dma_start(dst, S_nat[h * HD:(h + 1) * HD, h * HD:(h + 1) * HD]).then_inc(s_sent, 16)
                sp.wait_ge(o_ready, i + 1)
                sp.dma_start(A["oaT"][bass.ds(i, 1)].rearrange("a p n -> (a p) n"), oT[:, :]).then_inc(o_sent, 16)
            sp.wait_ge(tok_sent, 16 * 16)
            sp.wait_ge(s_sent, 16 * 16)
            sp.wait_ge(o_sent, 8 * 16)

        @block.vector
        def _(dve):
            link = same_engine(dve, dve_chain)
            v = nc.vector
            tt, ts, stt = v.tensor_tensor, v.tensor_scalar, v.scalar_tensor_tensor
            v.memset(epsg[:, :], GN_EPS)
            v.memset(VZ[:, :, 0, :], 0.0)
            v.memset(L[:, :], 0.0).then_inc(in_free, 1)
            dve.wait_ge(consts, 16 * (N_CONST + 1))

            def shift_mix(x, d, u, mu, prev, f):
                four = lambda t: t[:, :, SEQ:NT].rearrange("p f (b t) -> p f b t", t=DEC_T)
                tt(d[:, :, 1:SEQ], x[:, :, 0:SEQ - 1], x[:, :, 1:SEQ], ALU.subtract)
                ts(d[:, :, 0:1], x[:, :, 0:1], -1.0, None, ALU.mult)
                for k in range(f):
                    xf, df = four(x)[:, k], four(d)[:, k]
                    tt(df[:, :, 1:DEC_T], xf[:, :, 0:DEC_T - 1], xf[:, :, 1:DEC_T], ALU.subtract)
                    last = tt(df[:, :, 0:1], prev[:, k, :, None], xf[:, :, 0:1], ALU.subtract)
                link(last)
                for k in range(f):
                    last = stt(out=u[:, k, :], in0=d[:, k, :], scalar=mu[:, k:k + 1], in1=x[:, k, :],
                               op0=ALU.mult, op1=ALU.add)
                return last
            shift_mix(lora_in[:, None, :], lora_d[:, None, :], lora[:, None, :], lora_mu,
                      lora_shift[:, None, :], 1).then_inc(lora_ready, 1)
            link.restart()
            with dve.Fori(0, 8) as i:
                def got(name):
                    dve.wait_ge(pe_jobs, i * NJ + at[name])
                dve.wait_ge(pair_pe, i + 1)
                dve.wait_ge(pair_act, i + 1)
                dve.wait_ge(loaded, (i + 1) * 64)
                shift_mix(in4, d4, u4, par, shift, 4).then_inc(mixed, 1)
                dve.wait_ge(mixed, i + 1)
                link(ts(par[:, OMKA:OMKA + 1], par[:, KA:KA + 1], -1.0, 1.0, ALU.mult, ALU.add))
                dve.wait_ge(ev_act, i * NA + at["za", "act"])
                link(ts(L[:, :], sw[:, 0:SEQ], DECAY_SCALE, None, ALU.mult))
                link(v.tensor_tensor_scan(out=cum[:, :], data0=m_scan, data1=L[:, :], initial=0.0,
                                          op0=ALU.mult, op1=ALU.add))
                tt(cumL[:, :], cum[:, :], L[:, :], ALU.subtract).then_inc(cum_ready, 1)
                link(ts(kb[:, :], a[:, 0:SEQ], par[:, KA:KA + 1], par[:, OMKA:OMKA + 1], ALU.mult, ALU.add))
                link(tt(k2[:, :], u4[:, K_, 0:SEQ], kb[:, :], ALU.mult))
                stt(out=rk[:, :], in0=u4[:, R_, 0:SEQ], scalar=par[:, RK:RK + 1], in1=k2[:, :],
                    op0=ALU.mult, op1=ALU.mult).then_inc(rk_ready, 1)
                got("knorm")
                ts(rn[:, :], bank[:, bank_of["knorm"], :], 1e-24, None, ALU.max).then_inc(ev_dve, 1)
                dve.wait_ge(knorm_sqrt, i + 1)
                link(v.reciprocal(rn[:, :], rn[:, :]))
                link(stt(out=kk[:, :], in0=u4[:, K_, 0:SEQ], scalar=par[:, KK_K:KK_K + 1], in1=rn[:, :],
                         op0=ALU.mult, op1=ALU.mult))
                link(tt(kb[:, :], kk[:, :], a[:, 0:SEQ], ALU.mult))
                dve.wait_ge(exps_ready, (i + 1) * 3)
                by = lambda t: t[:, :].rearrange("p (n c) -> p n c", c=CH)
                tt(BK[:, :, 0, :], by(kb), by(Ei), ALU.mult)
                tt(BK[:, :, 1, :], by(k2), by(Ei), ALU.mult)
                tt(KR[:, :, 0, :], by(kk), by(E0), ALU.mult)
                tt(KR[:, :, 1, :], u4[:, R_, 0:SEQ].rearrange("p (n c) -> p n c", c=CH), by(E1), ALU.mult)
                v.tensor_copy(VZ[:, :, 1, :], u4[:, V_, 0:SEQ].rearrange("p (n c) -> p n c", c=CH))
                v.memset(S[:, :], 0.0).then_inc(operands, 1)
                got("bonus")
                tt(bonus[:, :], bank[:, bank_of["bonus"], :], u4[:, V_, 0:SEQ], ALU.mult).then_inc(ev_dve, 1)
                m = mats
                pb = lambda name: bank[:, bank_of[name], :].rearrange("p (n c) -> p n c", c=CH)
                over = lambda t: t[:, None, :].to_broadcast([P, NCH, CH])
                got("N")
                tt(m["D"][:, :, :], pb("N"), over(m_D), ALU.mult)
                link(tt(m["F"][:, :, :], pb("N"), over(m_F), ALU.mult))
                tt(m["ImD"][:, :, :], over(m_I), m["D"][:, :, :], ALU.subtract).then_inc(ev_dve, 1)
                got("NT")
                tt(m["DT"][:, :, :], pb("NT"), over(m_DT), ALU.mult).then_inc(ev_dve, 1)
                got("DT2")
                tt(m["IpDT2"][:, :, :], pb("DT2"), over(m_I), ALU.add)
                v.tensor_copy(m["DT2"][:, :, :], pb("DT2")).then_inc(ev_dve, 1)

                def g_quarter(q):
                    got(f"G{q}")
                    src = bank[:, bank_of[f"G{q}"], :].rearrange("p (n c) -> p n c", c=P)
                    tt(G[:, q // 2, 4 * (q % 2):4 * (q % 2) + 4, :], src,
                       m_G[:, None, :].to_broadcast([P, 4, P]), ALU.mult).then_inc(ev_dve, 1)
                g_quarter(0)
                g_quarter(1)
                got("DT4")
                tt(m["IpDT4"][:, :, :], pb("DT4"), over(m_I), ALU.add)
                v.tensor_copy(m["DT4"][:, :, :], pb("DT4")).then_inc(ev_dve, 1)
                g_quarter(2)
                g_quarter(3)
                got("D8")
                tt(m["IpD8"][:, :, :], pb("D8"), over(m_I), ALU.add).then_inc(ev_dve, 1)
                got("DiT")
                v.tensor_copy(m["DiT"][:, :, :], pb("DiT")).then_inc(ev_dve, 1)
                got("E")
                v.tensor_copy(m["E"][:, :, :], pb("E"))
                tt(m["ImE"][:, :, :], over(m_I), pb("E"), ALU.subtract).then_inc(ev_dve, 1)
                got("ET")
                v.tensor_copy(m["ET"][:, :, :], pb("ET"))
                tt(m["ImET"][:, :, :], over(m_I), pb("ET"), ALU.subtract).then_inc(ev_dve, 1)
                got("E2")
                tt(m["IpE2"][:, :, :], pb("E2"), over(m_I), ALU.add).then_inc(ev_dve, 1)
                got("M1T")
                v.tensor_copy(m["M1T"][:, :, :], pb("M1T")).then_inc(ev_dve, 1)
                for n in range(NCH):
                    last_p = E1[:, (n + 1) * CH - 1:(n + 1) * CH]
                    link(ts(Sd[:, :], S[:, :], last_p, None, ALU.mult))
                    dve.wait_ge(ev_act, i * NA + at["W2b", "act"])
                    got(f"U{n}")
                    stt(out=UV[0:CH, n, :].rearrange("p (h i) -> p h i", h=2),
                        in0=bank[0:CH, bank_of[f"U{n}"], 0:P].rearrange("p (h i) -> p h i", h=2), scalar=-1.0,
                        in1=W2[:, :, n, :], op0=ALU.mult, op1=ALU.subtract).then_inc(ev_dve, 1)
                    got(f"S{n}")
                    for h, hp in enumerate((slice(0, CH), slice(CH, P))):
                        last = stt(out=S[hp, h * CH:(h + 1) * CH], in0=bank[hp, bank_of[f"S{n}"], 0:CH],
                                   scalar=last_p[hp], in1=Sd[hp, h * CH:(h + 1) * CH], op0=ALU.mult, op1=ALU.add)
                    last.then_inc(ev_dve, 1)
                    dve.wait_ge(ev_dve, i * ND + at[f"S{n}", "dve"])
                got("mean")
                tt(oc[:, :], oT[:, :], bank[:, bank_of["mean"], :], ALU.subtract).then_inc(ev_dve, 1)
                dve.wait_ge(std_ready, i + 1)
                link(v.reciprocal(osd[:, :], osd[:, :]))
                link(stt(out=oc[:, :], in0=oc[:, :], scalar=par[:, GNW:GNW + 1], in1=osd[:, :],
                         op0=ALU.mult, op1=ALU.mult))
                link(stt(out=oc[:, :], in0=oc[:, :], scalar=par[:, GNB:GNB + 1], in1=bonus[:, :],
                         op0=ALU.add, op1=ALU.add))
                dve.wait_ge(gate_ready, i + 1)
                link(tt(gate[:, :], gate[:, :], u4[:, G_, 0:SEQ], ALU.mult))
                tt(oT[:, :], oc[:, :], gate[:, :], ALU.mult).then_inc(o_ready, 1)
                dve.wait_ge(o_ready, i + 1)
                v.memset(Sd[:, 0:1], 0.0).then_inc(in_free, 1)
                link.restart()

        @block.scalar
        def _(act):
            act.wait_ge(lora_ready, 1)
            nc.scalar.activation(lora[0:HD, :], lora[0:HD, :], ACT.Tanh).then_inc(tanh_done, 1)
            f = nc.scalar.activation
            act.wait_ge(tanh_done, 1)
            act.sem_inc(pair_act, 1)
            with act.Fori(0, 8) as i:
                def got(name):
                    act.wait_ge(pe_jobs, i * NJ + at[name])

                def out(name, dst, src=None, func=ACT.Copy, **kw):
                    got(name)
                    f(dst, bank[:, bank_of[name], :] if src is None else src, func, **kw).then_inc(ev_act, 1)
                act.wait_ge(pair_pe, i + 1)
                act.wait_ge(mixed, i + 1)
                f(sqk[:, :], u4[:, K_, 0:SEQ], ACT.Square, scale=par[:, KK_K:KK_K + 1]).then_inc(sqk_ready, 1)
                two = lambda t: t[:, :].rearrange("p (a n) -> p a n", a=2)
                out("zw", two(sw), bank[:, 0:2, 0:HALF], ACT.Sigmoid, bias=par[:, W0:W0 + 1])
                out("za", two(a), bank[:, 2:4, 0:HALF], ACT.Sigmoid, bias=par[:, A0:A0 + 1])
                f(gate[:, :], u4[:, G_, 0:SEQ], ACT.Sigmoid).then_inc(gate_ready, 1)
                out("tok_a", tok6[:, 0:4, :], bank[0:NS, bank_of["tok_a"], :].rearrange("p (f d) -> p f d", f=4))
                out("tok_b", tok6[:, 4:6, :], bank[0:NS, bank_of["tok_b"], 0:2 * P].rearrange("p (f d) -> p f d", f=2))
                act.wait_ge(cum_ready, i + 1)
                f(E1[:, :], cum[:, :], ACT.Exp).then_inc(exps_ready, 1)
                f(Ei[:, :], cum[:, :], ACT.Exp, scale=-1.0).then_inc(exps_ready, 1)
                f(E0[:, :], cumL[:, :], ACT.Exp).then_inc(exps_ready, 1)
                act.wait_ge(ev_dve, i * ND + at["knorm", "dve"])
                f(rn[:, :], rn[:, :], ACT.Sqrt).then_inc(knorm_sqrt, 1)
                m = mats
                pb = lambda name: bank[:, bank_of[name], :].rearrange("p (n c) -> p n c", c=CH)
                pw = lambda name: bank[:, bank_of[name], :].rearrange("p (n c) -> p n c", c=P)
                out("bk_tok0", BKtok[:, 0:4, :], pw("bk_tok0"))
                out("bk_tok1", BKtok[:, 4:8, :], pw("bk_tok1"))
                out("v_tok0", UV[CH:P, 0:4, :], pw("v_tok0")[CH:P])
                out("v_tok1", UV[CH:P, 4:8, :], pw("v_tok1")[CH:P])
                out("kk_tok", m["kk_tok"][:, :, :], pb("kk_tok"))
                for name in ("D2", "D4", "Q1T", "X2", "Q2", "Di", "Tt", "W1T"):
                    out(name, m[name][:, :, :], pb(name))
                for h, name in enumerate(("W2a", "W2b")):
                    out(name, W2[:, h, :, :], pb(name)[0:CH])
                for n in range(NCH):
                    out(f"O{n}", oT[:, n * CH:(n + 1) * CH], bank[:, bank_of[f"O{n}"], 0:CH])
                out("S_out", S_nat[:, :], bank[:, bank_of["S_out"], 0:P])
                act.wait_ge(ev_dve, i * ND + at["mean", "dve"])
                f(osq[:, :], oc[:, :], ACT.Square).then_inc(sq_ready, 1)
                got("var")
                f(osd[:, :], bank[:, bank_of["var"], :], ACT.Sqrt, bias=epsg[:, 0:1]).then_inc(std_ready, 1)
                act.wait_ge(std_ready, i + 1)
                act.sem_inc(ev_act, 1)
                act.wait_ge(o_sent, (i + 1) * 16)
                act.wait_ge(tok_sent, (i + 1) * 32)
                act.wait_ge(s_sent, (i + 1) * 32)
                act.sem_inc(pair_act, 1)

        @block.tensor
        def _(pe):
            mm = nc.tensor.matmul
            pe.wait_ge(consts, 16 * (N_CONST + 1))
            pe.wait_ge(tanh_done, 1)
            pe.sem_inc(pair_pe, 1)

            def settle():
                pe.sem_inc(settled, 1)
            with pe.Fori(0, 8) as i:
                def job(name, *needs):
                    taken(pe, i, *before[name], *needs)
                    settle()

                def done(ins):
                    ins.then_inc(pe_jobs, 1)
                pe.wait_ge(mixed, i + 1)
                for name, rows in (("zw", slice(0, HD)), ("za", slice(HD, P))):
                    job(name)
                    for h in range(2):
                        ins = mm(bank[:, bank_of[name] + h, 0:HALF], wup[rows, :],
                                 lora[rows, h * HALF:(h + 1) * HALF], start=True, stop=True)
                    done(ins)
                job("tok_a", "za")
                for f in range(4):
                    ins = mm(bank[0:NS, 0, f * P:(f + 1) * P], u4[:, f, SEQ:NT], ident[:, :], start=True, stop=True)
                done(ins)
                job("tok_b")
                for f, t in enumerate((sw, a)):
                    ins = mm(bank[0:NS, 1, f * P:(f + 1) * P], t[:, SEQ:NT], ident[:, :], start=True, stop=True)
                done(ins)
                pe.wait_ge(sqk_ready, i + 1)
                job("knorm")
                done(mm(bank[:, 2, :], headsum[:, :], sqk[:, :], start=True, stop=True))
                pe.wait_ge(rk_ready, i + 1)
                job("bonus")
                done(mm(bank[:, 3, :], headsum[:, :], rk[:, :], start=True, stop=True))
                pe.wait_ge(operands, i + 1)
                for name, src, n0 in (("bk_tok0", BK, 0), ("bk_tok1", BK, 4), ("v_tok0", VZ, 0), ("v_tok1", VZ, 4)):
                    job(name)
                    for n in range(4):
                        ins = mm(bank[:, bank_of[name], n * P:(n + 1) * P],
                                 src[:, n0 + n, :, :].rearrange("p a c -> p (a c)"), ident[:, :],
                                 start=True, stop=True)
                    done(ins)
                H = (slice(0, CH), slice(CH, P))

                def both(name, lhsT, rhs, *needs):
                    job(name, *needs)
                    for n in range(NCH):
                        for hp in H:
                            ins = mm(bank[hp, bank_of[name], n * CH:(n + 1) * CH], lhsT(hp, n), rhs(hp, n),
                                     start=True, stop=True)
                    done(ins)
                B = lambda hp, n: BK[hp, n, 0, :]
                KK = lambda hp, n: KR[hp, n, 0, :]
                M = lambda name: (lambda hp, n: mats[name][hp, n, :])
                both("N", B, KK)
                both("NT", KK, B)
                both("kk_tok", KK, lambda hp, n: ident[hp, hp])
                both("D2", M("DT"), M("D"), "N", "NT")
                both("DT2", M("D"), M("DT"))

                def g_quarter(q):
                    job(f"G{q}")
                    hp = H[q // 2]
                    for n in range(4):
                        nn = 4 * (q % 2) + n
                        ins = mm(bank[:, bank_of[f"G{q}"], n * P:(n + 1) * P],
                                 BK[hp, nn, :, :].rearrange("p a c -> p (a c)"),
                                 KR[hp, nn, :, :].rearrange("p a c -> p (a c)"), start=True, stop=True)
                    done(ins)
                g_quarter(0)
                g_quarter(1)
                both("D4", M("DT2"), M("D2"), "D2", "DT2")
                both("DT4", M("D2"), M("DT2"))
                g_quarter(2)
                g_quarter(3)
                both("Q1T", M("ImD"), M("IpDT2"))
                both("D8", M("DT4"), M("D4"), "D4", "DT4")
                job("X2", "G0", "G1", "G2", "G3", "v_tok0", "v_tok1")
                for n in range(NCH):
                    for h, hp in enumerate(H):
                        ins = mm(bank[hp, bank_of["X2"], n * CH:(n + 1) * CH], G[CH:P, h, n, 0:CH],
                                 UV[CH:P, n, h * CH:(h + 1) * CH], start=True, stop=True)
                done(ins)
                both("Q2", M("IpDT4"), M("IpD8"), "D8")
                both("Di", M("Q1T"), M("Q2"), "Q1T", "Q2")
                both("DiT", M("Q2"), M("Q1T"))
                both("E", M("DiT"), M("F"), "DiT")
                both("ET", M("F"), M("DiT"))
                both("E2", M("ET"), M("E"), "E", "ET")
                both("M1T", M("IpE2"), M("ImET"), "E2")
                both("Tt", M("M1T"), M("Di"), "M1T", "Di")
                both("W1T", M("kk_tok"), M("Tt"), "Tt", "kk_tok", "X2")
                for h, name in enumerate(("W2a", "W2b")):
                    job(name)
                    for n in range(NCH):
                        ins = mm(bank[0:CH, bank_of[name], n * CH:(n + 1) * CH], mats["Tt"][H[h], n, :],
                                 mats["X2"][H[h], n, :], start=True, stop=True)
                    done(ins)
                for n in range(NCH):
                    job(f"U{n}", "W1T", *([f"S{n - 1}"] if n else []))
                    done(mm(bank[0:CH, bank_of[f"U{n}"], 0:P], mats["W1T"][:, n, :], S[:, :], start=True, stop=True))
                    job(f"O{n}", f"U{n}", "bk_tok1")
                    mm(bank[:, bank_of[f"O{n}"], 0:CH], S[:, :], KR[:, n, 1, :], start=True, stop=False)
                    for h, hp in enumerate(H):
                        ins = mm(bank[hp, bank_of[f"O{n}"], 0:CH], UV[:, n, h * CH:(h + 1) * CH],
                                 G[:, h, n, CH:P], start=False, stop=True)
                    done(ins)
                    job(f"S{n}")
                    for h, hp in enumerate(H):
                        ins = mm(bank[hp, bank_of[f"S{n}"], 0:CH], BKtok[:, n, h * CH:(h + 1) * CH],
                                 UV[:, n, h * CH:(h + 1) * CH], start=True, stop=True)
                    done(ins)
                job("S_out", f"S{NCH - 1}", f"O{NCH - 1}")
                done(mm(bank[:, bank_of["S_out"], 0:P], S[:, :], ident[:, :], start=True, stop=True))
                job("mean")
                done(mm(bank[:, bank_of["mean"], :], headmean[:, :], oT[:, :], start=True, stop=True))
                pe.wait_ge(sq_ready, i + 1)
                job("var")
                done(mm(bank[:, bank_of["var"], :], headmean[:, :], osq[:, :], start=True, stop=True))
                taken(pe, i, "S_out", "mean", "var", f"S{NCH - 1}")
                pe.sem_inc(pair_pe, 1)


def rwkv_samples(nc, A):
    with ExitStack() as ctx:
        sb = lambda name, shape: ctx.enter_context(nc.sbuf_tensor(name, shape, F32))
        sem = nc.alloc_semaphore
        X = sb("sx", [P, DEC_T, 6, HD])
        tab = sb("stab", [P, 5, HD])
        S, Sw, outer, prod = (sb(n, [P, HD, HD]) for n in ("sS", "sSw", "s_outer", "s_prod"))
        w, kraw, sq, kk, b, k2, rk, o, oc, gate = (
            sb("s_" + n, [P, DEC_T, HD]) for n in ("w", "kraw", "sq", "kk", "b", "k2", "rk", "o", "oc", "gate"))
        ss, mean, var, bonus = (sb("s_" + n, [P, DEC_T]) for n in ("ss", "mean", "var", "bonus"))
        sa, eps = sb("s_sa", [P, HD]), sb("s_eps", [P, 1])
        loaded, chain, act_done, ready = sem("s_loaded"), sem("s_chain"), sem("s_act_done"), sem("s_ready_in")
        norm_in, var_in, state_new, pool_chain, decayed = (
            sem(n) for n in ("s_norm_in", "s_var_in", "s_state_new", "s_pool_chain", "s_decayed"))
        o_done, sent = sem("s_o_done"), sem("s_sent")
        block = ctx.enter_context(nc.Block())
        last_dim = lambda t, i: t[:, i, None, :].to_broadcast([P, HD, HD])
        over_j = lambda t: t[:, :, None].to_broadcast([P, HD, HD])
        over_d = lambda t: t[:, :, None].to_broadcast([P, DEC_T, HD])
        over_t = lambda k: tab[:, None, k, :].to_broadcast([P, DEC_T, HD])
        r, k, v, g, sw, a = (X[:, :, f, :] for f in range(6))

        @block.sync
        def _(sp):
            sp.dma_start(X[:, :, :, :], A["smp"].rearrange("h (b t) f -> (h b) (t f)", t=DEC_T)
                         .rearrange("p (t f d) -> p t f d", t=DEC_T, f=6)).then_inc(loaded, 16)
            sp.dma_start(tab[:, :, :], A["stab"]).then_inc(loaded, 16)
            sp.dma_start(S[:, :, :], A["state"]).then_inc(loaded, 16)
            sp.wait_ge(o_done, 1)
            sp.dma_start(A["s_rwkv"], S[:, :, :]).then_inc(sent, 16)
            sp.dma_start(A["oS"].rearrange("h n d -> (h n d)").rearrange("(p n) -> p n", p=P),
                         o[:, :, :].rearrange("p t d -> p (t d)")).then_inc(sent, 16)
            sp.wait_ge(sent, 32)

        @block.scalar
        def _(act):
            f = nc.scalar.activation
            act.wait_ge(loaded, 48)
            f(w[:, :, :], sw, ACT.Exp, scale=DECAY_SCALE).then_inc(act_done, 1)
            f(gate[:, :, :], g, ACT.Sigmoid).then_inc(act_done, 1)
            act.wait_ge(norm_in, 1)
            f(ss[:, :], ss[:, :], ACT.Sqrt).then_inc(act_done, 1)
            act.wait_ge(var_in, 1)
            f(var[:, :], var[:, :], ACT.Sqrt, bias=eps[:, 0:1], scale=1.0 / HD).then_inc(act_done, 1)

        @block.gpsimd
        def _(pool):
            tt = nc.gpsimd.tensor_tensor
            link = same_engine(pool, pool_chain)
            pool.wait_ge(ready, 1)
            pool.wait_ge(act_done, 2)
            for t in range(DEC_T):
                if t:
                    pool.wait_ge(decayed, t)
                link(tt(outer[:, :, :], over_j(v[:, t, :]), last_dim(k2, t), ALU.mult))
                if t:
                    pool.wait_ge(state_new, t)
                link(tt(Sw[:, :, :], S[:, :, :], last_dim(w, t), ALU.mult))
                tt(Sw[:, :, :], Sw[:, :, :], outer[:, :, :], ALU.add).then_inc(decayed, 1)

        @block.vector
        def _(dve):
            link = same_engine(dve, chain)
            vv = nc.vector
            tt, ts, stt = vv.tensor_tensor, vv.tensor_scalar, vv.scalar_tensor_tensor
            red = lambda out, x: vv.reduce_sum(out, x, axis=AX.X)
            vv.memset(eps[:, :], GN_EPS)
            dve.wait_ge(loaded, 48)
            link(tt(kraw[:, :, :], k, over_t(0), ALU.mult))
            link(tt(sq[:, :, :], kraw[:, :, :], kraw[:, :, :], ALU.mult))
            link(red(ss[:, :], sq[:, :, :]))
            ts(ss[:, :], ss[:, :], 1e-24, None, ALU.max).then_inc(norm_in, 1)
            link(ts(k2[:, :, :], a, 1.0, None, ALU.subtract))
            link(tt(k2[:, :, :], k2[:, :, :], over_t(1), ALU.mult))
            link(stt(out=k2[:, :, :], in0=k2[:, :, :], scalar=1.0, in1=k, op0=ALU.add, op1=ALU.mult))
            dve.wait_ge(act_done, 3)
            link(vv.reciprocal(ss[:, :], ss[:, :]))
            link(tt(kk[:, :, :], kraw[:, :, :], over_d(ss), ALU.mult))
            tt(b[:, :, :], kk[:, :, :], a, ALU.mult).then_inc(ready, 1)
            dve.wait_ge(ready, 1)
            for t in range(DEC_T):
                link(tt(prod[:, :, :], S[:, :, :], last_dim(kk, t), ALU.mult))
                link(red(sa[:, :], prod[:, :, :]))
                link(tt(prod[:, :, :], over_j(sa), last_dim(b, t), ALU.mult))
                dve.wait_ge(decayed, t + 1)
                tt(S[:, :, :], Sw[:, :, :], prod[:, :, :], ALU.subtract).then_inc(state_new, 1)
                dve.wait_ge(state_new, t + 1)
                link(tt(prod[:, :, :], S[:, :, :], last_dim(X[:, t], 0), ALU.mult))
                link(red(o[:, t, :], prod[:, :, :]))
            link(red(mean[:, :], o[:, :, :]))
            link(ts(mean[:, :], mean[:, :], 1.0 / HD, None, ALU.mult))
            link(tt(oc[:, :, :], o[:, :, :], over_d(mean), ALU.subtract))
            link(tt(sq[:, :, :], oc[:, :, :], oc[:, :, :], ALU.mult))
            red(var[:, :], sq[:, :, :]).then_inc(var_in, 1)
            link(tt(rk[:, :, :], r, k2[:, :, :], ALU.mult))
            link(tt(rk[:, :, :], rk[:, :, :], over_t(2), ALU.mult))
            link(red(bonus[:, :], rk[:, :, :]))
            link(tt(rk[:, :, :], v, over_d(bonus), ALU.mult))
            dve.wait_ge(act_done, 4)
            link(vv.reciprocal(var[:, :], var[:, :]))
            link(tt(oc[:, :, :], oc[:, :, :], over_d(var), ALU.mult))
            link(tt(oc[:, :, :], oc[:, :, :], over_t(3), ALU.mult))
            link(tt(oc[:, :, :], oc[:, :, :], over_t(4), ALU.add))
            link(tt(oc[:, :, :], oc[:, :, :], rk[:, :, :], ALU.add))
            link(tt(gate[:, :, :], gate[:, :, :], g, ALU.mult))
            tt(o[:, :, :], oc[:, :, :], gate[:, :, :], ALU.mult).then_inc(o_done, 1)


STRIDE = 16
N_CHUNK = PAST // STRIDE


def compress(nc, A):
    with ExitStack() as ctx:
        sb = lambda name, shape: ctx.enter_context(nc.sbuf_tensor(name, shape, F32))
        sem = nc.alloc_semaphore
        table = ctx.enter_context(nc.sbuf_tensor("table", [1, DEC_B * N_PAGES], I32))
        X = [sb(f"rows{i}", [P, STRIDE, KVW]) for i in range(2)]
        pw = sb("pos_w", [P, 4, STRIDE, HD])
        prod = [sb(f"prod{i}", [P, STRIDE, 2 * P]) for i in range(4)]
        C = sb("C", [P, 4, 2 * P])
        pooled, kv = sb("pooled", [P, 4, P]), sb("kv", [P, 4, P])
        ident, shift = sb("c_ident", [P, P]), sb("c_shift", [P, P])
        wbd = sb("wbd", [P, 2, P])
        ps_pool = ctx.enter_context(nc.psum_tensor("ps_pool", [P, 4, P], F32))
        ps_proj = ctx.enter_context(nc.psum_tensor("ps_proj", [P, 4, P], F32))
        consts, wts, zeroed = sem("c_consts"), sem("c_wts"), sem("c_zeroed")
        rows = [sem(f"c_rows{i}") for i in range(2)]
        pool_mul, dve_mul, C_ready, C_free = sem("c_pool_mul"), sem("c_dve_mul"), sem("c_C_ready"), sem("c_C_free")
        prod_free, used_pool, used_dve = sem("c_prod_free"), sem("c_used_pool"), sem("c_used_dve")
        pool_mm, pooled_ready, proj_mm, kv_ready, kv_sent = (
            sem("c_" + n) for n in ("pool_mm", "pooled_ready", "proj_mm", "kv_ready", "kv_sent"))
        x_zero, table_in = sem("c_x_zero"), sem("c_table")
        block = ctx.enter_context(nc.Block())
        NB = DEC_B + 1

        @block.sync
        def _(sp):
            sp.dma_start(table[:, :], A["page_table"]).then_inc(table_in, 16)
            sp.wait_ge(table_in, 16)

            def load_rows(b, slot):
                for p in range(N_PAGES):
                    page = sp.value_load(table[0:1, bass.ds(b * N_PAGES + p, 1)], min_val=0, max_val=N_POOL - 1)
                    sp.dma_start(X[slot][8 * p:8 * p + 8, :, :].rearrange("p s c -> p (s c)"),
                                 A["cmp_rows"][bass.ds(page, 1)].rearrange("a n x -> (a n) x"),
                                 max_dma_last_dim=8192).then_inc(rows[slot], 16)
            load_rows(0, 0)
            load_rows(1, 1)
            for dst, src in ((pw, "pos_w"), (ident, "ident"), (shift, "shift1")):
                sp.dma_start(dst[:], A[src]).then_inc(consts, 16)
            sp.wait_ge(zeroed, 1)
            for k, src in enumerate(("w_cmp_k", "w_cmp_v")):
                for h in range(2):
                    sp.dma_start(wbd[h * HD:(h + 1) * HD, k, h * HD:(h + 1) * HD], A[src]).then_inc(wts, 16)
            with sp.Fori(1, 4) as i:
                for j in range(2):
                    sp.wait_ge(used_pool, i * 2 + j - 1)
                    sp.wait_ge(used_dve, i * 2 + j - 1)
                    load_rows(i * 2 + j, j)
            sp.wait_ge(x_zero, 1)
            for t in range(4):
                src = A["u_tok"][:, t, P:P + KVW].rearrange("(n s) c -> n s c", s=STRIDE)
                sp.dma_start(X[0][8 * t:8 * t + 8, :, :], src).then_inc(rows[0], 16)

        def loop(eng, body, chain=None):
            with eng.Fori(0, 4) as i:
                for j in range(2):
                    body(i * 2 + j, j)
            body(8, 0)

        def rows_in(eng, b, slot):
            if isinstance(b, int):
                eng.wait_ge(rows[0], 16 * (4 * N_PAGES + 4))
            else:
                eng.wait_ge(rows[slot], (b - slot) * 8 * N_PAGES + 16 * N_PAGES)

        def multiply(eng, slot, kvr):
            x = X[slot][:, :, (kvr // 2) * 2 * P:(kvr // 2 + 1) * 2 * P].rearrange("p s (g d) -> p s g d", d=HD)
            w = pw[:, kvr, :, None, :].to_broadcast([P, STRIDE, 4, HD])
            out = prod[kvr][:, :, :].rearrange("p s (g d) -> p s g d", d=HD)
            return eng.tensor_tensor(out, x, w, ALU.mult)

        @block.gpsimd
        def _(pool):
            nc.gpsimd.memset(wbd[:, :, :], 0.0).then_inc(zeroed, 1)
            pool.wait_ge(consts, 48)

            def body(b, slot):
                rows_in(pool, b, slot)
                pool.wait_ge(prod_free, b * 1 + 1)
                multiply(nc.gpsimd, slot, 2).then_inc(pool_mul, 1)
                multiply(nc.gpsimd, slot, 3).then_inc(pool_mul, 1)
                pool.wait_ge(pool_mul, b * 2 + 2)
                pool.sem_inc(used_pool, 1)
            loop(pool, body)

        @block.vector
        def _(dve):
            dve.sem_inc(prod_free, 1)
            dve.wait_ge(consts, 48)

            def body(b, slot):
                if isinstance(b, int):
                    dve.wait_ge(used_pool, 7)
                    nc.vector.memset(X[0][:, :, :], 0.0).then_inc(x_zero, 1)
                rows_in(dve, b, slot)
                multiply(nc.vector, slot, 0).then_inc(dve_mul, 1)
                multiply(nc.vector, slot, 1).then_inc(dve_mul, 1)
                dve.wait_ge(dve_mul, b * 2 + 2)
                dve.sem_inc(used_dve, 1)
                dve.wait_ge(C_free, b * 1 + 1)
                for kvr in range(4):
                    if kvr == 2:
                        dve.wait_ge(pool_mul, b * 2 + 2)
                    ins = nc.vector.reduce_sum(C[:, kvr, :], prod[kvr][:, :, :].rearrange("p s c -> p c s"),
                                               axis=AX.X)
                ins.then_inc(C_ready, 1)
                dve.wait_ge(C_ready, b * 1 + 1)
                dve.sem_inc(prod_free, 1)
            loop(dve, body)

        @block.tensor
        def _(pe):
            pe.wait_ge(consts, 48)
            pe.wait_ge(wts, 64)

            def body(b, slot):
                pe.wait_ge(C_ready, b * 1 + 1)
                for kv_ in range(2):
                    for gp in range(2):
                        c = slice(gp * P, (gp + 1) * P)
                        nc.tensor.matmul(ps_pool[:, 2 * kv_ + gp, :], C[:, 2 * kv_, c], ident[:, :],
                                         start=True, stop=False)
                        ins = nc.tensor.matmul(ps_pool[:, 2 * kv_ + gp, :], C[:, 2 * kv_ + 1, c], shift[:, :],
                                               start=False, stop=True)
                ins.then_inc(pool_mm, 1)
                pe.wait_ge(pooled_ready, b * 1 + 1)
                for gp in range(2):
                    nc.tensor.matmul(ps_proj[:, gp, :], wbd[:, 0, :], pooled[:, gp, :], start=True, stop=True)
                for gp in range(2):
                    ins = nc.tensor.matmul(ps_proj[:, 2 + gp, :], pooled[:, 2 + gp, :], wbd[:, 1, :],
                                           start=True, stop=True)
                ins.then_inc(proj_mm, 1)
            loop(pe, body)

        @block.scalar
        def _(act):
            act.sem_inc(kv_sent, 32)
            act.sem_inc(C_free, 1)

            def body(b, slot):
                act.wait_ge(pool_mm, b * 1 + 1)
                nc.scalar.activation(pooled[:, :, :], ps_pool[:, :, :], ACT.Copy).then_inc(pooled_ready, 1)
                act.wait_ge(pooled_ready, b * 1 + 1)
                act.sem_inc(C_free, 1)
                act.wait_ge(proj_mm, b * 1 + 1)
                act.wait_ge(kv_sent, b * 32 + 32)
                nc.scalar.activation(kv[:, :, :], ps_proj[:, :, :], ACT.Copy).then_inc(kv_ready, 1)
                act.wait_ge(kv_ready, b * 1 + 1)
                act.dma_start(A["kcT"][bass.ds(b, 1)].rearrange("a k p n -> (a p) k n"), kv[:, 0:2, :])\
                    .then_inc(kv_sent, 16)
                act.dma_start(A["vc"][bass.ds(b, 1)].rearrange("a p k n -> (a p) k n"), kv[:, 2:4, :])\
                    .then_inc(kv_sent, 16)
            loop(act, body)
            act.wait_ge(kv_sent, 32 * (NB + 1))


N_TILE = SEQ // P
G_KV = 4
REP = 4
N_CMP_PAD = 32


def attend_prompt(nc, A):
    UNITS = [(r, t) for r in range(REP) for t in range(N_TILE)]
    NU = len(UNITS)
    with ExitStack() as ctx:
        sb = lambda name, shape: ctx.enter_context(nc.sbuf_tensor(name, shape, F32))
        sem = nc.alloc_semaphore
        psum = lambda name: ctx.enter_context(nc.psum_tensor(name, [P, 512], F32))
        q = [sb(f"a_q{j}", [HD, REP, SEQ]) for j in range(2)]
        kT = [sb(f"a_kT{j}", [HD, 2, SEQ]) for j in range(2)]
        vv = [sb(f"a_v{j}", [P, 2, N_TILE, HD]) for j in range(2)]
        kcT = [sb(f"a_kcT{j}", [HD, N_CMP_PAD]) for j in range(2)]
        vc = [sb(f"a_vc{j}", [N_CMP_PAD, HD]) for j in range(2)]
        bias = [sb(f"a_bias{j}", [P, REP, SEQ]) for j in range(2)]
        cbias = [sb(f"a_cbias{j}", [P, NU, N_CMP_PAD]) for j in range(2)]
        gates = [sb(f"a_gates{j}", [P, N_TILE, 3, REP]) for j in range(2)]
        ident, cmask = sb("a_ident", [P, P]), sb("a_cmask", [P, N_TILE, N_CMP_PAD])
        S = [sb(f"a_S{j}", [P, 2, SEQ]) for j in range(2)]
        Pm = [sb(f"a_P{j}", [P, 2, SEQ]) for j in range(2)]
        PT = [sb(f"a_PT{j}", [P, 2, SEQ]) for j in range(2)]
        Sc, Pc = sb("a_Sc", [P, NU, N_CMP_PAD]), sb("a_Pc", [P, NU, N_CMP_PAD])
        PTc = [sb(f"a_PTc{j}", [N_CMP_PAD, P]) for j in range(2)]
        cmax, csum, coef_c = sb("a_cmax", [P, NU]), sb("a_csum", [P, NU]), sb("a_coef_c", [P, NU])
        mx, sums, coef = sb("a_mx", [P, 2, 2]), sb("a_sums", [P, 4, 2]), sb("a_coef", [P, 2, 2])
        acc = sb("a_acc", [P, HD])
        out = [sb(f"a_out{j}", [P, N_TILE, REP, HD]) for j in range(2)]
        s_bank = [[psum(f"s_{n}{j}") for n in ("sel", "win")] for j in range(2)]
        pt_bank = [psum("pt_sel"), psum("pt_win")]
        c_bank, o_bank = psum("c_bank"), psum("o_bank")

        consts, g_in = sem("a_consts"), [sem(f"a_in{j}") for j in range(2)]
        q_scaled, c_scores, c_sub, c_exp, c_ready, gate_done = (
            sem("a_" + n) for n in ("q_scaled", "c_scores", "c_sub", "c_exp", "c_ready", "gate_done"))
        scores, max_ready, exp_done, t_done, evA, evB, pv_done, out_done = (
            sem("a_" + n) for n in ("scores", "max_ready", "exp_done", "t_done", "evA", "evB", "pv_done", "out_done"))
        chain, sent, cmax_ready = sem("a_chain"), sem("a_sent"), sem("a_cmax_ready")
        freed = sem("a_freed")
        settled, settled_dve = sem("a_settled"), sem("a_settled_dve")
        block = ctx.enter_context(nc.Block())
        N_IN = 13

        def keys(t):
            return (t + 1) * P

        @block.sync
        def _(sp):
            sp.dma_start(ident[:, :], A["ident"]).then_inc(consts, 16)
            sp.dma_start(cmask[:, :, :], A["cmask"]).then_inc(consts, 16)
            with sp.Fori(0, 2) as i:
                for j in range(2):
                    g = i * 2 + j
                    sp.wait_ge(freed, g + 1)
                    rows = lambda base: A["uT"][bass.ds(g * HD + base, HD), 0:SEQ]
                    dma = lambda dst, src: sp.dma_start(dst, src).then_inc(g_in[j], 16)
                    dma(q[j][:, :, :], A["uT"][bass.ds(g * (REP * HD) + COL_Q, REP * HD), 0:SEQ]
                        .rearrange("(r d) n -> d r n", r=REP))
                    dma(kT[j][:, 0, :], rows(COL_S))
                    dma(kT[j][:, 1, :], rows(COL_W))
                    for k, col in enumerate((COL_S, COL_W)):
                        c0 = col + 2 * P - 48 * P
                        dma(vv[j][:, k, :, :], A["u_tok"][:, :, bass.ds(g * HD + c0, HD)])
                    dma(kcT[j][:, :], A["kcT"][DEC_B, i, j * HD:(j + 1) * HD, 0:N_CMP_PAD]
                        if isinstance(i, int) else
                        A["kcT"][DEC_B][bass.ds(i, 1)].rearrange("a p n -> (a p) n")[j * HD:(j + 1) * HD, 0:N_CMP_PAD])
                    dma(vc[j][:, :], A["vc"][DEC_B, 0:N_CMP_PAD, :, :].rearrange("p k n -> p (k n)")
                        [:, bass.ds(g * HD, HD)])
                    for t in range(N_TILE):
                        dma(gates[j][:, t, :, :], A["u_tok"][:, t, COL_GATE - 48 * P:COL_GATE - 48 * P + N_GATE]
                            .rearrange("p (b g r) -> g p b r", b=3, g=G_KV)[bass.ds(g, 1)]
                            .rearrange("a p b r -> (a p) b r"))
                    dma(bias[j][:, :, :], A["bias_p"][bass.ds(g, 1)].rearrange("a p r n -> (a p) r n"))
                    dma(cbias[j][:, :, :], A["cbias_p"][bass.ds(g, 1)].rearrange("a p u n -> (a p) u n"))

        @block.scalar
        def _(act):
            f = nc.scalar.activation
            act.sem_inc(freed, 2)
            with act.Fori(0, 2) as i:
                for j in range(2):
                    g = i * 2 + j
                    act.wait_ge(g_in[j], i * 16 * N_IN + 16 * N_IN)
                    f(q[j][:, :, :], q[j][:, :, :], ACT.Copy, scale=HD ** -0.5).then_inc(q_scaled, 1)
                    f(gates[j][:, :, :, :], gates[j][:, :, :, :], ACT.Sigmoid).then_inc(gate_done, 1)

                    def exps(u):
                        r, t = UNITS[u]
                        act.wait_ge(max_ready, g * NU + u + 1)
                        for k in range(2):
                            ins = f(Pm[u % 2][:, k, 0:keys(t)], S[u % 2][:, k, 0:keys(t)], ACT.Exp,
                                    bias=mx[:, u % 2, k:k + 1], accum_out=sums[:, u % 4, k:k + 1])
                        ins.then_inc(exp_done, 1)
                    act.wait_ge(c_sub, g + 1)
                    f(Pc[:, :, :], Sc[:, :, :], ACT.Exp).then_inc(c_exp, 1)
                    exps(0)
                    for u, (r, t) in enumerate(UNITS):
                        if u + 1 < NU:
                            exps(u + 1)
                        act.wait_ge(t_done, g * NU + u + 1)
                        f(PT[u % 2][:, 0, 0:keys(t)], pt_bank[0][:, 0:keys(t)], ACT.Copy)
                        f(PTc[u % 2][:, :], c_bank[0:N_CMP_PAD, 0:P], ACT.Copy).then_inc(evA, 1)
                    act.wait_ge(out_done, g * NU + NU)
                    act.dma_start(A["obN"][:, :, bass.ds(g * (REP * HD), REP * HD)],
                                  out[j][:, :, :, :].rearrange("p t r d -> p t (r d)")).then_inc(sent, 16)
                    act.wait_ge(sent, g * 16 + 16)
                    act.sem_inc(freed, 1)

        @block.vector
        def _(dve):
            v = nc.vector
            link = same_engine(dve, chain)
            dve.wait_ge(consts, 32)
            with dve.Fori(0, 2) as i:
                for j in range(2):
                    g = i * 2 + j

                    def maxes(u):
                        r, t = UNITS[u]
                        dve.wait_ge(scores, g * NU + u + 1)
                        dve.sem_inc(settled_dve, 1)
                        for k in range(2):
                            last = v.tensor_tensor_reduce(
                                out=S[u % 2][:, k, 0:keys(t)], in0=s_bank[u % 2][k][:, 0:keys(t)],
                                in1=bias[j][:, r, SEQ - keys(t):SEQ], scale=1.0, scalar=-3e38,
                                op0=ALU.add, op1=ALU.max, accum_out=mx[:, u % 2, k:k + 1])
                        link(last)
                        v.tensor_scalar(mx[:, u % 2, :], mx[:, u % 2, :], -1.0, None, ALU.mult).then_inc(max_ready, 1)
                    dve.wait_ge(c_scores, g + 1)
                    link(v.tensor_tensor(Sc[:, :, :], c_bank[:, :].rearrange("p (u n) -> p u n", n=N_CMP_PAD),
                                         cbias[j][:, :, :], ALU.add))
                    link(v.tensor_reduce(cmax[:, :], Sc[:, :, :], axis=AX.X, op=ALU.max))
                    v.tensor_tensor(Sc[:, :, :], Sc[:, :, :], cmax[:, :, None].to_broadcast([P, NU, N_CMP_PAD]),
                                    ALU.subtract).then_inc(c_sub, 1)
                    maxes(0)
                    dve.wait_ge(c_exp, g + 1)
                    for r in range(REP):
                        last = v.tensor_tensor(Pc[:, 4 * r:4 * r + 4, :], Pc[:, 4 * r:4 * r + 4, :], cmask[:, :, :],
                                               ALU.mult)
                    last.then_inc(c_ready, 1)
                    dve.wait_ge(c_ready, g + 1)
                    link(v.reduce_sum(csum[:, :], Pc[:, :, :], axis=AX.X))
                    link(v.tensor_scalar(csum[:, :], csum[:, :], 1e-30, None, ALU.max))
                    link(v.reciprocal(csum[:, :], csum[:, :]))
                    dve.wait_ge(gate_done, g + 1)
                    link(v.tensor_tensor(coef_c[:, :].rearrange("p (r t) -> p r t", t=N_TILE),
                                         csum[:, :].rearrange("p (r t) -> p r t", t=N_TILE),
                                         gates[j][:, :, 0, :].rearrange("p t r -> p r t"), ALU.mult))

                    def outs(u):
                        r, t = UNITS[u]
                        link(v.reciprocal(coef[:, u % 2, :], sums[:, u % 4, :]))
                        link(v.tensor_tensor(coef[:, u % 2, :], coef[:, u % 2, :], gates[j][:, t, 1:3, r], ALU.mult))
                        dve.wait_ge(pv_done, g * NU + u + 1)
                        o = lambda k: o_bank[:, k * HD:(k + 1) * HD]
                        dst = out[j][:, t, r, :]
                        link(v.tensor_scalar(acc[:, :], o(0), coef[:, u % 2, 0:1], None, ALU.mult))
                        link(v.scalar_tensor_tensor(out=acc[:, :], in0=o(1), scalar=coef[:, u % 2, 1:2], in1=acc[:, :],
                                                    op0=ALU.mult, op1=ALU.add))
                        v.scalar_tensor_tensor(out=dst, in0=o(2), scalar=coef_c[:, u:u + 1],
                                               in1=acc[:, :], op0=ALU.mult, op1=ALU.add).then_inc(out_done, 1)
                    for u, (r, t) in enumerate(UNITS):
                        if u + 1 < NU:
                            maxes(u + 1)
                        dve.wait_ge(t_done, g * NU + u + 1)
                        v.tensor_copy(PT[u % 2][:, 1, 0:keys(t)], pt_bank[1][:, 0:keys(t)]).then_inc(evB, 1)
                        if u:
                            outs(u - 1)
                    outs(NU - 1)
                link.restart()

        @block.tensor
        def _(pe):
            mm = nc.tensor.matmul
            settle = lambda: pe.sem_inc(settled, 1)
            pe.wait_ge(consts, 32)
            with pe.Fori(0, 2) as i:
                for j in range(2):
                    g = i * 2 + j

                    def score(u):
                        r, t = UNITS[u]
                        if u >= 2:
                            pe.wait_ge(max_ready, g * NU + u - 1)
                            settle()
                        for k in range(2):
                            ins = mm(s_bank[u % 2][k][:, 0:keys(t)], q[j][:, r, t * P:(t + 1) * P],
                                     kT[j][:, k, 0:keys(t)], start=True, stop=True)
                        ins.then_inc(scores, 1)
                    pe.wait_ge(q_scaled, g + 1)
                    settle()
                    for u, (r, t) in enumerate(UNITS):
                        ins = mm(c_bank[:, u * N_CMP_PAD:(u + 1) * N_CMP_PAD], q[j][:, r, t * P:(t + 1) * P],
                                 kcT[j][:, :], start=True, stop=True)
                    ins.then_inc(c_scores, 1)
                    score(0)

                    def values(u):
                        r, t = UNITS[u]
                        pe.wait_ge(evA, g * NU + u + 1)
                        pe.wait_ge(evB, g * NU + u + 1)
                        if u:
                            pe.wait_ge(out_done, g * NU + u)
                        settle()
                        for k in range(2):
                            for b in range(t + 1):
                                mm(o_bank[:, k * HD:(k + 1) * HD], PT[u % 2][:, k, b * P:(b + 1) * P],
                                   vv[j][:, k, b, :], start=(b == 0), stop=(b == t))
                        mm(o_bank[:, 2 * HD:3 * HD], PTc[u % 2][:, :], vc[j][:, :], start=True, stop=True)\
                            .then_inc(pv_done, 1)
                    for u, (r, t) in enumerate(UNITS):
                        if u + 1 < NU:
                            score(u + 1)
                        pe.wait_ge(exp_done, g * NU + u + 1)
                        if u == 0:
                            pe.wait_ge(c_ready, g + 1)
                        else:
                            pe.wait_ge(evA, g * NU + u)
                            pe.wait_ge(evB, g * NU + u)
                        settle()
                        for k in range(2):
                            for b in range(t + 1):
                                nc.tensor.transpose(pt_bank[k][:, b * P:(b + 1) * P],
                                                    Pm[u % 2][:, k, b * P:(b + 1) * P], ident[:, :])
                        nc.tensor.transpose(c_bank[0:N_CMP_PAD, 0:P], Pc[:, u, :], ident[:, :]).then_inc(t_done, 1)
                        if u:
                            values(u - 1)
                    values(NU - 1)
                    pe.wait_ge(out_done, g * NU + NU)
                    settle()


S_SEL, S_SNEW, S_WIN, S_WNEW, S_CMP, S_END = 0, 2048, 2052, 2564, 2568, 2696
N_SELECT = 16


def attend_samples(nc, A):
    with ExitStack() as ctx:
        sb = lambda name, shape: ctx.enter_context(nc.sbuf_tensor(name, shape, F32))
        sem = nc.alloc_semaphore
        table = ctx.enter_context(nc.sbuf_tensor("d_table", [1, DEC_B * N_PAGES], I32))
        kvS = [[sb(f"d_kv{j}{b}", [P, N_PAGES, 4 * P]) for b in range(2)] for j in range(2)]
        kW, vW = ([sb(f"d_{n}{b}", [P, 2, WINDOW]) for b in range(2)] for n in ("kW", "vW"))
        kC, vC = ([sb(f"d_{n}{b}", [P, 2, P]) for b in range(2)] for n in ("kC", "vC"))
        vN = [sb(f"d_vN{b}", [DEC_T, 2, 2 * P]) for b in range(2)]
        q_raw, q_all = sb("d_q_raw", [P, 2, REP, NS]), sb("d_q_all", [P, DEC_B, 2, 32])
        q = sb("d_q", [P, 2, 2, 32])
        kN_all, kN = sb("d_kN_all", [P, 2, 2, NS]), sb("d_kN", [P, 2, 2, 2, DEC_T])
        bias, S, PT = sb("d_bias", [P, S_END]), sb("d_S", [P, S_END]), sb("d_PT", [P, N_PAGES, P])
        PTc, PTw, PTn = sb("d_PTc", [P, P]), sb("d_PTw", [P, 4, P]), sb("d_PTn", [DEC_T, 2, P])
        ident, gsum, overlap = sb("d_ident", [P, P]), sb("d_gsum", [P, P]), sb("d_overlap", [P, N_SEL])
        selc = sb("d_selc", [P, 2, N_SEL])
        lower = sb("d_lower", [P, N_SEL, N_SEL])
        gmask = sb("d_gmask", [P, G_KV])
        imp, score, rank, mb = (sb("d_" + n, [P, N_SEL]) for n in ("imp", "score", "rank", "mb"))
        gt, eq = sb("d_gt", [P, N_SEL, N_SEL]), sb("d_eq", [P, N_SEL, N_SEL])
        mx, nmx, sums, coef = sb("d_mx", [P, 3]), sb("d_nmx", [P, 3]), sb("d_sums", [P, 3]), sb("d_coef", [P, 3])
        gates = sb("d_gates", [P, 4, 3])
        tok_gates, own_head = sb("d_tok_gates", [NS, N_GATE]), sb("d_own_head", [P, 16])
        spread = PT[0:NS, 0:4, :]
        row_gates = eq[:, 0:12, 0:16]
        gates_now = sb("d_gates_now", [P, 3])
        acc, o = sb("d_acc", [P, G_KV, HD]), sb("d_o", [P, HD])
        psum = lambda name: ctx.enter_context(nc.psum_tensor(name, [P, 512], F32))
        sc = [psum("d_sc0"), psum("d_sc1")]
        small, pt, ob, oc, ps_imp = psum("d_small"), [psum("d_pt0"), psum("d_pt1")], psum("d_ob"), psum("d_oc"), psum("d_ps_imp")

        names = ("consts", "table_in", "q_in", "zeroed", "q_ready", "set_up", "small_done", "small_out", "win_sc",
                 "c_exp", "c_norm", "c_max", "ptc_done", "ptc_out", "imp_done", "imp_out", "imp2_done", "w_max", "w_exp",
                 "s_max", "s_exp", "o_done", "freed", "sent", "settled", "chain", "o_ready", "sel_sc", "sel_out",
                 "pt_done", "pt_out", "gates_ready", "gates_spread", "pv_c", "win_out", "ptn_done")
        s = {n: sem("d_" + n) for n in names}
        pages_in = [sem(f"d_pages_in{j}") for j in range(2)]
        rest_in = sem("d_rest_in")
        block = ctx.enter_context(nc.Block())
        N_REST = 10
        GROUPS = [(kind, n) for kind in ("w", "s") for n in range(1 if kind == "w" else 4)]

        @block.sync
        def _(sp):
            sp.dma_start(table[:, :], A["page_table"]).then_inc(s["table_in"], 16)
            for dst, src in ((ident, "ident"), (gsum, "gsum"), (overlap, "overlap"), (selc, "selc"), (lower, "lower"),
                             (gmask, "gmask"), (bias, "bias_s")):
                sp.dma_start(dst[:], A[src]).then_inc(s["consts"], 16)
            for g2 in range(2):
                for gp in range(2):
                    row = COL_Q + (2 * gp + g2) * REP * HD
                    sp.dma_start(q_raw[g2 * HD:(g2 + 1) * HD, gp, :, :],
                                 A["uT"][row:row + REP * HD, SEQ:NT].rearrange("(r d) n -> d r n", r=REP))\
                        .then_inc(s["q_in"], 16)
            for k, col in enumerate((COL_S, COL_W)):
                sp.dma_start(kN_all[:, k, :, :], A["uT"][col:col + 2 * P, SEQ:NT].rearrange("(g p) n -> p g n", g=2))\
                    .then_inc(s["q_in"], 16)
            sp.dma_start(tok_gates[:, :], A["u_tail"][1:1 + NS, COL_GATE:COL_GATE + N_GATE]).then_inc(s["q_in"], 16)
            sp.dma_start(spread, A["spread"]).then_inc(s["q_in"], 16)
            sp.dma_start(own_head[:, :], A["own_head"]).then_inc(s["q_in"], 16)
            sp.wait_ge(s["table_in"], 16)
            with sp.Fori(0, 2) as i:
                for j in range(2):
                    bp = i * 2 + j
                    sp.wait_ge(s["freed"], bp + 2)
                    for b2 in range(2):
                        for p in range(N_PAGES):
                            page = sp.value_load(table[0:1, bass.ds(bp * (2 * N_PAGES) + b2 * N_PAGES + p, 1)],
                                                 min_val=0, max_val=N_POOL - 1)
                            sp.dma_start(kvS[j][b2][:, p, :], A["sel_kv"][bass.ds(page, 1)]
                                         .rearrange("a p n -> (a p) n")).then_inc(pages_in[j], 16)
                    sp.wait_ge(s["freed"], bp + 3)
                    for b2 in range(2):
                        b = bp * 2 + b2
                        one = lambda name: A[name][bass.ds(b, 1)]
                        for dst, src in ((kW[b2][:, :, :], one("win_k").rearrange("a k p n -> p (a k) n")),
                                         (vW[b2][:, :, :].rearrange("p a (c n) -> p (a c) n", n=2 * P),
                                          one("win_v").rearrange("a p t n -> (a p) t n")),
                                         (kC[b2][:, :, :], one("kcT").rearrange("a k p n -> p (a k) n")),
                                         (vC[b2][:, :, :], one("vc").rearrange("a p k n -> (a p) k n")),
                                         (vN[b2][:, :, :], A["u_tail"][bass.ds(b * DEC_T + 1, DEC_T), COL_S + 2 * P:COL_W + 4 * P]
                                          .rearrange("p (k n) -> p k n", n=2 * P)[:, 0:3:2, :])):
                            sp.dma_start(dst, src).then_inc(rest_in, 16)

        @block.scalar
        def _(act):
            f = nc.scalar.activation
            act.sem_inc(s["freed"], 3)
            act.wait_ge(s["q_in"], 16 * 9)
            act.wait_ge(s["zeroed"], 1)
            for g2 in range(2):
                rows = slice(g2 * HD, (g2 + 1) * HD)
                for gp in range(2):
                    ins = f(q_all[rows, :, gp, g2 * 16:(g2 + 1) * 16].rearrange("p b (t r) -> p b t r", r=REP),
                            q_raw[rows, gp, :, :].rearrange("p r (b t) -> p b t r", t=DEC_T), ACT.Copy, scale=HD ** -0.5)
            ins.then_inc(s["q_ready"], 1)
            f(tok_gates[:, :], tok_gates[:, :], ACT.Sigmoid).then_inc(s["gates_ready"], 1)
            with act.Fori(0, 2) as i:
                for j in range(2):
                    bp = i * 2 + j
                    w = lambda name, n=1, k=1: act.wait_ge(s[name], bp * n + k)

                    def soft(name, a, b, k):
                        f(S[:, a:b], S[:, a:b], ACT.Exp, bias=nmx[:, k:k + 1], accum_out=sums[:, k:k + 1])\
                            .then_inc(s[name], 1)
                    w("c_max")
                    soft("c_exp", S_CMP, S_END, 2)
                    w("ptc_done")
                    f(PTc[:, :], pt[0][:, 0:P], ACT.Copy).then_inc(s["ptc_out"], 1)
                    w("imp_done")
                    f(imp[:, :], ps_imp[:, 0:N_SEL], ACT.Copy).then_inc(s["imp_out"], 1)
                    w("w_max")
                    soft("w_exp", S_WIN, S_CMP, 1)
                    w("pt_done", 5, 1)
                    f(PTw[:, :, :], pt[1][:, :].rearrange("p (k n) -> p k n", k=4), ACT.Copy).then_inc(s["pt_out"], 1)
                    w("s_max")
                    soft("s_exp", S_SEL, S_WIN, 0)
                    w("ptn_done")
                    f(PTn[:, :, :], ps_imp[0:DEC_T, 0:2 * P].rearrange("p (k n) -> p k n", k=2), ACT.Copy)\
                        .then_inc(s["pt_out"], 1)
                    for n in range(4):
                        w("pt_done", 5, n + 2)
                        f(PT[:, 4 * n:4 * n + 4, :], pt[n % 2][:, :].rearrange("p (k n) -> p k n", k=4), ACT.Copy)\
                            .then_inc(s["pt_out"], 1)
                    w("o_ready")
                    act.dma_start(A["obS"][bass.ds(bp, 1)].rearrange("a p n -> (a p) n"), o[:, :]).then_inc(s["sent"], 16)
                    w("sent", 16, 16)
                    act.sem_inc(s["freed"], 1)

        @block.vector
        def _(dve):
            v = nc.vector
            tt, ts, stt = v.tensor_tensor, v.tensor_scalar, v.scalar_tensor_tensor
            link = same_engine(dve, s["chain"])
            v.memset(q_all[:, :, :, :], 0.0).then_inc(s["zeroed"], 1)
            dve.wait_ge(s["consts"], 16 * 7)
            dve.wait_ge(s["q_ready"], 1)
            dve.wait_ge(s["gates_spread"], 1)
            link(tt(row_gates, small[:, 0:4 * N_GATE].rearrange("p (x h) -> p x h", h=16),
                    own_head[:, None, :].to_broadcast([P, 12, 16]), ALU.mult))
            link(v.reduce_sum(gates[:, :, :].rearrange("p b c -> p (b c)"), row_gates, axis=AX.X))
            link.restart()
            with dve.Fori(0, 2) as i:
                for j in range(2):
                    bp = i * 2 + j
                    w = lambda name, n=1, k=1: dve.wait_ge(s[name], bp * n + k)
                    w("freed", 1, 3)
                    v.tensor_copy(q[:, :, :, :], q_all[:, bass.ds(bp * 2, 2), :, :])
                    v.tensor_copy(gates_now[:, :], gates[:, bass.ds(bp, 1), :].rearrange("p a c -> p (a c)"))
                    for b2 in range(2):
                        last = v.tensor_copy(kN[:, b2, :, :, :], kN_all[:, :, :, bass.ds(bp * (2 * DEC_T) + b2 * DEC_T, DEC_T)])
                    last.then_inc(s["set_up"], 1)
                    w("small_done")
                    tt(S[:, S_CMP:S_END], small[:, 0:P], bias[:, S_CMP:S_END], ALU.add)
                    tt(S[:, S_SNEW:S_WIN], small[:, P:P + DEC_T], bias[:, S_SNEW:S_WIN], ALU.add)
                    link(tt(S[:, S_WNEW:S_CMP], small[:, P + DEC_T:P + 2 * DEC_T], bias[:, S_WNEW:S_CMP], ALU.add))

                    def neg_max(a, b, k, name):
                        link(v.reduce_max(mx[:, k:k + 1], S[:, a:b], axis=AX.X))
                        ts(nmx[:, k:k + 1], mx[:, k:k + 1], -1.0, None, ALU.mult).then_inc(s[name], 1)
                    neg_max(S_CMP, S_END, 2, "c_max")
                    for n in range(5):
                        w("sel_sc", 5, n + 1)
                        a = S_WIN if n == 0 else 512 * (n - 1)
                        tt(S[:, a:a + 512], sc[n % 2][:, :], bias[:, a:a + 512], ALU.add).then_inc(s["sel_out"], 1)
                        if n == 0:
                            w("sel_out", 5, 1)
                            neg_max(S_WIN, S_CMP, 1, "w_max")
                        if n == 1:
                            w("c_exp")
                            link(v.reciprocal(coef[:, 2:3], sums[:, 2:3]))
                            ts(S[:, S_CMP:S_END], S[:, S_CMP:S_END], coef[:, 2:3], None, ALU.mult).then_inc(s["c_norm"], 1)
                    w("sel_out", 5, 5)
                    w("imp2_done")
                    link(tt(score[:, :], ps_imp[:, 64:64 + N_SEL], selc[:, 0, :], ALU.mult))
                    link(tt(score[:, :], score[:, :], selc[:, 1, :], ALU.add))
                    si = score[:, None, :].to_broadcast([P, N_SEL, N_SEL])
                    sj = score[:, :, None].to_broadcast([P, N_SEL, N_SEL])
                    tt(gt[:, :, :], si, sj, ALU.is_gt)
                    link(tt(eq[:, :, :], si, sj, ALU.is_equal))
                    link(tt(eq[:, :, :], eq[:, :, :], lower[:, :, :], ALU.mult))
                    link(tt(gt[:, :, :], gt[:, :, :], eq[:, :, :], ALU.add))
                    link(v.reduce_sum(rank[:, :], gt[:, :, :], axis=AX.X))
                    link(ts(mb[:, :], rank[:, :], N_SELECT - 0.5, NEG, ALU.is_gt, ALU.mult))
                    link(tt(S[:, 0:PAST].rearrange("p (j k) -> p j k", k=SEL_BLOCK),
                            S[:, 0:PAST].rearrange("p (j k) -> p j k", k=SEL_BLOCK),
                            mb[:, 0:N_SEL - 1, None].to_broadcast([P, N_SEL - 1, SEL_BLOCK]), ALU.add))
                    link(ts(S[:, S_SNEW:S_WIN], S[:, S_SNEW:S_WIN], mb[:, N_SEL - 1:N_SEL], None, ALU.add))
                    neg_max(S_SEL, S_WIN, 0, "s_max")
                    w("s_exp")
                    w("w_exp")
                    link(v.reciprocal(coef[:, 0:2], sums[:, 0:2]))
                    link(tt(coef[:, 0:2], coef[:, 0:2], gates_now[:, 1:3], ALU.mult))
                    w("o_done")
                    flat = acc[:, :, :].rearrange("p g d -> p (g d)")
                    link(ts(flat, ob[:, 0:2 * P], coef[:, 0:1], None, ALU.mult))
                    link(stt(out=flat, in0=ob[:, 2 * P:4 * P], scalar=coef[:, 1:2], in1=flat, op0=ALU.mult, op1=ALU.add))
                    link(stt(out=flat, in0=oc[:, 0:2 * P], scalar=gates_now[:, 0:1], in1=flat, op0=ALU.mult, op1=ALU.add))
                    link(tt(acc[:, :, :], acc[:, :, :], gmask[:, :, None].to_broadcast([P, G_KV, HD]), ALU.mult))
                    v.reduce_sum(o[:, :], acc[:, :, :].rearrange("p g d -> p d g"), axis=AX.X).then_inc(s["o_ready"], 1)
                link.restart()

        @block.tensor
        def _(pe):
            mm = nc.tensor.matmul
            pe.wait_ge(s["consts"], 16 * 7)
            pe.wait_ge(s["gates_ready"], 1)
            for bp in range(4):
                ins = mm(small[:, bp * N_GATE:(bp + 1) * N_GATE], spread[:, bp, :], tok_gates[:, :], start=True, stop=True)
            ins.then_inc(s["gates_spread"], 1)
            with pe.Fori(0, 2) as i:
                for j in range(2):
                    bp = i * 2 + j

                    def w(*conditions):
                        for name, n, k in conditions:
                            pe.wait_ge(s[name], bp * n + k)
                        pe.sem_inc(s["settled"], 1)
                    rows = lambda b2, gp: slice(b2 * HD + gp * 32, b2 * HD + gp * 32 + 32)
                    PAIRS = [(b2, gp) for b2 in range(2) for gp in range(2)]
                    pe.wait_ge(rest_in, bp * (16 * N_REST) + 16 * N_REST)
                    w(("set_up", 1, 1))
                    for b2, gp in PAIRS:
                        mm(small[rows(b2, gp), 0:P], q[:, b2, gp, :], kC[b2][:, gp, :], start=True, stop=True)
                        for k in range(2):
                            c = P + k * DEC_T
                            ins = mm(small[rows(b2, gp), c:c + DEC_T], q[:, b2, gp, :], kN[:, b2, k, gp, :],
                                     start=True, stop=True)
                    ins.then_inc(s["small_done"], 1)
                    for n in range(5):
                        if n >= 2:
                            w(("sel_out", 5, n - 1))
                        if n == 1:
                            pe.wait_ge(pages_in[j], i * (2 * N_PAGES * 16) + 2 * N_PAGES * 16)
                            pe.sem_inc(s["settled"], 1)
                        for b2, gp in PAIRS:
                            rhs = kW[b2][:, gp, :] if n == 0 else kvS[j][b2][:, 4 * (n - 1):4 * n, gp * P:(gp + 1) * P]
                            out = sc[n % 2][rows(b2, gp), :]
                            if n:
                                out = out.rearrange("p (a k) -> p a k", k=PAGE)
                            ins = mm(out, q[:, b2, gp, :], rhs, start=True, stop=True)
                        ins.then_inc(s["sel_sc"], 1)
                    w(("c_norm", 1, 1))
                    nc.tensor.transpose(pt[0][:, 0:P], S[:, S_CMP:S_END], ident[:, :]).then_inc(s["ptc_done"], 1)
                    w(("ptc_out", 1, 1))
                    mm(ps_imp[:, 0:N_SEL], PTc[:, :], overlap[:, :], start=True, stop=True).then_inc(s["imp_done"], 1)
                    w(("imp_out", 1, 1))
                    mm(ps_imp[:, 64:64 + N_SEL], gsum[:, :], imp[:, :], start=True, stop=True).then_inc(s["imp2_done"], 1)
                    halves = [slice(b2 * HD, (b2 + 1) * HD) for b2 in range(2)]
                    for b2, h in enumerate(halves):
                        mm(oc[h, 0:2 * P], PTc[:, h], vC[b2][:, :, :].rearrange("p a n -> p (a n)"), start=True, stop=True)
                    w(("w_exp", 1, 1))
                    for n in range(4):
                        ins = nc.tensor.transpose(pt[1][:, n * P:(n + 1) * P], S[:, S_WIN + n * P:S_WIN + (n + 1) * P],
                                                  ident[:, :])
                    ins.then_inc(s["pt_done"], 1)
                    w(("s_exp", 1, 1))
                    for k, c in enumerate((S_SNEW, S_WNEW)):
                        ins = nc.tensor.transpose(ps_imp[0:DEC_T, k * P:(k + 1) * P], S[:, c:c + DEC_T], ident[:, :])
                    ins.then_inc(s["ptn_done"], 1)
                    for n in range(4):
                        w(("pt_out", 6, 1 if n < 2 else n + 1))
                        for k in range(4):
                            c = (4 * n + k) * P
                            ins = nc.tensor.transpose(pt[n % 2][:, k * P:(k + 1) * P], S[:, c:c + P], ident[:, :])
                        ins.then_inc(s["pt_done"], 1)
                    w(("pt_out", 6, 6))
                    for b2, h in enumerate(halves):
                        for kind, tiles, pts, vals in ((0, N_PAGES, PT, kvS[j][b2][:, :, 2 * P:4 * P]),
                                                       (1, 4, PTw, vW[b2][:, :, :].rearrange("p a (c n) -> p (a c) n", n=2 * P))):
                            out = ob[h, kind * 2 * P:(kind + 1) * 2 * P]
                            for n in range(tiles):
                                mm(out, pts[:, n, h], vals[:, n, :], start=(n == 0), stop=False)
                            ins = mm(out, PTn[:, kind, h], vN[b2][:, kind, :], start=False, stop=True)
                    ins.then_inc(s["o_done"], 1)


KW = A_WIDTH // P
N_OUT = D_MODEL // P


def merge_and_out(nc, A):
    with ExitStack() as ctx:
        sb = lambda name, shape, dt=F32: ctx.enter_context(nc.sbuf_tensor(name, shape, dt))
        sem = nc.alloc_semaphore
        o_lo = sb("m_o_lo", [P, KD, NT], F32R)
        w = [sb(f"m_w{j}", [P, KD, P]) for j in range(2)]
        w_hi, w_lo = ([sb(f"m_w_{n}{j}", [P, KD, P], F32R) for j in range(2)] for n in ("hi", "lo"))
        gates = [sb(f"m_gates{j}", [P, 2, NT]) for j in range(2)]
        prod = sb("m_prod", [P, 2, NT])
        xr, sq = (sb("m_" + n, [P, 2, NT]) for n in ("xr", "sq"))
        oa_s, ob_s = (t[0:NS, :, :].rearrange("p a n -> p (a n)")[:, 0:1024] for t in (xr, sq))
        ident, ones, g_out, eps = sb("m_ident", [P, P]), sb("m_ones", [P, P]), sb("m_g_out", [P, KD]), sb("m_eps", [P, 1])
        own = lambda stack, name, shape, dt: stack.enter_context(nc.sbuf_tensor(name, shape, dt))
        with ExitStack() as place:
            o_hi = own(place, "m_o_hi", [P, KD, NT], F32R)
            with ExitStack() as upper:
                buf = own(upper, "m_buf", [P, KD * NT], F32)
                o_raw = own(upper, "m_o_raw", [P, KD, NT], F32)
                gT = buf[:, 0:KW * NT].rearrange("p (k n) -> p k n", n=NT)
                ob_tok = buf[:, KW * NT:KW * NT + 4096].rearrange("p (t n) -> p t n", t=4)
                sg = o_raw[:, KW:KD, :]
            m_hi, m_lo = (own(place, "m_m_" + n, [P, KD, NT], F32R) for n in ("hi", "lo"))
        h = own(ctx, "m_h", [P, KD, NT], F32)
        ps = [[ctx.enter_context(nc.psum_tensor(f"m_ps{j}{k}", [P, 2, 512], F32)) for k in range(2)] for j in range(2)]
        sum_sq = ps[0][1]
        g_in, ob_in, oa_in, consts = sem("m_g_in"), sem("m_ob_in"), sem("m_oa_in"), sem("m_consts")
        sig, silu, tps, taken, o_hi_done, o_lo_done = (
            sem("m_" + n) for n in ("sig", "silu", "tps", "taken", "o_hi_done", "o_lo_done"))
        w_in, gates_in, x_in = ([sem(f"m_{n}{j}") for j in range(2)] for n in ("w_in", "gates_in", "x_in"))
        w_hi_done, w_lo_done, mm_done, multiplied, m_sum, m_hi_done, m_lo_done = (
            sem("m_" + n) for n in ("w_hi_done", "w_lo_done", "mm_done", "multiplied", "m_sum", "m_hi_done", "m_lo_done"))
        added, squared, summed, rooted, scaled, sent = (
            sem("m_" + n) for n in ("added", "squared", "summed", "rooted", "scaled", "sent"))
        chain, settled, ones_set = sem("m_chain"), sem("m_settled"), sem("m_ones_set")
        block = ctx.enter_context(nc.Block())
        two = lambda t: t.rearrange("p (a n) -> p a n", a=2)

        @block.sync
        def _(sp):
            def weights(c, j):
                src = A["w_mo"][bass.ds(c, 1)].rearrange("a p k n -> (a p) k n")
                sp.dma_start(w[j][:, :, :], src).then_inc(w_in[j], 16)

            def merge_gates(c, j):
                src = A["uT"][ROW_M:N_ROWS, :].rearrange("(k c p) n -> c p k n", k=2, p=P)[bass.ds(c, 1)]
                sp.dma_start(gates[j][:, :, :], src.rearrange("a p k n -> (a p) k n")).then_inc(gates_in[j], 16)

            def residual(n, j):
                sp.dma_start(xr[:, j, :], A["xT"][:, bass.ds(n, 1), :].rearrange("p a n -> p (a n)"))\
                    .then_inc(x_in[j], 16)
            sp.dma_start(ob_tok, A["obN"]).then_inc(ob_in, 16)
            sp.dma_start(o_raw[:, 0:KW, 0:SEQ], A["oaT"].rearrange("c p n -> p c n")).then_inc(oa_in, 16)
            for c in range(2):
                weights(c, c)
                merge_gates(c, c)
            with sp.Fori(1, 8) as i:
                for j in range(2):
                    c = i * 2 + j
                    sp.wait_ge(w_lo_done, c - 1)
                    weights(c, j)
                    sp.wait_ge(multiplied, c + 1)
                    merge_gates(c, j)
            for c in (N_OUT, N_OUT + 1):
                sp.wait_ge(w_lo_done, c - 1)
                weights(c, c % 2)
            for n in range(2):
                residual(n, n)
            with sp.Fori(9, 16) as i:
                for j in range(2):
                    c = i * 2 + j
                    sp.wait_ge(w_lo_done, c - 1)
                    weights(c, j)
                    sp.wait_ge(added, c - 1 - N_OUT)
                    residual(c - N_OUT, j)

        @block.gpsimd
        def _(pool):
            nc.gpsimd.memset(ones[:, :], 1.0).then_inc(ones_set, 1)
            for q in range(4):
                pool.wait_ge(scaled, 4 * q + 4)
                pool.dma_start(A["yT"][:, 4 * q:4 * q + 4, :], h[:, 4 * q:4 * q + 4, :]).then_inc(sent, 16)
            pool.wait_ge(sent, 64)

        @block.scalar
        def _(act):
            f = nc.scalar.activation
            act.dma_start(gT, A["uT"][COL_GB:COL_GB + 1024, :].rearrange("(c p) n -> p c n", p=P)).then_inc(g_in, 16)
            for dst, src in ((ident, "ident"), (g_out, "g_out")):
                act.dma_start(dst[:, :], A[src]).then_inc(consts, 16)
            act.dma_start(oa_s[:, :].rearrange("n (h d) -> n h d", h=16), A["oS"].rearrange("h n d -> n h d"))\
                .then_inc(ob_in, 16)
            for b in range(DEC_B):
                src = A["obS"][b // 2, (b % 2) * HD:(b % 2 + 1) * HD, :].rearrange("(g t r) d -> t g (r d)", g=G_KV, t=DEC_T)
                act.dma_start(ob_s[b * DEC_T:(b + 1) * DEC_T, :].rearrange("n (g x) -> n g x", g=G_KV), src)\
                    .then_inc(ob_in, 16)
            act.wait_ge(g_in, 16)
            f(sg, gT, ACT.Sigmoid).then_inc(sig, 1)

            def high_part(c, j):
                act.wait_ge(w_in[j], (c - j) * 8 + 16)
                act.wait_ge(mm_done, c)
                f(w_hi[j][:, :, :], w[j][:, :, :], ACT.Copy).then_inc(w_hi_done, 1)
            act.wait_ge(w_in[0], 16)
            f(w_hi[0][:, :, :], w[0][:, :, :], ACT.Copy).then_inc(w_hi_done, 1)
            for c in range(KW):
                act.wait_ge(taken, c + 1)
                f(o_hi[:, c, :], o_raw[:, c, :], ACT.Copy)
                f(o_hi[:, KW + c, :], o_raw[:, KW + c, :], ACT.Copy).then_inc(o_hi_done, 1)
            with act.Fori(0, 8) as i:
                for j in range(2):
                    c = i * 2 + j
                    high_part(c + 1, 1 - j)
                    act.wait_ge(m_sum, c + 1)
                    f(m_hi[:, bass.ds(c, 1), :].rearrange("p a n -> p (a n)"), prod[:, 0, :], ACT.Copy)\
                        .then_inc(m_hi_done, 1)

            def square(c, j):
                n = c - N_OUT
                act.wait_ge(added, n + 1)
                act.wait_ge(summed, n + 1)
                src = h[:, n, :] if isinstance(c, int) else h[:, bass.ds(n, 1), :].rearrange("p a n -> p (a n)")
                f(sq[:, j, :], src, ACT.Square).then_inc(squared, 1)
            with act.Fori(8, 15) as i:
                for j in range(2):
                    c = i * 2 + j
                    high_part(c + 1, 1 - j)
                    square(c, j)
            high_part(31, 1)
            square(30, 0)
            square(31, 1)
            act.wait_ge(summed, 2 + N_OUT)
            f(two(prod[:, 0, :]), sum_sq[:, :, 0:HALF], ACT.Sqrt, bias=eps[:, 0:1], scale=1.0 / D_MODEL).then_inc(rooted, 1)

        @block.vector
        def _(dve):
            v = nc.vector
            link = same_engine(dve, chain)
            link(v.memset(eps[:, :], RMS_EPS))
            dve.sem_inc(multiplied, 2)

            def low_part(c, j):
                dve.wait_ge(w_hi_done, c + 1)
                v.tensor_tensor(w_lo[j][:, :, :], w[j][:, :, :], w_hi[j][:, :, :].bitcast(F32), ALU.subtract)\
                    .then_inc(w_lo_done, 1)
            dve.wait_ge(sig, 1)
            v.tensor_tensor(gT, gT, sg, ALU.mult).then_inc(silu, 1)
            low_part(0, 0)
            dve.wait_ge(silu, 1)
            dve.wait_ge(oa_in, 16)

            def o_low(c):
                dve.wait_ge(o_hi_done, c + 1)
                for k in (c, KW + c):
                    ins = v.tensor_tensor(o_lo[:, k, :], o_raw[:, k, :], o_hi[:, k, :].bitcast(F32), ALU.subtract)
                ins.then_inc(o_lo_done, 1)
            for c in range(KW):
                dve.wait_ge(tps, c + 1)
                p = ps[c % 2]
                v.tensor_tensor(o_raw[:, KW + c, 0:SEQ], p[0][:, 0, :], gT[:, c, 0:SEQ], ALU.mult)
                v.tensor_tensor(o_raw[:, KW + c, SEQ:NT], p[1][:, 0, 0:NS], gT[:, c, SEQ:NT], ALU.mult)
                v.tensor_copy(o_raw[:, c, SEQ:NT], p[1][:, 0, NS:2 * NS]).then_inc(taken, 1)
                if c:
                    o_low(c - 1)
            o_low(KW - 1)
            dve.wait_ge(o_lo_done, KW)
            link.restart()
            with dve.Fori(0, 8) as i:
                for j in range(2):
                    c = i * 2 + j
                    low_part(c + 1, 1 - j)
                    dve.wait_ge(mm_done, c + 2)
                    dve.wait_ge(gates_in[j], i * 16 + 16)
                    for k in range(2):
                        ins = v.tensor_tensor(two(prod[:, k, :]), ps[j][k][:, :, 0:HALF], two(gates[j][:, k, :]), ALU.mult)
                    ins.then_inc(multiplied, 1)
                    dve.wait_ge(multiplied, c + 3)
                    v.tensor_tensor(prod[:, 0, :], prod[:, 0, :], prod[:, 1, :], ALU.add).then_inc(m_sum, 1)
                    dve.wait_ge(m_hi_done, c + 1)
                    one = lambda t: t[:, bass.ds(c, 1), :].rearrange("p a n -> p (a n)")
                    v.tensor_tensor(one(m_lo), prod[:, 0, :], one(m_hi).bitcast(F32), ALU.subtract).then_inc(m_lo_done, 1)
                    dve.wait_ge(m_lo_done, c + 1)

            def add_residual(c, j):
                n = c - N_OUT
                dve.wait_ge(mm_done, c + 2)
                dve.wait_ge(x_in[j], (n - j) * 8 + 16)
                dst = h[:, n, :] if isinstance(c, int) else h[:, bass.ds(n, 1), :].rearrange("p a n -> p (a n)")
                v.tensor_tensor(two(dst), ps[j][0][:, :, 0:HALF], two(xr[:, j, :]), ALU.add).then_inc(added, 1)
            with dve.Fori(8, 15) as i:
                for j in range(2):
                    c = i * 2 + j
                    low_part(c + 1, 1 - j)
                    add_residual(c, j)
            low_part(31, 1)
            add_residual(30, 0)
            add_residual(31, 1)
            dve.wait_ge(rooted, 1)
            link(v.reciprocal(prod[:, 1, :], prod[:, 0, :]))
            dve.wait_ge(consts, 32)
            dve.wait_ge(squared, N_OUT)
            for k in range(N_OUT):
                v.scalar_tensor_tensor(out=h[:, k, :], in0=h[:, k, :], scalar=g_out[:, k:k + 1], in1=prod[:, 1, :],
                                       op0=ALU.mult, op1=ALU.mult).then_inc(scaled, 1)

        @block.tensor
        def _(pe):
            mm = nc.tensor.matmul
            pe.sem_inc(mm_done, 1)
            pe.sem_inc(summed, 2)
            pe.wait_ge(consts, 32)
            pe.wait_ge(ob_in, 16 * 10)
            for c in range(KW):
                if c >= 2:
                    pe.wait_ge(taken, c - 1)
                p = ps[c % 2]
                cols = slice(c * P, (c + 1) * P)
                for t in range(4):
                    nc.tensor.transpose(p[0][:, 0, t * P:(t + 1) * P], ob_tok[:, t, cols], ident[:, :])
                mm(p[1][:, 0, 0:NS], ob_s[:, cols], ident[0:NS, 0:NS], start=True, stop=True)
                mm(p[1][:, 0, NS:2 * NS], oa_s[:, cols], ident[0:NS, 0:NS], start=True, stop=True).then_inc(tps, 1)
            pe.wait_ge(o_lo_done, KW)

            def product(out, j, tiles, x_hi, x_lo):
                parts = ((w_hi[j], x_hi), (w_hi[j], x_lo), (w_lo[j], x_hi))
                for k in tiles:
                    for n, (a, x) in enumerate(parts):
                        for half in range(2):
                            ins = mm(out[:, half, 0:HALF], a[:, k, :], x[:, k, half * HALF:(half + 1) * HALF],
                                     start=(k == tiles[0] and n == 0), stop=(k == tiles[-1] and n == 2))
                return ins
            with pe.Fori(0, 8) as i:
                for j in range(2):
                    c = i * 2 + j
                    pe.wait_ge(w_lo_done, c + 1)
                    pe.wait_ge(multiplied, c + 1)
                    pe.sem_inc(settled, 1)
                    product(ps[j][0], j, range(KW), o_hi, o_lo)
                    product(ps[j][1], j, range(KW, KD), o_hi, o_lo).then_inc(mm_done, 1)
            pe.wait_ge(m_lo_done, N_OUT)
            pe.wait_ge(ones_set, 1)

            def square_sum(n, j):
                pe.wait_ge(squared, n + 1)
                pe.sem_inc(settled, 1)
                for half in range(2):
                    ins = mm(sum_sq[:, half, 0:HALF], ones[:, :], sq[:, j, half * HALF:(half + 1) * HALF],
                             start=(isinstance(n, int) and n == 0), stop=(isinstance(n, int) and n == N_OUT - 1))
                ins.then_inc(summed, 1)

            def y_chunk(c, j):
                pe.wait_ge(w_lo_done, c + 1)
                if isinstance(c, int) and c < N_OUT + 2:
                    pe.wait_ge(multiplied, 2 + N_OUT)
                else:
                    pe.wait_ge(added, c - 1 - N_OUT)
                pe.sem_inc(settled, 1)
                product(ps[j][0], j, range(KD), m_hi, m_lo).then_inc(mm_done, 1)
            y_chunk(16, 0)
            y_chunk(17, 1)
            square_sum(0, 0)
            with pe.Fori(9, 16) as i:
                for j in range(2):
                    c = i * 2 + j
                    y_chunk(c, j)
                    square_sum(c - N_OUT - 1, 1 - j)
            square_sum(N_OUT - 1, 1)



def program(nc, A):
    for phase in (project, rwkv, rwkv_samples, compress, attend_prompt, attend_samples, merge_and_out):
        before = nc.snapshot_sems()
        phase(nc, A)
        nc.clear_and_free_semaphores(nc.allocated_since(before))
        nc.all_engine_barrier()


def laid_out(i):
    w = i["w_in"][0].reshape(KD, P, -1).transpose(1, 0, 2)

    def groups(a, b):
        return w[:, :, a:b].reshape(P, KD, (b - a) // GRP, GRP).transpose(2, 0, 1, 3)
    x = np.concatenate([i["x_prompt"].reshape(SEQ, D_MODEL), i["x_sample"].reshape(NS, D_MODEL)])
    per_channel = lambda v: v.reshape(-1, P).T
    out = {
        "x": x,
        "xT": x.T.reshape(KD, P, NT).transpose(1, 0, 2),
        "g_in": per_channel(i["norm_in"][0]),
        "w_main": groups(0, 30 * GRP),
        "w_tail": w[:, :, 30 * GRP:COL_GATE + N_GATE],
        "w_merge": groups(COL_GATE + N_GATE, COL_GATE + N_GATE + 2 * D_MODEL),
        "par": np.concatenate([i["mu_shift"][0][:4 * A_WIDTH].reshape(4, 8, P).transpose(1, 2, 0)]
                              + [i[n][0].reshape(8, P, 1) for n in ("w0", "a0", "k_k", "k_a", "r_k", "gn_w", "gn_b")]
                              + [np.zeros((8, P, 1), np.float32)], axis=2),
        "wup": np.concatenate([i["w_up"][0], i["a_up"][0]]).reshape(P, 8, P).transpose(1, 0, 2),
        "lora_mu": i["mu_shift"][0][4 * A_WIDTH:].reshape(P, 1),
        "shift": i["state_shift"][0][:, :4 * A_WIDTH].reshape(DEC_B, 4, 8, P).transpose(2, 3, 1, 0),
        "lora_shift": i["state_shift"][0][:, 4 * A_WIDTH:].T,
        "stab": np.stack([np.repeat(i[n][0].reshape(16, HD), DEC_B, axis=0)
                          for n in ("k_k", "k_a", "r_k", "gn_w", "gn_b")], axis=1),
        "state": i["state_rwkv"][0].transpose(1, 0, 2, 3).reshape(P, HD, HD),
        "cmp_rows": i["cache_cmp_kv"][0].reshape(N_POOL, 8, STRIDE * KVW),
        "pos_w": np.broadcast_to(np.stack([i["cmp_pos_k"][0].reshape(2, STRIDE, HD),
                                           i["cmp_pos_v"][0].reshape(2, STRIDE, HD)]).reshape(1, 4, STRIDE, HD),
                                 (P, 4, STRIDE, HD)),
        "w_cmp_k": i["w_cmp_k"][0], "w_cmp_v": i["w_cmp_v"][0],
        "page_table": i["page_table"].reshape(1, DEC_B * N_PAGES),
        "sel_kv": np.concatenate([
            i["cache_sel_kv"][0][:, :, 0].reshape(N_POOL, PAGE, 2, P).transpose(0, 3, 2, 1).reshape(N_POOL, P, 2 * P),
            i["cache_sel_kv"][0][:, :, 1].reshape(N_POOL, PAGE, 2 * P)], axis=2),
        "win_k": i["cache_win_kv"][0][:, :, 0].reshape(DEC_B, WINDOW, 2, P).transpose(0, 2, 3, 1),
        "win_v": i["cache_win_kv"][0][:, :, 1].reshape(DEC_B, 4, P, 2 * P).transpose(0, 2, 1, 3),
        "w_mo": np.concatenate([
            np.concatenate([i["w_pa"][0], i["w_pb"][0]]).reshape(16, P, 16, P).transpose(2, 1, 0, 3),
            i["w_o"][0].reshape(16, P, 16, P).transpose(2, 1, 0, 3)]),
        "g_out": per_channel(i["norm_out"][0] if i["norm_out"].ndim > 1 else i["norm_out"]),
        "win_in": i["cache_win_kv"][0].reshape(DEC_B, WINDOW, KVW),
    }
    return out


def constants():
    f = lambda a: np.asarray(a, np.float32)
    s, t = np.arange(CH)[:, None], np.arange(CH)[None, :]
    same16 = s // 16 == t // 16
    two = lambda m: np.concatenate([m, m])
    head = np.arange(P) // HD
    rmask = np.concatenate([
        np.broadcast_to(np.arange(SEQ) % CH != 0, (P, SEQ)),
        np.concatenate([two(s < t), two(s <= t)], axis=1),
        two((s < t) & same16), two((s < t) & ~same16), two((s > t) & same16), two(s == t), two(s == t)], axis=1)
    slope = np.exp2(-8.0 * np.arange(1, 17, dtype=np.float32) / 16).astype(np.float32).reshape(4, 4)
    q, key = np.arange(P)[:, None], np.arange(SEQ)[None, :]
    dist = q + SEQ - P - key
    bias_p = np.where(dist[None, :, None, :] >= 0, -slope[:, None, :, None] * f(dist)[None, :, None, :], NEG)
    tok = (np.arange(4)[:, None] * P + np.arange(P)[None, :])[:, :, None]
    n = np.arange(32)[None, None, :]
    cdist = tok - (n * STRIDE + 2 * STRIDE - 1)
    cmp_ok = (cdist >= 0) & (n < 31)
    cbias_p = np.where(cmp_ok[None, :, :, None, :], -slope[:, None, None, :, None] * f(cdist)[None, :, :, None, :], NEG)
    cbias_p = cbias_p.transpose(0, 2, 3, 1, 4).reshape(4, P, 16, 32)
    row = np.arange(P)
    rg, rt, rr = row // 16 % 4, row // 4 % 4, row % 4
    pos = PAST + rt[:, None]

    def alibi(key, seen):
        d = pos - key[None, :]
        return np.where(seen(d), -slope[rg, rr][:, None] * f(d), NEG)
    new = PAST + np.arange(DEC_T)
    causal = lambda d: d >= 0
    window = lambda d: (d >= 0) & (d <= WINDOW)
    n128 = np.arange(P)
    bias_s = np.concatenate([alibi(np.arange(PAST), causal), alibi(new, causal),
                             alibi(PAST - WINDOW + np.arange(WINDOW), window), alibi(new, window),
                             np.where(n128 < 127, alibi(n128 * STRIDE + 2 * STRIDE - 1, causal), NEG)], axis=1)
    same_group = (row[:, None] // 4) == (row[None, :] // 4)
    cs, bs = n128[:, None] * STRIDE, np.arange(N_SEL)[None, :] * SEL_BLOCK
    overlap = np.clip(np.minimum(cs + 2 * STRIDE, bs + SEL_BLOCK) - np.maximum(cs, bs), 0, None) / (2 * STRIDE)
    forced = np.isin(np.arange(N_SEL), (0, N_SEL - 2, N_SEL - 1))
    selc = np.broadcast_to(np.stack([~forced, forced * 1e4]), (P, 2, N_SEL))
    jj = np.arange(N_SEL)
    same_head = f(head[:, None] == head[None, :])
    return {
        "ident": np.eye(P, dtype=np.float32),
        "headsum": same_head, "headmean": same_head / HD, "rmask": f(rmask),
        "bias_p": f(bias_p), "cbias_p": f(cbias_p), "cmask": f(np.broadcast_to(cmp_ok.transpose(1, 0, 2), (P, 4, 32))),
        "bias_s": f(bias_s), "gsum": f(same_group), "overlap": f(overlap), "selc": f(selc),
        "lower": f(np.broadcast_to(jj[None, None, :] < jj[None, :, None], (P, N_SEL, N_SEL))),
        "spread": f(np.arange(NS)[:, None, None] == (np.arange(4)[None, :, None] * 2 + (row // HD)[None, None, :]) * 4
                    + rt[None, None, :]),
        "own_head": f((rg * 4 + rr)[:, None] == np.arange(16)[None, :]),
        "gmask": f(rg[:, None] == np.arange(4)[None, :]),
        "shift1": np.eye(P, k=-1, dtype=np.float32),
    }


_SCRATCH = [("uT", (N_ROWS, NT)), ("u_tail", (33, 62 * P)), ("u_tok", (P, 4, 14 * P)),
            ("smp", (16, NS, 6 * HD)), ("oaT", (8, P, SEQ)),
            ("oS", (16, NS, HD)), ("obN", (P, 4, 1024)), ("obS", (4, P, HD)), ("kcT", (DEC_B + 1, 2, P, P)), ("vc", (DEC_B + 1, P, 2, P))]


_OUTS = [
    ("yT", (P, KD, NT)),
    ("p_cmp", (SEQ, KVW)), ("p_sel", (SEQ, KVW)), ("p_win", (SEQ, KVW)),
    ("p_rwkv", (16, HD, HD)), ("p_shift", (1, A_COLS)),
    ("s_cmp", (NS, KVW)), ("s_sel", (NS, KVW)), ("s_win", (DEC_B, WINDOW, KVW)),
    ("s_rwkv", (P, HD, HD)), ("s_shift", (DEC_B, A_COLS)),
]
_RESULTS = ["y_prompt", "y_sample"] + [n for n, _ in _OUTS[1:]]
_SHAPES = [
    (1, SEQ, D_MODEL), (DEC_B, DEC_T, D_MODEL),
    (1, 1, SEQ, 2, 4, HD), (1, 1, SEQ, 2, 4, HD), (1, 1, SEQ, 2, 4, HD), (1, 1, 16, HD, HD), (1, 1, A_COLS),
    (1, DEC_B, DEC_T, 2, 4, HD), (1, DEC_B, DEC_T, 2, 4, HD), (1, DEC_B, WINDOW, 2, 4, HD),
    (1, DEC_B, 16, HD, HD), (1, DEC_B, A_COLS),
]


def kernel(**inputs):
    import concourse.bacc as bacc
    from concourse.bass_utils import run_bass_kernel_spmd

    arrays = laid_out({k: np.asarray(v) for k, v in inputs.items()})
    arrays.update(constants())
    nc = bacc.Bacc("TRN2", target_bir_lowering=False, num_devices=1)
    A = {}
    for name, a in arrays.items():
        arrays[name] = a = np.ascontiguousarray(a)
        A[name] = nc.dram_tensor(f"in_{name}", a.shape, mybir.dt.from_np(a.dtype), kind="ExternalInput").ap()
    for name, shape in _OUTS:
        A[name] = nc.dram_tensor(f"out_{name}", shape, F32, kind="ExternalOutput").ap()
    for name, shape in _SCRATCH:
        A[name] = nc.dram_tensor(f"tmp_{name}", shape, F32, kind="Internal").ap()
    program(nc, A)
    r = run_bass_kernel_spmd(nc, [{f"in_{n}": a for n, a in arrays.items()}], core_ids=[0])
    out = {n: np.asarray(r.results[0][f"out_{n}"]) for n, _ in _OUTS}
    out["s_rwkv"] = out["s_rwkv"].reshape(16, DEC_B, HD, HD).transpose(1, 0, 2, 3)
    y = out["yT"].transpose(2, 1, 0).reshape(NT, D_MODEL)
    out["y_prompt"], out["y_sample"] = y[:SEQ], y[SEQ:]
    return tuple(out[n].reshape(s) for n, s in zip(_RESULTS, _SHAPES))
```

```python
from contextlib import ExitStack

import numpy as np

import concourse.bass as bass
from concourse import mybir

F32 = mybir.dt.float32
F32R = mybir.dt.float32r
I32 = mybir.dt.int32
ALU = mybir.AluOpType
ACT = mybir.ActivationFunctionType
AX = mybir.AxisListType

P = 128
D_MODEL = 2048
KD = D_MODEL // P
SEQ, DEC_B, DEC_T = 512, 8, 4
NS = DEC_B * DEC_T
NT = SEQ + NS
HALF = NT // 2
PAST, PAGE = 2048, 128
N_PAGES = PAST // PAGE
N_POOL = DEC_B * N_PAGES * 5 // 4
A_WIDTH, A_COLS = 1024, 4224
HD = 64
KVW = 512
COL_Q, COL_GB, COL_C, COL_S, COL_W = 4224, 5248, 6272, 6784, 7296
COL_GATE = 7808
N_GATE = 48
ROW_M = COL_GATE + P
N_ROWS = ROW_M + 2 * D_MODEL
GRP = 256
RMS_EPS, GN_EPS = 1e-6, 64e-5
NEG = -1e30
WINDOW = 512
N_SEL, SEL_BLOCK = 33, 64


def same_engine(eng, sem):
    count = [0]

    def link(ins):
        count[0] += 1
        ins.then_inc(sem, 1)
        eng.wait_ge(sem, count[0])
        return ins

    def restart():
        eng.sem_clear(sem)
        count[0] = 0

    link.restart = restart
    return link


def project(nc, A):
    G_A, G_ALL = 31, 47
    FULL0 = 48
    RING = 4
    with ExitStack() as ctx:
        sb = lambda name, shape: ctx.enter_context(nc.sbuf_tensor(name, shape, F32))
        ps = lambda name, shape: ctx.enter_context(nc.psum_tensor(name, shape, F32))
        sem = nc.alloc_semaphore
        sbr = lambda name, shape: ctx.enter_context(nc.sbuf_tensor(name, shape, F32R))
        late = sb("late", [P, KD * NT])
        xT = late[:, :].rearrange("p (k n) -> p k n", n=NT)
        u_tok = late[:, 0:4 * 14 * P].rearrange("p (t n) -> p t n", t=4)
        xh, xl = sbr("xh", [P, KD, NT]), sbr("xl", [P, KD, NT])
        Wh, Wl = ([sbr(f"W{n}{j}", [P, KD, P]) for j in range(2)] for n in "hl")
        g_in = sb("g_in", [P, KD])
        ones = sb("ones", [P, P])
        ident = sb("ident", [P, P])
        W = [sb(f"W{i}", [P, KD, GRP]) for i in range(2)]
        ub = [sb(f"ub{i}", [P, NT]) for i in range(RING)]
        rs, sq = ub[0], ub[2:4]
        u_tail = sb("u_tail", [33, 62 * P])
        acc = [ps(f"acc{i}", [P, 2, 512]) for i in range(2)]
        tps = [ps(f"tps{i}", [P, 512]) for i in range(2)]
        tpf = [ps(f"tpf{i}", [P, 512]) for i in range(2)]
        x_in, g_ld, consts = sem("x_in"), sem("g_ld"), sem("consts")
        w_in = [sem(f"w_in{i}") for i in range(2)]
        squared, ssum, sq_free = sem("squared"), sem("ssum"), sem("sq_free")
        rs_ready, xT_ready, eps_ready = sem("rs_ready"), sem("xT_ready"), sem("eps_ready")
        xh_ready, xl_ready, w_hi, w_lo = sem("xh_ready"), sem("xl_ready"), sem("w_hi"), sem("w_lo")
        proj_done, evac_done = sem("proj_done"), sem("evac_done")
        stored = [sem(f"stored{i}") for i in range(RING)]
        tail_tp, tail_ev, full_tp, full_ev = sem("tail_tp"), sem("tail_ev"), sem("full_tp"), sem("full_ev")
        rs_chain, act_chain, rows_out = sem("rs_chain"), sem("act_chain"), sem("rows_out")
        eps = sb("eps", [P, 1])
        block = ctx.enter_context(nc.Block())

        def w_src(s):
            if isinstance(s, int) and s == G_A - 1:
                return A["w_tail"]
            if isinstance(s, int) and s >= G_A or not isinstance(s, int) and s_merge[0]:
                return A["w_merge"][bass.ds(s - G_A, 1)].rearrange("a p k n -> (a p) k n")
            return A["w_main"][bass.ds(s, 1)].rearrange("a p k n -> (a p) k n")
        s_merge = [False]

        def plan(eng, group):
            for s in (0, 1):
                group(s, s % 2)
            with eng.Fori(1, 12) as i:
                for j in range(2):
                    group(i * 2 + j, j)
            for s in range(24, 32):
                group(s, s % 2)
            s_merge[0] = True
            with eng.Fori(16, 23) as i:
                for j in range(2):
                    group(i * 2 + j, j)
            s_merge[0] = False
            group(46, 0)

        @block.sync
        def _(sp):
            sp.dma_start(g_in[:, :], A["g_in"]).then_inc(g_ld, 16)
            sp.wait_ge(g_ld, 16)
            sp.dma_start(ident[:, :], A["ident"]).then_inc(g_ld, 16)
            for q in range(4):
                sp.dma_start(xT[:, 4 * q:4 * q + 4, :], A["xT"][:, 4 * q:4 * q + 4, :]).then_inc(x_in, 16)
                sp.wait_ge(x_in, 16 * (q + 1))

            def group(s, slot):
                if not isinstance(s, int) or s >= 2:
                    sp.wait_ge(w_lo, s * 2 - 2)
                src = w_src(s)
                dst = W[slot][:, :, 0:176] if isinstance(s, int) and s == G_A - 1 else W[slot][:, :, :]
                sp.dma_start(dst, src).then_inc(w_in[slot], 16)
            plan(sp, group)

        @block.gpsimd
        def _(pool):
            nc.gpsimd.memset(ones[:, :], 1.0).then_inc(consts, 1)
            pool.wait_ge(tail_ev, 62)
            pool.wait_ge(full_ev, 14)
            pool.dma_start(A["u_tail"], u_tail[:, :]).then_inc(rows_out, 16)
            pool.dma_start(A["p_shift"], u_tail[0:1, 0:A_COLS]).then_inc(rows_out, 16)
            for b in range(DEC_B):
                r = 1 + 4 * b + 3
                pool.dma_start(A["s_shift"][b:b + 1, :], u_tail[r:r + 1, 0:A_COLS]).then_inc(rows_out, 16)
            for name, k in (("s_cmp", 49), ("s_sel", 53)):
                pool.dma_start(A[name], u_tail[1:33, k * P:k * P + KVW]).then_inc(rows_out, 16)
            for b in range(DEC_B):
                pool.dma_start(A["s_win"][b, 508:512, :], u_tail[1 + 4 * b:5 + 4 * b, COL_W:COL_W + KVW])\
                    .then_inc(rows_out, 16)
                pool.dma_start(A["s_win"][b, 0:508, :], A["win_in"][b, 4:512, :]).then_inc(rows_out, 16)
            for name, k in (("p_cmp", 1), ("p_sel", 5), ("p_win", 9)):
                pool.dma_start(A[name].rearrange("(t p) c -> p t c", p=P), u_tok[:, :, k * P:k * P + KVW])\
                    .then_inc(rows_out, 16)
            pool.dma_start(A["u_tok"], u_tok[:, :, :]).then_inc(rows_out, 16)
            pool.wait_ge(rows_out, 16 * (1 + 1 + 8 + 2 + 16 + 3 + 1))

        @block.scalar
        def _(act):
            link = same_engine(act, act_chain)
            for k in range(KD):
                if k % 4 == 0:
                    act.wait_ge(x_in, 16 * (k // 4 + 1))
                if k >= 2:
                    act.wait_ge(ssum, k - 1)
                nc.scalar.activation(sq[k % 2][:, :], xT[:, k, :], ACT.Square).then_inc(squared, 1)
            act.wait_ge(ssum, KD)
            act.wait_ge(eps_ready, 1)
            nc.scalar.activation(rs[:, :].rearrange("p (a n) -> p a n", a=2), acc[0][:, :, 0:HALF], ACT.Sqrt,
                                 bias=eps[:, 0:1], scale=1.0 / D_MODEL).then_inc(rs_ready, 1)
            act.wait_ge(w_in[0], 16)
            nc.scalar.activation(Wh[0][:, :, :], W[0][:, :, 0:P], ACT.Copy).then_inc(w_hi, 1)
            for k in range(KD):
                act.wait_ge(xT_ready, k + 1)
                nc.scalar.activation(xh[:, k, :], xT[:, k, :], ACT.Copy).then_inc(xh_ready, 1)

            def high_part(s, slot, j):
                c = s * 2 + j
                if isinstance(c, int) and c == 2 * G_ALL - 1:
                    return
                if j == 1:
                    act.wait_ge(w_in[1 - slot], 16 * ((s + 1) // 2 + 1) if isinstance(s, int)
                                else (s - slot) * 8 + 16 * (slot + 1))
                if not isinstance(c, int) or c >= 1:
                    act.wait_ge(proj_done, c)
                src = W[slot][:, :, P:2 * P] if j == 0 else W[1 - slot][:, :, 0:P]
                nc.scalar.activation(Wh[1 - j][:, :, :], src, ACT.Copy).then_inc(w_hi, 1)

            def group(s, slot):
                for j in range(2):
                    c = s * 2 + j
                    b = 2 * slot + j
                    high_part(s, slot, j)
                    act.wait_ge(proj_done, c + 1)
                    if not isinstance(s, int) or s >= 2:
                        act.wait_ge(stored[b], (c - b) * 4)
                        if isinstance(s, int):
                            act.wait_ge(tail_tp, min(c - 3, 62))
                            if c - 4 >= FULL0:
                                act.wait_ge(full_tp, min(c - 3 - FULL0, 14))
                        elif not s_merge[0]:
                            act.wait_ge(tail_tp, c - 3)
                    merge = s_merge[0] or isinstance(s, int) and s >= G_A
                    m = N_GATE if isinstance(s, int) and s == G_A - 1 and j == 1 else P
                    out = ub[b][0:m, :].rearrange("p (a n) -> p a n", a=2)
                    nc.scalar.activation(out, acc[j][0:m, :, 0:HALF], ACT.Sigmoid if merge else ACT.Copy)\
                        .then_inc(evac_done, 1)
                    act.wait_ge(evac_done, c + 1)
                    if isinstance(c, int):
                        dst = A["uT"][c * P:c * P + m, :]
                    else:
                        dst = A["uT"][bass.ds(c * P, P), :]
                    act.dma_start(dst, ub[b][0:m, :]).then_inc(stored[b], 16)
            plan(act, group)
            for b in range(RING):
                act.wait_ge(stored[b], 16 * (24 if b < 2 else 23))

        @block.vector
        def _(dve):
            link = same_engine(dve, rs_chain)
            nc.vector.memset(eps[:, :], RMS_EPS).then_inc(eps_ready, 1)
            dve.wait_ge(rs_ready, 1)
            link(nc.vector.reciprocal(rs[:, :], rs[:, :]))
            dve.wait_ge(g_ld, 32)
            dve.wait_ge(w_hi, 1)
            nc.vector.tensor_tensor(Wl[0][:, :, :], W[0][:, :, 0:P], Wh[0][:, :, :].bitcast(F32), ALU.subtract)\
                .then_inc(w_lo, 1)
            for k in range(KD + 1):
                if k < KD:
                    nc.vector.scalar_tensor_tensor(out=xT[:, k, :], in0=xT[:, k, :], scalar=g_in[:, k:k + 1],
                                                   in1=rs[:, :], op0=ALU.mult, op1=ALU.mult).then_inc(xT_ready, 1)
                if k:
                    dve.wait_ge(xh_ready, k)
                    nc.vector.tensor_tensor(xl[:, k - 1, :], xT[:, k - 1, :], xh[:, k - 1, :].bitcast(F32),
                                            ALU.subtract).then_inc(xl_ready, 1)
            dve.wait_ge(xl_ready, KD)

            def low_part(s, slot, j):
                c = s * 2 + j
                if isinstance(c, int) and c == 2 * G_ALL - 1:
                    return
                dve.wait_ge(w_hi, c + 2)
                src = W[slot][:, :, P:2 * P] if j == 0 else W[1 - slot][:, :, 0:P]
                nc.vector.tensor_tensor(Wl[1 - j][:, :, :], src, Wh[1 - j][:, :, :].bitcast(F32), ALU.subtract)\
                    .then_inc(w_lo, 1)

            def copies(c):
                dve.wait_ge(tail_tp, c + 1)
                if isinstance(c, int):
                    m = N_GATE if c == 61 else P
                    dst = u_tail[:, c * P:c * P + m]
                else:
                    m = P
                    dst = u_tail[:, bass.ds(c * P, P)]
                slot = c % 2 if isinstance(c, int) else parity[0]
                nc.vector.tensor_copy(dst, tps[slot][0:33, 0:m]).then_inc(tail_ev, 1)
                if isinstance(c, int) and c >= FULL0:
                    f = c - FULL0
                    dve.wait_ge(full_tp, f + 1)
                    nc.vector.tensor_copy(u_tok[:, :, f * P:f * P + m],
                                          tpf[f % 2][:, :].rearrange("p (t n) -> p t n", t=4)[:, :, 0:m])\
                        .then_inc(full_ev, 1)
            parity = [0]

            def group(s, slot):
                for j in range(2):
                    low_part(s, slot, j)
                    c = s * 2 + j - 1
                    parity[0] = (j + 1) % 2
                    if isinstance(s, int) and (c < 0 or c > 61):
                        continue
                    if s_merge[0]:
                        continue
                    copies(c)
            nc.vector.memset(u_tail[:, 61 * P + N_GATE:62 * P], 0.0)
            nc.vector.memset(u_tok[:, :, 13 * P + N_GATE:14 * P], 0.0).then_inc(eps_ready, 1)
            dve.wait_ge(eps_ready, 2)
            plan(dve, group)

        @block.tensor
        def _(pe):
            pe.wait_ge(consts, 1)
            for k in range(KD):
                pe.wait_ge(squared, k + 1)
                for h in range(2):
                    ins = nc.tensor.matmul(acc[0][:, h, 0:HALF], ones[:, :], sq[k % 2][:, h * HALF:(h + 1) * HALF],
                                           start=(k == 0), stop=(k == KD - 1))
                ins.then_inc(ssum, 1)
            pe.wait_ge(xT_ready, 1)

            def copies(c, b):
                m = N_GATE if isinstance(c, int) and c == 61 else P
                pe.wait_ge(evac_done, c + 1)
                if not isinstance(c, int) or c >= 2:
                    pe.wait_ge(tail_ev, c - 1)
                nc.tensor.matmul(tps[b % 2][0:33, 0:m], ub[b][0:m, SEQ - 1:NT], ident[0:m, 0:m],
                                 start=True, stop=True).then_inc(tail_tp, 1)
                if isinstance(c, int) and c >= FULL0:
                    f = c - FULL0
                    if f >= 2:
                        pe.wait_ge(full_ev, f - 1)
                    for t in range(4):
                        ins = nc.tensor.transpose(tpf[f % 2][:, t * P:t * P + m],
                                                  ub[b][0:m, t * P:(t + 1) * P], ident[0:m, 0:m])
                    ins.then_inc(full_tp, 1)

            pe.wait_ge(g_ld, 32)

            def group(s, slot):
                for j in range(2):
                    c = s * 2 + j
                    pe.wait_ge(w_lo, c + 1)
                    if not isinstance(c, int) or c >= 2:
                        pe.wait_ge(evac_done, c - 1)
                    parts = ((Wh[j], xh), (Wh[j], xl), (Wl[j], xh))
                    for k in range(KD):
                        if isinstance(c, int) and c == 0:
                            pe.wait_ge(xl_ready, k + 1)
                        for n, (w, x) in enumerate(parts):
                            for h in range(2):
                                ins = nc.tensor.matmul(acc[j][:, h, 0:HALF], w[:, k, :],
                                                       x[:, k, h * HALF:(h + 1) * HALF],
                                                       start=(k == 0 and n == 0), stop=(k == KD - 1 and n == 2))
                    ins.then_inc(proj_done, 1)
                    p = c - 1
                    if isinstance(p, int) and (p < 0 or p > 61) or s_merge[0]:
                        continue
                    copies(p, (2 * slot + j - 1) % 4)
            plan(pe, group)


CH = 64
NCH = SEQ // CH
DECAY_SCALE = -float(np.exp(-0.5))
R_, K_, V_, G_ = range(4)
STRIDE = 16
POOL_AT, PROJ_AT = 1, 4
(MU, W0, A0, KK_K, KA, RK, GNW, GNB, OMKA) = (0, 4, 5, 6, 7, 8, 9, 10, 11)
N_PAR = 12

HEAD_JOBS = {"zw": (4, 2, "act"), "za": (4, 2, "act"), "tok_a": (5, 1, "act"), "knorm": (4, 1, "dve"),
             "tok_b": (4, 1, "act")}
HEAD_AT = {0: "tok_a", 1: "knorm", 4: "tok_b"}
head_job = lambda name: (name,) + HEAD_JOBS[name]
RWKV_JOBS = [
    ("bk_tok0", 0, 1, "act"), ("bk_tok1", 1, 1, "act"), ("v_tok0", 2, 1, "act"), ("v_tok1", 3, 1, "act"),
    ("bonus", 5, 1, "dve"),
    ("N", 0, 1, "dve"), ("NT", 1, 1, "dve"), ("kk_tok", 2, 1, "act"),
    ("D2", 3, 1, "act"), ("DT2", 0, 1, "dve"),
    ("G0", 1, 1, "dve"), ("G1", 2, 1, "dve"),
    ("D4", 3, 1, "act"), ("DT4", 0, 1, "dve"),
    ("G2", 1, 1, "dve"), ("G3", 2, 1, "dve"),
    ("Q1T", 3, 1, "act"), ("D8", 0, 1, "dve"),
    ("X2", 1, 1, "act"), ("Q2", 2, 1, "act"),
    ("Di", 3, 1, "act"), ("DiT", 0, 1, "dve"),
    ("E", 1, 1, "dve"), ("ET", 2, 1, "dve"), ("E2", 3, 1, "dve"), ("M1T", 0, 1, "dve"),
    head_job("zw"), ("Tt", 1, 1, "act"), ("W1T", 2, 1, "act"), head_job("za"), ("W2a", 3, 1, "act"), ("W2b", 0, 1, "act"),
]
for _n in range(NCH):
    RWKV_JOBS += [(f"U{_n}", 1 + _n % 2, 1, "dve"), (f"O{_n}", 3, 1, "act"), (f"S{_n}", 0, 1, "dve")]
    if _n in HEAD_AT:
        RWKV_JOBS.append(head_job(HEAD_AT[_n]))
RWKV_JOBS += [("S_out", 1, 1, "act"), ("mean", 2, 1, "dve"), ("var", 3, 1, "act")]


def job_counts(jobs):
    n, out, before, last_user = {"act": 0, "dve": 0}, {}, {}, {}
    for at, (name, b0, nb, eng) in enumerate(jobs):
        n[eng] += 1
        out[name, eng] = n[eng]
        out[name] = at + 1
        before[name] = {last_user[b] for b in range(b0, b0 + nb) if b in last_user}
        for b in range(b0, b0 + nb):
            last_user[b] = name
    return out, n, before, set(last_user.values())


def rwkv(nc, A):
    at, per_pair, before, last_users = job_counts(RWKV_JOBS)
    at0, per_head, before0, last_users0 = job_counts([head_job(n) for n in HEAD_JOBS])
    NJ, HJ = len(RWKV_JOBS), len(HEAD_JOBS)
    bank_of = {name: b0 for name, b0, _, _ in RWKV_JOBS}
    engine_of = {name: e for name, _, _, e in RWKV_JOBS}

    def done_count(i, name):
        return at0[name] if i is None else i * NJ + HJ + at[name]

    def out_count(i, name):
        e = engine_of[name]
        return at0[name, e] if i is None else i * per_pair[e] + per_head[e] + at[name, e]
    with ExitStack() as ctx:
        sb = lambda name, shape: ctx.enter_context(nc.sbuf_tensor(name, shape, F32))
        sem = nc.alloc_semaphore
        bank = ctx.enter_context(nc.psum_tensor("rbank", [P, 6, 512], F32))
        in4, d4, u4 = sb("in4", [P, 4, NT]), sb("d4", [P, 4, NT]), sb("u4", [P, 4, NT])
        par, wup, shift = sb("par", [P, N_PAR]), sb("wup", [P, P]), sb("shift", [P, 4, DEC_B])
        lora_in, lora_d, lora = sb("lora_in", [P, NT]), sb("lora_d", [P, NT]), sb("lora", [P, NT])
        lora_mu, lora_shift = sb("lora_mu", [P, 1]), sb("lora_shift", [P, DEC_B])
        sw, a = sb("sw", [P, NT]), sb("a", [P, NT])
        ident, headsum, headmean = (sb(n, [P, P]) for n in ("r_ident", "headsum", "headmean"))
        mask = sb("mask", [P, 512 + P + 5 * CH])
        m_scan, m_G = mask[:, 0:512], mask[:, 512:512 + P]
        m_D, m_F, m_DT, m_I = (mask[:, 512 + P + k * CH:512 + P + (k + 1) * CH] for k in range(4))
        L, cum, cumL = sb("L", [P, SEQ]), sb("cum", [P, SEQ]), sb("cumL", [P, SEQ])
        E1, Ei, E0 = sb("E1", [P, SEQ]), sb("Ei", [P, SEQ]), sb("E0", [P, SEQ])
        rn, kk, k2 = (sb(n, [P, SEQ]) for n in ("rn", "kk", "k2"))
        bonus, kb = lora_in[:, 0:SEQ], lora_d[:, 0:SEQ]
        sqk, rk, osq, osd = (d4[:, f, 0:SEQ] for f in range(4))
        BK, KR, VZ = (sb(n, [P, NCH, 2, CH]) for n in ("BK", "KR", "VZ"))
        tok6 = sb("tok6", [NS, 6, P])
        BKtok, UV = sb("BKtok", [P, NCH, P]), sb("UV", [P, NCH, P])
        G = sb("G", [P, 2, NCH, P])
        mats = {n: sb("m_" + n, [P, NCH, CH]) for n in (
            "D", "ImD", "F", "DT", "kk_tok", "D2", "DT2", "IpDT2", "IpD2", "D4", "DT4", "IpDT4", "IpD8", "Q1T",
            "Q2", "Di", "DiT", "E", "ET", "ImET", "IpE2", "M1T", "Tt", "X2", "W1T")}
        W2 = sb("W2", [CH, 2, NCH, CH])
        S, Sd, S_nat = sb("S", [P, P]), sb("Sd", [P, P]), sb("S_nat", [P, P])
        oT, oc = sb("oT", [P, SEQ]), sb("oc", [P, SEQ])
        gate = sb("gate", [P, SEQ])
        epsg = sb("epsg", [P, 1])

        par_in = sb("par_in", [P, N_PAR])
        gn, chunk_decay = sb("gn", [P, 2]), sb("chunk_decay", [P, NCH])
        table = ctx.enter_context(nc.sbuf_tensor("table", [1, DEC_B * N_PAGES], I32))
        X = [sb(f"rows{i}", [P, STRIDE, P]) for i in range(2)]
        pos_w, weighted = sb("pos_w", [P, 4, STRIDE, HD]), sb("weighted", [P, STRIDE, P])
        C = sb("C", [P, 4, 2 * P])
        pooled, kv = sb("pooled", [P, 4, P]), sb("kv", [P, 4, P])
        shift1, wbd = sb("shift1", [P, P]), sb("wbd", [P, 2, P])
        ps_pool = ctx.enter_context(nc.psum_tensor("ps_pool", [P, 4, P], F32))
        ps_proj = ctx.enter_context(nc.psum_tensor("ps_proj", [P, 4, P], F32))
        table_in, rows_in = sem("c_table"), [sem(f"c_rows{i}") for i in range(2)]
        c_consts, wts, zeroed = sem("c_consts"), sem("c_wts"), sem("c_zeroed")
        x_used, pool_chain, C_ready, pool_mm, pooled_ready, proj_mm, kv_ready, kv_sent = (
            sem("c_" + n) for n in ("x_used", "pool_chain", "C_ready", "pool_mm", "pooled_ready", "proj_mm",
                                    "kv_ready", "kv_sent"))

        loaded, consts = sem("r_loaded"), sem("r_consts")
        pe_jobs, ev_act, ev_dve = sem("pe_jobs"), sem("ev_act"), sem("ev_dve")
        mixed, lora_ready, tanh_done = sem("mixed"), sem("lora_ready"), sem("tanh_done")
        cum_ready, exps_ready, sqk_ready, knorm2 = sem("cum_ready"), sem("exps_ready"), sem("sqk_ready"), sem("knorm2")
        knorm_sqrt, operands, tok_sent, rk_ready = sem("knorm_sqrt"), sem("operands"), sem("tok_sent"), sem("rk_ready")
        centered, sq_ready, std_ready, gate_ready = sem("centered"), sem("sq_ready"), sem("std_ready"), sem("gate_ready")
        o_ready, o_sent, s_ready, s_sent = sem("r_o_ready"), sem("r_o_sent"), sem("r_s_ready"), sem("r_s_sent")
        pair_pe, pair_act, pair_dve, pre = sem("pair_pe"), sem("pair_act"), sem("pair_dve"), sem("r_pre")
        dve_chain, settled = sem("r_dve_chain"), sem("settled")
        settled_dve, settled_sp = sem("r_settled_dve"), sem("r_settled_sp")
        state_ready = sem("state_ready")
        block = ctx.enter_context(nc.Block())

        def taken(eng, i, *names):
            for e, sem_ in (("act", ev_act), ("dve", ev_dve)):
                counts = at0 if i is None else at
                places = [counts[name, e] for name in names if engine_of[name] == e]
                if places:
                    eng.wait_ge(sem_, max(places) if i is None else i * per_pair[e] + per_head[e] + max(places))

        N_CONST = 6

        @block.sync
        def _(sp):
            for dst, src in ((ident, "ident"), (headsum, "headsum"), (headmean, "headmean"), (mask, "rmask"),
                             (lora_mu, "lora_mu"), (lora_shift, "lora_shift")):
                sp.dma_start(dst[:, :], A[src]).then_inc(consts, 16)
            sp.dma_start(lora_in[:, :], A["uT"][4 * A_WIDTH:4 * A_WIDTH + P, :]).then_inc(consts, 16)
            for store, n in ((s_sent, 32), (o_sent, 16)):
                sp.sem_inc(store, n)

            def pair_inputs(i):
                u = A["uT"][0:4 * A_WIDTH, :].rearrange("(f c p) n -> c p f n", f=4, p=P)
                sp.dma_start(in4[:, :, :], u[bass.ds(i, 1)].rearrange("a p f n -> (a p) f n")).then_inc(loaded, 16)
                for dst, src in ((par_in, "par"), (wup, "wup")):
                    sp.dma_start(dst[:, :], A[src][bass.ds(i, 1)].rearrange("a p n -> (a p) n")).then_inc(loaded, 16)
                sp.dma_start(shift[:, :, :], A["shift"][bass.ds(i, 1)].rearrange("a p f n -> (a p) f n"))\
                    .then_inc(loaded, 16)

            def load_rows(b, q):
                sp.sem_inc(settled_sp, 1)
                for p in range(N_PAGES):
                    page = sp.value_load(table[0:1, bass.ds(b * N_PAGES + p, 1)], min_val=0, max_val=N_POOL - 1)
                    sp.dma_start(X[q % 2][8 * p:8 * p + 8, :, :].rearrange("p s c -> p (s c)"),
                                 A["cmp_rows"][bass.ds(page, 1), q].rearrange("a n x -> (a n) x"))\
                        .then_inc(rows_in[q % 2], 16)
            pair_inputs(0)
            sp.dma_start(table[:, :], A["page_table"]).then_inc(table_in, 16)
            for dst, src in ((pos_w, "pos_w"), (shift1, "shift1")):
                sp.dma_start(dst[:], A[src]).then_inc(c_consts, 16)
            sp.wait_ge(table_in, 16)
            load_rows(0, 0)
            load_rows(0, 1)
            sp.wait_ge(zeroed, 1)
            for k, src in enumerate(("w_cmp_k", "w_cmp_v")):
                for h in range(2):
                    sp.dma_start(wbd[h * HD:(h + 1) * HD, k, h * HD:(h + 1) * HD], A[src]).then_inc(wts, 16)

            def sample_inputs(i, p):
                sp.wait_ge(ev_act, out_count(i, "tok_b"))
                for h in range(2):
                    dst = A["smp"][bass.ds(p * 2 + h, 1)].rearrange("a t (f d) -> (a t) f d", f=6)
                    sp.dma_start(dst, tok6[:, :, h * HD:(h + 1) * HD]).then_inc(tok_sent, 16)
            sample_inputs(None, 0)
            pair_inputs(1)

            def pair(i):
                for q in (2, 3):
                    sp.wait_ge(x_used, i * 4 + q - 1)
                    load_rows(i, q)
                last = isinstance(i, int) and i == 7
                if not last:
                    for q in (0, 1):
                        sp.wait_ge(x_used, i * 4 + q + 3)
                        load_rows(i + 1, q)
                    sample_inputs(i, i + 1)
                    pair_inputs(7 if isinstance(i, int) else i + 2)
                sp.wait_ge(ev_act, out_count(i, "S_out"))
                for h in range(2):
                    dst = A["p_rwkv"][bass.ds(i * 2 + h, 1)].rearrange("a t d -> (a t) d")
                    sp.dma_start(dst, S_nat[h * HD:(h + 1) * HD, h * HD:(h + 1) * HD]).then_inc(s_sent, 16)
                sp.wait_ge(o_ready, i + 2)
                sp.dma_start(A["oaT"][bass.ds(i, 1)].rearrange("a p n -> (a p) n"), oT[:, :]).then_inc(o_sent, 16)
            with sp.Fori(0, 6) as i:
                pair(i)
            pair(6)
            pair(7)
            sp.wait_ge(tok_sent, 32 * 8)
            sp.wait_ge(s_sent, 32 * 9)
            sp.wait_ge(o_sent, 16 * 9)

        @block.gpsimd
        def _(pool):
            link = same_engine(pool, pool_chain)
            tt = nc.gpsimd.tensor_tensor
            nc.gpsimd.memset(wbd[:, :, :], 0.0).then_inc(zeroed, 1)
            pool.wait_ge(c_consts, 32)
            with pool.Fori(0, 8) as i:
                pool.wait_ge(pool_mm, i + 1)
                for q in range(4):
                    pool.wait_ge(rows_in[q % 2], i * 32 * N_PAGES + (q // 2 + 1) * 16 * N_PAGES)
                    x = X[q % 2][:, :, :].rearrange("p s (g d) -> p s g d", d=HD)
                    parts = (weighted, X[q % 2])
                    for half, y in enumerate(parts):
                        w = pos_w[:, 2 * (q // 2) + half, :, None, :].to_broadcast([P, STRIDE, 2, HD])
                        last = tt(y[:, :, :].rearrange("p s (g d) -> p s g d", d=HD), x, w, ALU.mult)
                        if half == 0:
                            link(last)
                    link(last)
                    for n in (8, 4, 2):
                        for y in parts:
                            last = tt(y[:, 0:n, :], y[:, 0:n, :], y[:, n:2 * n, :], ALU.add)
                        link(last)
                    for half, y in enumerate(parts):
                        last = tt(C[:, 2 * (q // 2) + half, (q % 2) * P:(q % 2 + 1) * P], y[:, 0, :], y[:, 1, :], ALU.add)
                    last.then_inc(x_used, 1)
                    pool.wait_ge(x_used, i * 4 + q + 1)
                pool.sem_inc(C_ready, 1)
                link.restart()

        @block.vector
        def _(dve):
            link = same_engine(dve, dve_chain)
            v = nc.vector
            tt, ts, stt = v.tensor_tensor, v.tensor_scalar, v.scalar_tensor_tensor
            v.memset(epsg[:, :], GN_EPS)
            v.memset(VZ[:, :, 0, :], 0.0)
            v.memset(L[:, :], 0.0)
            dve.wait_ge(consts, 16 * (N_CONST + 1))

            def shift_mix(x, d, u, mu, prev, f):
                four = lambda t: t[:, :, SEQ:NT].rearrange("p f (b t) -> p f b t", t=DEC_T)
                tt(d[:, :, 1:SEQ], x[:, :, 0:SEQ - 1], x[:, :, 1:SEQ], ALU.subtract)
                ts(d[:, :, 0:1], x[:, :, 0:1], -1.0, None, ALU.mult)
                for k in range(f):
                    xf, df = four(x)[:, k], four(d)[:, k]
                    tt(df[:, :, 1:DEC_T], xf[:, :, 0:DEC_T - 1], xf[:, :, 1:DEC_T], ALU.subtract)
                    last = tt(df[:, :, 0:1], prev[:, k, :, None], xf[:, :, 0:1], ALU.subtract)
                link(last)
                for k in range(f):
                    last = stt(out=u[:, k, :], in0=d[:, k, :], scalar=mu[:, k:k + 1], in1=x[:, k, :],
                               op0=ALU.mult, op1=ALU.add)
                return last
            shift_mix(lora_in[:, None, :], lora_d[:, None, :], lora[:, None, :], lora_mu,
                      lora_shift[:, None, :], 1).then_inc(lora_ready, 1)
            link.restart()
            dve.sem_inc(o_ready, 1)
            by = lambda t: t.rearrange("p (n c) -> p n c", c=CH)

            def mix_pieces(p):
                four = lambda t: t[:, :, SEQ:NT].rearrange("p f (b t) -> p f b t", t=DEC_T)

                def params():
                    dve.wait_ge(loaded, p * 64 + 64)
                    if not isinstance(p, int):
                        link(v.tensor_copy(gn[:, :], par[:, GNW:GNB + 1]))
                    link(v.tensor_copy(par[:, :], par_in[:, :]))
                    link(ts(par[:, OMKA:OMKA + 1], par[:, KA:KA + 1], -1.0, 1.0, ALU.mult, ALU.add))

                def difference(k):
                    tt(d4[:, k, 1:SEQ], in4[:, k, 0:SEQ - 1], in4[:, k, 1:SEQ], ALU.subtract)
                    ts(d4[:, k, 0:1], in4[:, k, 0:1], -1.0, None, ALU.mult)
                    xf, df = four(in4)[:, k], four(d4)[:, k]
                    tt(df[:, :, 1:DEC_T], xf[:, :, 0:DEC_T - 1], xf[:, :, 1:DEC_T], ALU.subtract)
                    link(tt(df[:, :, 0:1], shift[:, k, :, None], xf[:, :, 0:1], ALU.subtract))

                def mix(k):
                    last = stt(out=u4[:, k, :], in0=d4[:, k, :], scalar=par[:, k:k + 1], in1=in4[:, k, :],
                               op0=ALU.mult, op1=ALU.add)
                    if k == 3:
                        last.then_inc(mixed, 1)
                return ([params] + [lambda k=k: difference(k) for k in range(4)]
                        + [lambda k=k: mix(k) for k in range(4)])

            def operand_pieces(i, p):
                def log_decay():
                    dve.wait_ge(ev_act, out_count(i, "za"))
                    link(ts(L[:, :], sw[:, 0:SEQ], DECAY_SCALE, None, ALU.mult))

                def running_sum():
                    link(v.tensor_tensor_scan(out=cum[:, :], data0=m_scan, data1=L[:, :], initial=0.0,
                                              op0=ALU.mult, op1=ALU.add))

                def shifted_sum():
                    tt(cumL[:, :], cum[:, :], L[:, :], ALU.subtract).then_inc(cum_ready, 1)

                def k2_factor():
                    link(ts(kb[:, :], a[:, 0:SEQ], par[:, KA:KA + 1], par[:, OMKA:OMKA + 1], ALU.mult, ALU.add))

                def make_k2():
                    link(tt(k2[:, :], u4[:, K_, 0:SEQ], kb[:, :], ALU.mult))

                def make_rk():
                    stt(out=rk[:, :], in0=u4[:, R_, 0:SEQ], scalar=par[:, RK:RK + 1], in1=k2[:, :],
                        op0=ALU.mult, op1=ALU.mult).then_inc(rk_ready, 1)

                def knorm():
                    dve.wait_ge(pe_jobs, done_count(i, "knorm"))
                    ts(rn[:, :], bank[:, bank_of["knorm"], :], 1e-24, None, ALU.max).then_inc(ev_dve, 1)

                def inverse(q):
                    if q == 0:
                        dve.wait_ge(knorm_sqrt, p + 1)
                    link(v.reciprocal(rn[:, q * P:(q + 1) * P], rn[:, q * P:(q + 1) * P]))

                def make_kk():
                    link(stt(out=kk[:, :], in0=u4[:, K_, 0:SEQ], scalar=par[:, KK_K:KK_K + 1], in1=rn[:, :],
                             op0=ALU.mult, op1=ALU.mult))

                def make_b():
                    link(tt(kb[:, :], kk[:, :], a[:, 0:SEQ], ALU.mult))

                def scaled_b():
                    dve.wait_ge(exps_ready, p * 3 + 3)
                    tt(BK[:, :, 0, :], by(kb), by(Ei[:, :]), ALU.mult)

                def scaled_k2():
                    tt(BK[:, :, 1, :], by(k2[:, :]), by(Ei[:, :]), ALU.mult)
                return [log_decay, running_sum, shifted_sum, knorm, k2_factor, make_k2, make_rk,
                        *[lambda q=q: inverse(q) for q in range(4)], make_kk, make_b, scaled_b, scaled_k2]

            def last_operands():
                v.tensor_copy(VZ[:, :, 1, :], by(u4[:, V_, 0:SEQ]))
                tt(KR[:, :, 0, :], by(kk[:, :]), by(E0[:, :]), ALU.mult)
                tt(KR[:, :, 1, :], by(u4[:, R_, 0:SEQ]), by(E1[:, :]), ALU.mult)
                v.tensor_copy(chunk_decay[:, :], by(E1[:, :])[:, :, CH - 1])
                v.memset(S[:, :], 0.0).then_inc(operands, 1)
            for piece in mix_pieces(0) + operand_pieces(None, 0) + [last_operands]:
                piece()
            dve.wait_ge(operands, 1)
            link.restart()
            with dve.Fori(0, 8) as i:
                def got(name):
                    dve.wait_ge(pe_jobs, done_count(i, name))
                dve.wait_ge(pair_pe, i + 1)
                dve.wait_ge(pair_act, i + 1)
                dve.wait_ge(operands, i + 1)
                mixing, preparing = mix_pieces(i + 1), operand_pieces(i, i + 1)

                def go_on(pieces, n=1):
                    for _ in range(n):
                        if pieces:
                            pieces.pop(0)()
                got("bonus")
                tt(bonus[:, :], bank[:, bank_of["bonus"], :], u4[:, V_, 0:SEQ], ALU.mult).then_inc(ev_dve, 1)
                m = mats
                pb = lambda name: bank[:, bank_of[name], :].rearrange("p (n c) -> p n c", c=CH)
                over = lambda t: t[:, None, :].to_broadcast([P, NCH, CH])
                m = mats
                pb = lambda name: bank[:, bank_of[name], :].rearrange("p (n c) -> p n c", c=CH)
                over = lambda t: t[:, None, :].to_broadcast([P, NCH, CH])
                got("N")
                tt(m["D"][:, :, :], pb("N"), over(m_D), ALU.mult)
                link(tt(m["F"][:, :, :], pb("N"), over(m_F), ALU.mult))
                tt(m["ImD"][:, :, :], over(m_I), m["D"][:, :, :], ALU.subtract).then_inc(ev_dve, 1)
                got("NT")
                tt(m["DT"][:, :, :], pb("NT"), over(m_DT), ALU.mult).then_inc(ev_dve, 1)
                got("DT2")
                tt(m["IpDT2"][:, :, :], pb("DT2"), over(m_I), ALU.add)
                v.tensor_copy(m["DT2"][:, :, :], pb("DT2")).then_inc(ev_dve, 1)
                dve.wait_ge(gate_ready, i + 1)
                link(tt(gate[:, :], gate[:, :], u4[:, G_, 0:SEQ], ALU.mult))
                go_on(mixing, 2)

                def g_quarter(q):
                    got(f"G{q}")
                    src = bank[:, bank_of[f"G{q}"], :].rearrange("p (n c) -> p n c", c=P)
                    tt(G[:, q // 2, 4 * (q % 2):4 * (q % 2) + 4, :], src,
                       m_G[:, None, :].to_broadcast([P, 4, P]), ALU.mult).then_inc(ev_dve, 1)
                g_quarter(0)
                g_quarter(1)
                go_on(mixing, 1)
                got("DT4")
                tt(m["IpDT4"][:, :, :], pb("DT4"), over(m_I), ALU.add)
                v.tensor_copy(m["DT4"][:, :, :], pb("DT4")).then_inc(ev_dve, 1)
                g_quarter(2)
                g_quarter(3)
                go_on(mixing, 1)
                got("D8")
                tt(m["IpD8"][:, :, :], pb("D8"), over(m_I), ALU.add).then_inc(ev_dve, 1)
                go_on(mixing, 2)
                got("DiT")
                v.tensor_copy(m["DiT"][:, :, :], pb("DiT")).then_inc(ev_dve, 1)
                go_on(mixing, 1)
                got("E")
                v.tensor_copy(m["E"][:, :, :], pb("E")).then_inc(ev_dve, 1)
                go_on(mixing, 1)
                got("ET")
                v.tensor_copy(m["ET"][:, :, :], pb("ET"))
                tt(m["ImET"][:, :, :], over(m_I), pb("ET"), ALU.subtract).then_inc(ev_dve, 1)
                got("E2")
                tt(m["IpE2"][:, :, :], pb("E2"), over(m_I), ALU.add).then_inc(ev_dve, 1)
                go_on(mixing, len(mixing))
                got("M1T")
                v.tensor_copy(m["M1T"][:, :, :], pb("M1T")).then_inc(ev_dve, 1)
                for n in range(NCH):
                    last_p = chunk_decay[:, n:n + 1]
                    link(ts(Sd[:, :], S[:, :], last_p, None, ALU.mult))
                    if n:
                        go_on(preparing)
                    dve.wait_ge(ev_act, out_count(i, "W2b"))
                    got(f"U{n}")
                    stt(out=UV[0:CH, n, :].rearrange("p (h i) -> p h i", h=2),
                        in0=bank[0:CH, bank_of[f"U{n}"], 0:P].rearrange("p (h i) -> p h i", h=2), scalar=-1.0,
                        in1=W2[:, :, n, :], op0=ALU.mult, op1=ALU.subtract).then_inc(ev_dve, 1)
                    go_on(preparing)
                    got(f"S{n}")
                    for h, hp in enumerate((slice(0, CH), slice(CH, P))):
                        last = stt(out=S[hp, h * CH:(h + 1) * CH], in0=bank[hp, bank_of[f"S{n}"], 0:CH],
                                   scalar=last_p[hp], in1=Sd[hp, h * CH:(h + 1) * CH], op0=ALU.mult, op1=ALU.add)
                    last.then_inc(ev_dve, 1)
                    dve.wait_ge(ev_dve, out_count(i, f"S{n}"))
                go_on(preparing, len(preparing))
                got("S_out")
                last_operands()
                got("mean")
                tt(oc[:, :], oT[:, :], bank[:, bank_of["mean"], :], ALU.subtract).then_inc(ev_dve, 1)
                dve.wait_ge(std_ready, i + 1)
                link(v.reciprocal(osd[:, :], osd[:, :]))
                link(stt(out=oc[:, :], in0=oc[:, :], scalar=gn[:, 0:1], in1=osd[:, :],
                         op0=ALU.mult, op1=ALU.mult))
                link(stt(out=oc[:, :], in0=oc[:, :], scalar=gn[:, 1:2], in1=bonus[:, :],
                         op0=ALU.add, op1=ALU.add))
                tt(oT[:, :], oc[:, :], gate[:, :], ALU.mult).then_inc(o_ready, 1)
                dve.wait_ge(o_ready, i + 2)
                dve.sem_inc(settled_dve, 1)
                link.restart()

        @block.scalar
        def _(act):
            act.wait_ge(lora_ready, 1)
            nc.scalar.activation(lora[0:HD, :], lora[0:HD, :], ACT.Tanh).then_inc(tanh_done, 1)
            f = nc.scalar.activation
            act.wait_ge(tanh_done, 1)
            act.sem_inc(pair_act, 1)
            act.sem_inc(kv_sent, 32)
            act.sem_inc(kv_ready, 1)
            two = lambda t: t[:, :].rearrange("p (a n) -> p a n", a=2)

            def out_of(i, name, dst, src=None, func=ACT.Copy, **kw):
                act.wait_ge(pe_jobs, done_count(i, name))
                f(dst, bank[:, bank_of[name], :] if src is None else src, func, **kw).then_inc(ev_act, 1)

            def head_zw(i, p):
                act.wait_ge(mixed, p + 1)
                f(sqk, u4[:, K_, 0:SEQ], ACT.Square, scale=par[:, KK_K:KK_K + 1]).then_inc(sqk_ready, 1)
                out_of(i, "zw", two(sw), bank[:, 4:6, 0:HALF], ACT.Sigmoid, bias=par[:, W0:W0 + 1])

            def head_za(i):
                out_of(i, "za", two(a), bank[:, 4:6, 0:HALF], ACT.Sigmoid, bias=par[:, A0:A0 + 1])

            def head_tok_a(i):
                if i is not None:
                    act.wait_ge(tok_sent, i * 32 + 32)
                out_of(i, "tok_a", tok6[:, 0:4, :], bank[0:NS, bank_of["tok_a"], :].rearrange("p (f d) -> p f d", f=4))

            def head_exps(p):
                act.wait_ge(cum_ready, p + 1)
                f(E1[:, :], cum[:, :], ACT.Exp).then_inc(exps_ready, 1)
                f(Ei[:, :], cum[:, :], ACT.Exp, scale=-1.0).then_inc(exps_ready, 1)
                f(E0[:, :], cumL[:, :], ACT.Exp).then_inc(exps_ready, 1)

            def head_sqrt(i, p):
                act.wait_ge(ev_dve, out_count(i, "knorm"))
                f(rn[:, :], rn[:, :], ACT.Sqrt).then_inc(knorm_sqrt, 1)

            def head_tok_b(i):
                out_of(i, "tok_b", tok6[:, 4:6, :],
                       bank[0:NS, bank_of["tok_b"], 0:2 * P].rearrange("p (f d) -> p f d", f=2))
            head_zw(None, 0)
            head_za(None)
            head_tok_a(None)
            head_exps(0)
            head_sqrt(None, 0)
            head_tok_b(None)
            with act.Fori(0, 8) as i:
                def out(name, *args):
                    out_of(i, name, *args)
                act.wait_ge(pair_pe, i + 1)
                act.wait_ge(operands, i + 1)
                m = mats
                pb = lambda name: bank[:, bank_of[name], :].rearrange("p (n c) -> p n c", c=CH)
                pw = lambda name: bank[:, bank_of[name], :].rearrange("p (n c) -> p n c", c=P)
                out("bk_tok0", BKtok[:, 0:4, :], pw("bk_tok0"))
                out("bk_tok1", BKtok[:, 4:8, :], pw("bk_tok1"))
                out("v_tok0", UV[CH:P, 0:4, :], pw("v_tok0")[CH:P])
                out("v_tok1", UV[CH:P, 4:8, :], pw("v_tok1")[CH:P])
                out("kk_tok", m["kk_tok"][:, :, :], pb("kk_tok"))
                out("D2", m["D2"][:, :, :], pb("D2"))
                act.wait_ge(o_ready, i + 1)
                f(gate[:, :], u4[:, G_, 0:SEQ], ACT.Sigmoid).then_inc(gate_ready, 1)
                for name in ("D4", "Q1T", "X2", "Q2", "Di"):
                    out(name, m[name][:, :, :], pb(name))
                head_zw(i, i + 1)
                for name in ("Tt", "W1T"):
                    out(name, m[name][:, :, :], pb(name))
                head_za(i)
                for h, name in enumerate(("W2a", "W2b")):
                    out(name, W2[:, h, :, :], pb(name)[0:CH])
                act.wait_ge(o_sent, i * 16 + 16)
                for n in range(NCH):
                    out(f"O{n}", oT[:, n * CH:(n + 1) * CH], bank[:, bank_of[f"O{n}"], 0:CH])
                    if n == 0:
                        head_tok_a(i)
                    if n == 2:
                        head_exps(i + 1)
                    if n == 3:
                        head_sqrt(i, i + 1)
                    if n == 4:
                        head_tok_b(i)
                    if n == POOL_AT:
                        act.wait_ge(pool_mm, i + 2)
                        f(pooled[:, :, :], ps_pool[:, :, :], ACT.Copy).then_inc(pooled_ready, 1)
                    if n == PROJ_AT:
                        act.wait_ge(proj_mm, i + 1)
                        act.wait_ge(kv_sent, i * 32 + 32)
                        f(kv[:, :, :], ps_proj[:, :, :], ACT.Copy).then_inc(kv_ready, 1)
                        act.wait_ge(kv_ready, i + 2)
                        for name, half in (("kcT", slice(0, 2)), ("vc", slice(2, 4))):
                            act.dma_start(A[name][bass.ds(i, 1)].rearrange("a k p n -> (a p) k n" if name == "kcT"
                                                                           else "a p k n -> (a p) k n"),
                                          kv[:, half, :]).then_inc(kv_sent, 16)
                act.wait_ge(s_sent, i * 32 + 32)
                out("S_out", S_nat[:, :], bank[:, bank_of["S_out"], 0:P])
                act.wait_ge(ev_dve, out_count(i, "mean"))
                f(osq, oc[:, :], ACT.Square).then_inc(sq_ready, 1)
                act.wait_ge(pe_jobs, done_count(i, "var"))
                f(osd, bank[:, bank_of["var"], :], ACT.Sqrt, bias=epsg[:, 0:1]).then_inc(std_ready, 1)
                act.wait_ge(std_ready, i + 1)
                act.sem_inc(ev_act, 1)
                act.sem_inc(pair_act, 1)
            act.wait_ge(kv_sent, 32 * (DEC_B + 1))

        @block.tensor
        def _(pe):
            mm = nc.tensor.matmul
            pe.wait_ge(consts, 16 * (N_CONST + 1))
            pe.wait_ge(tanh_done, 1)
            pe.sem_inc(pair_pe, 1)
            pe.sem_inc(pool_mm, 1)

            def settle():
                pe.sem_inc(settled, 1)

            def done(ins):
                ins.then_inc(pe_jobs, 1)

            def head(name, i, p):
                needs = (before0 if i is None else before)[name]
                if needs:
                    taken(pe, i, *needs)
                if name == "zw":
                    pe.wait_ge(mixed, p + 1)
                if name == "knorm":
                    pe.wait_ge(sqk_ready, p + 1)
                if name == "tok_b":
                    taken(pe, i, "zw", "za")
                settle()
                if name in ("zw", "za"):
                    rows = slice(0, HD) if name == "zw" else slice(HD, P)
                    for h in range(2):
                        ins = mm(bank[:, bank_of[name] + h, 0:HALF], wup[rows, :],
                                 lora[rows, h * HALF:(h + 1) * HALF], start=True, stop=True)
                elif name == "knorm":
                    ins = mm(bank[:, bank_of[name], :], headsum[:, :], sqk, start=True, stop=True)
                else:
                    parts = [u4[:, f, SEQ:NT] for f in range(4)] if name == "tok_a" else [sw[:, SEQ:NT], a[:, SEQ:NT]]
                    for f, t in enumerate(parts):
                        ins = mm(bank[0:NS, bank_of[name], f * P:(f + 1) * P], t, ident[:, :], start=True, stop=True)
                done(ins)
            for name in HEAD_JOBS:
                head(name, None, 0)
            taken(pe, None, *last_users0)
            pe.wait_ge(c_consts, 32)
            pe.wait_ge(wts, 64)
            with pe.Fori(0, 8) as i:
                def job(name, *needs):
                    taken(pe, i, *before[name], *needs)
                    settle()
                pe.wait_ge(operands, i + 1)
                for name, src, n0 in (("bk_tok0", BK, 0), ("bk_tok1", BK, 4), ("v_tok0", VZ, 0), ("v_tok1", VZ, 4)):
                    job(name)
                    for n in range(4):
                        ins = mm(bank[:, bank_of[name], n * P:(n + 1) * P],
                                 src[:, n0 + n, :, :].rearrange("p a c -> p (a c)"), ident[:, :],
                                 start=True, stop=True)
                    done(ins)
                pe.wait_ge(rk_ready, i + 1)
                job("bonus")
                done(mm(bank[:, bank_of["bonus"], :], headsum[:, :], rk, start=True, stop=True))
                H = (slice(0, CH), slice(CH, P))

                def both(name, lhsT, rhs, *needs):
                    job(name, *needs)
                    for n in range(NCH):
                        for hp in H:
                            ins = mm(bank[hp, bank_of[name], n * CH:(n + 1) * CH], lhsT(hp, n), rhs(hp, n),
                                     start=True, stop=True)
                    done(ins)
                B = lambda hp, n: BK[hp, n, 0, :]
                KK = lambda hp, n: KR[hp, n, 0, :]
                M = lambda name: (lambda hp, n: mats[name][hp, n, :])
                both("N", B, KK)
                both("NT", KK, B)
                both("kk_tok", KK, lambda hp, n: ident[hp, hp])
                both("D2", M("DT"), M("D"), "N", "NT")
                both("DT2", M("D"), M("DT"))

                def g_quarter(q):
                    job(f"G{q}")
                    hp = H[q // 2]
                    for n in range(4):
                        nn = 4 * (q % 2) + n
                        ins = mm(bank[:, bank_of[f"G{q}"], n * P:(n + 1) * P],
                                 BK[hp, nn, :, :].rearrange("p a c -> p (a c)"),
                                 KR[hp, nn, :, :].rearrange("p a c -> p (a c)"), start=True, stop=True)
                    done(ins)
                g_quarter(0)
                g_quarter(1)
                both("D4", M("DT2"), M("D2"), "D2", "DT2")
                both("DT4", M("D2"), M("DT2"))
                g_quarter(2)
                g_quarter(3)
                both("Q1T", M("ImD"), M("IpDT2"))
                both("D8", M("DT4"), M("D4"), "D4", "DT4")
                job("X2", "G0", "G1", "G2", "G3", "v_tok0", "v_tok1")
                for n in range(NCH):
                    for h, hp in enumerate(H):
                        ins = mm(bank[hp, bank_of["X2"], n * CH:(n + 1) * CH], G[CH:P, h, n, 0:CH],
                                 UV[CH:P, n, h * CH:(h + 1) * CH], start=True, stop=True)
                done(ins)
                both("Q2", M("IpDT4"), M("IpD8"), "D8")
                both("Di", M("Q1T"), M("Q2"), "Q1T", "Q2")
                both("DiT", M("Q2"), M("Q1T"))
                both("E", M("DiT"), M("F"), "DiT")
                both("ET", M("F"), M("DiT"))
                both("E2", M("ET"), M("E"), "E", "ET")
                both("M1T", M("IpE2"), M("ImET"), "E2")
                head("zw", i, i + 1)
                both("Tt", M("M1T"), M("Di"), "M1T", "Di")
                both("W1T", M("kk_tok"), M("Tt"), "Tt", "kk_tok", "X2")
                head("za", i, i + 1)
                for h, name in enumerate(("W2a", "W2b")):
                    job(name)
                    for n in range(NCH):
                        ins = mm(bank[0:CH, bank_of[name], n * CH:(n + 1) * CH], mats["Tt"][H[h], n, :],
                                 mats["X2"][H[h], n, :], start=True, stop=True)
                    done(ins)
                for n in range(NCH):
                    job(f"U{n}", "W1T", *([f"S{n - 1}"] if n else []))
                    done(mm(bank[0:CH, bank_of[f"U{n}"], 0:P], mats["W1T"][:, n, :], S[:, :], start=True, stop=True))
                    job(f"O{n}", f"U{n}", "bk_tok1")
                    mm(bank[:, bank_of[f"O{n}"], 0:CH], S[:, :], KR[:, n, 1, :], start=True, stop=False)
                    for h, hp in enumerate(H):
                        ins = mm(bank[hp, bank_of[f"O{n}"], 0:CH], UV[:, n, h * CH:(h + 1) * CH],
                                 G[:, h, n, CH:P], start=False, stop=True)
                    done(ins)
                    job(f"S{n}")
                    for h, hp in enumerate(H):
                        ins = mm(bank[hp, bank_of[f"S{n}"], 0:CH], BKtok[:, n, h * CH:(h + 1) * CH],
                                 UV[:, n, h * CH:(h + 1) * CH], start=True, stop=True)
                    done(ins)
                    if n in HEAD_AT:
                        head(HEAD_AT[n], i, i + 1)
                    if n == POOL_AT:
                        pe.wait_ge(C_ready, i + 1)
                        settle()
                        for kp in range(4):
                            c = slice(kp % 2 * P, kp % 2 * P + P)
                            mm(ps_pool[:, kp, :], C[:, kp // 2 * 2, c], ident[:, :], start=True, stop=False)
                            ins = mm(ps_pool[:, kp, :], C[:, kp // 2 * 2 + 1, c], shift1[:, :], start=False, stop=True)
                        ins.then_inc(pool_mm, 1)
                    if n == PROJ_AT:
                        pe.wait_ge(pooled_ready, i + 1)
                        pe.wait_ge(kv_ready, i + 1)
                        settle()
                        for kp in range(2):
                            mm(ps_proj[:, kp, :], wbd[:, 0, :], pooled[:, kp, :], start=True, stop=True)
                        for kp in range(2, 4):
                            ins = mm(ps_proj[:, kp, :], pooled[:, kp, :], wbd[:, 1, :], start=True, stop=True)
                        ins.then_inc(proj_mm, 1)
                job("S_out", f"S{NCH - 1}", f"O{NCH - 1}")
                done(mm(bank[:, bank_of["S_out"], 0:P], S[:, :], ident[:, :], start=True, stop=True))
                job("mean")
                done(mm(bank[:, bank_of["mean"], :], headmean[:, :], oT[:, :], start=True, stop=True))
                pe.wait_ge(sq_ready, i + 1)
                job("var")
                done(mm(bank[:, bank_of["var"], :], headmean[:, :], osq[:, :], start=True, stop=True))
                taken(pe, i, *last_users, "S_out", "mean", "var", f"S{NCH - 1}")
                pe.sem_inc(pair_pe, 1)


def rwkv_samples(nc, A, ctx):
    sb = lambda name, shape: ctx.enter_context(nc.sbuf_tensor(name, shape, F32))
    sem = nc.alloc_semaphore
    X = sb("sx", [P, DEC_T, 6, HD])
    tab = sb("stab", [P, 5, HD])
    S, Sw, prod = (sb(n, [P, HD, HD]) for n in ("sS", "sSw", "s_prod"))
    w, kraw, sq, kk, b, k2, rk, o, oc, gate = (
        sb("s_" + n, [P, DEC_T, HD]) for n in ("w", "kraw", "sq", "kk", "b", "k2", "rk", "o", "oc", "gate"))
    ss, mean, var, bonus = (sb("s_" + n, [P, DEC_T]) for n in ("ss", "mean", "var", "bonus"))
    sa, eps = sb("s_sa", [P, HD]), sb("s_eps", [P, 1])
    loaded, chain, act_done, ready = sem("s_loaded"), sem("s_chain"), sem("s_act_done"), sem("s_ready_in")
    norm_in, var_in, pool_chain, stepped = sem("s_norm_in"), sem("s_var_in"), sem("s_pool_chain"), sem("s_stepped")
    o_done, sent = sem("s_o_done"), sem("s_sent")
    last_dim = lambda t, i: t[:, i, None, :].to_broadcast([P, HD, HD])
    over_j = lambda t: t[:, :, None].to_broadcast([P, HD, HD])
    over_d = lambda t: t[:, :, None].to_broadcast([P, DEC_T, HD])
    over_t = lambda k: tab[:, None, k, :].to_broadcast([P, DEC_T, HD])
    r, k, v, g, sw, a = (X[:, :, f, :] for f in range(6))

    def load(eng):
        eng.dma_start(X[:, :, :, :], A["smp"].rearrange("h (b t) f -> (h b) (t f)", t=DEC_T)
                      .rearrange("p (t f d) -> p t f d", t=DEC_T, f=6)).then_inc(loaded, 16)
        eng.dma_start(tab[:, :, :], A["stab"]).then_inc(loaded, 16)
        eng.dma_start(S[:, :, :], A["state"]).then_inc(loaded, 16)

    def store(eng):
        eng.wait_ge(stepped, 1)
        eng.dma_start(A["s_rwkv"], S[:, :, :]).then_inc(sent, 16)
        eng.wait_ge(o_done, 1)
        eng.dma_start(A["oS"].rearrange("h n d -> (h n d)").rearrange("(p n) -> p n", p=P),
                      o[:, :, :].rearrange("p t d -> p (t d)")).then_inc(sent, 16)
        eng.wait_ge(sent, 32)

    def act_before(act):
        f = nc.scalar.activation
        act.wait_ge(loaded, 48)
        f(w[:, :, :], sw, ACT.Exp, scale=DECAY_SCALE).then_inc(act_done, 1)
        f(gate[:, :, :], g, ACT.Sigmoid).then_inc(act_done, 1)
        act.wait_ge(norm_in, 1)
        f(ss[:, :], ss[:, :], ACT.Sqrt).then_inc(act_done, 1)

    def act_after(act):
        act.wait_ge(var_in, 1)
        nc.scalar.activation(var[:, :], var[:, :], ACT.Sqrt, bias=eps[:, 0:1], scale=1.0 / HD).then_inc(act_done, 1)

    def pool_steps(pool):
        tt = nc.gpsimd.tensor_tensor
        link = same_engine(pool, pool_chain)
        pool.wait_ge(ready, 1)
        pool.wait_ge(act_done, 2)

        def row_sums(out):
            n = HD // 2
            while n > 1:
                link(tt(prod[:, :, 0:n], prod[:, :, 0:n], prod[:, :, n:2 * n], ALU.add))
                n //= 2
            return tt(out, prod[:, :, 0], prod[:, :, 1], ALU.add)
        for t in range(DEC_T):
            tt(Sw[:, :, :], S[:, :, :], last_dim(w, t), ALU.mult)
            link(tt(prod[:, :, :], S[:, :, :], last_dim(kk, t), ALU.mult))
            link(row_sums(sa[:, :]))
            link(tt(prod[:, :, :], over_j(v[:, t, :]), last_dim(k2, t), ALU.mult))
            link(tt(Sw[:, :, :], Sw[:, :, :], prod[:, :, :], ALU.add))
            link(tt(prod[:, :, :], over_j(sa), last_dim(b, t), ALU.mult))
            link(tt(S[:, :, :], Sw[:, :, :], prod[:, :, :], ALU.subtract))
            link(tt(prod[:, :, :], S[:, :, :], last_dim(X[:, t], 0), ALU.mult))
            last = row_sums(o[:, t, :])
            if t < DEC_T - 1:
                link(last)
        last.then_inc(stepped, 1)

    vv = nc.vector
    tt, ts, stt = vv.tensor_tensor, vv.tensor_scalar, vv.scalar_tensor_tensor
    red = lambda out, x: vv.reduce_sum(out, x, axis=AX.X)

    def dve_before(dve):
        link = same_engine(dve, chain)
        vv.memset(eps[:, :], GN_EPS)
        dve.wait_ge(loaded, 48)
        link(tt(kraw[:, :, :], k, over_t(0), ALU.mult))
        link(tt(sq[:, :, :], kraw[:, :, :], kraw[:, :, :], ALU.mult))
        link(red(ss[:, :], sq[:, :, :]))
        ts(ss[:, :], ss[:, :], 1e-24, None, ALU.max).then_inc(norm_in, 1)
        link(ts(k2[:, :, :], a, 1.0, None, ALU.subtract))
        link(tt(k2[:, :, :], k2[:, :, :], over_t(1), ALU.mult))
        link(stt(out=k2[:, :, :], in0=k2[:, :, :], scalar=1.0, in1=k, op0=ALU.add, op1=ALU.mult))
        dve.wait_ge(act_done, 3)
        link(vv.reciprocal(ss[:, :], ss[:, :]))
        link(tt(kk[:, :, :], kraw[:, :, :], over_d(ss), ALU.mult))
        tt(b[:, :, :], kk[:, :, :], a, ALU.mult).then_inc(ready, 1)
        link(tt(rk[:, :, :], r, k2[:, :, :], ALU.mult))
        link(tt(rk[:, :, :], rk[:, :, :], over_t(2), ALU.mult))
        link(red(bonus[:, :], rk[:, :, :]))
        link(tt(rk[:, :, :], v, over_d(bonus), ALU.mult))
        link(tt(gate[:, :, :], gate[:, :, :], g, ALU.mult))
        link.restart()

    def dve_after(dve):
        link = same_engine(dve, chain)
        dve.wait_ge(stepped, 1)
        link(red(mean[:, :], o[:, :, :]))
        link(ts(mean[:, :], mean[:, :], 1.0 / HD, None, ALU.mult))
        link(tt(oc[:, :, :], o[:, :, :], over_d(mean), ALU.subtract))
        link(tt(sq[:, :, :], oc[:, :, :], oc[:, :, :], ALU.mult))
        red(var[:, :], sq[:, :, :]).then_inc(var_in, 1)
        dve.wait_ge(act_done, 4)
        link(vv.reciprocal(var[:, :], var[:, :]))
        link(tt(oc[:, :, :], oc[:, :, :], over_d(var), ALU.mult))
        link(tt(oc[:, :, :], oc[:, :, :], over_t(3), ALU.mult))
        link(tt(oc[:, :, :], oc[:, :, :], over_t(4), ALU.add))
        link(tt(oc[:, :, :], oc[:, :, :], rk[:, :, :], ALU.add))
        tt(o[:, :, :], oc[:, :, :], gate[:, :, :], ALU.mult).then_inc(o_done, 1)
    return load, store, act_before, act_after, pool_steps, dve_before, dve_after


def compress_prompt(nc, A):
    N = SEQ // STRIDE
    with ExitStack() as ctx:
        sb = lambda name, shape: ctx.enter_context(nc.sbuf_tensor(name, shape, F32))
        sem = nc.alloc_semaphore
        X, weighted = sb("cp_rows", [P, STRIDE, P]), [sb(f"cp_weighted{h}", [P, STRIDE, P]) for h in range(2)]
        pos_q, C = sb("cp_pos_q", [P, 2, STRIDE, HD]), sb("cp_C", [P, 2, P])
        pooled, kT, v = sb("cp_pooled", [P, 4, N]), sb("cp_kT", [P, 2, P]), sb("cp_v", [P, 2, P])
        ident, shift, wbd = sb("cp_ident", [P, P]), sb("cp_shift", [P, P]), sb("cp_wbd", [P, 2, P])
        ps_pool = [ctx.enter_context(nc.psum_tensor(f"cp_ps{q}", [P, 512], F32)) for q in range(4)]
        ps_k, ps_v = (ctx.enter_context(nc.psum_tensor("cp_ps_" + n, [P, 512], F32)) for n in "kv")
        rows_in, consts, zeroed, wts = sem("cp_rows_in"), sem("cp_consts"), sem("cp_zeroed"), sem("cp_wts")
        multiplied, C_ready, pool_mm, pooled_ready, proj_mm, kv_ready, kv_sent = (
            sem("cp_" + n) for n in ("multiplied", "C_ready", "pool_mm", "pooled_ready", "proj_mm", "kv_ready", "kv_sent"))
        block = ctx.enter_context(nc.Block())
        rows = lambda q: slice(N * q, N * q + N)

        @block.sync
        def _(sp):
            for q in range(4):
                c = P + q * P
                for t in range(4):
                    src = A["u_tok"][:, t, c:c + P].rearrange("(n s) c -> n s c", s=STRIDE)
                    sp.dma_start(X[N * q + 8 * t:N * q + 8 * t + 8, :, :], src).then_inc(rows_in, 16)

        @block.scalar
        def _(act):
            for dst, src in ((pos_q, "pos_q"), (ident, "ident"), (shift, "shift1")):
                act.dma_start(dst[:], A[src]).then_inc(consts, 16)
            act.wait_ge(zeroed, 1)
            for k, src in enumerate(("w_cmp_k", "w_cmp_v")):
                for h in range(2):
                    act.dma_start(wbd[h * HD:(h + 1) * HD, k, h * HD:(h + 1) * HD], A[src]).then_inc(wts, 16)
            act.wait_ge(pool_mm, 1)
            for q in range(4):
                ins = nc.scalar.activation(pooled[:, q, :], ps_pool[q][:, 0:N], ACT.Copy)
            ins.then_inc(pooled_ready, 1)
            act.wait_ge(proj_mm, 1)
            act.wait_ge(zeroed, 3)
            nc.scalar.activation(kT[:, :, 0:N], ps_k[:, 0:2 * N].rearrange("p (k n) -> p k n", k=2), ACT.Copy)
            nc.scalar.activation(v[0:N, :, :], ps_v[0:N, 0:2 * P].rearrange("p (k n) -> p k n", k=2), ACT.Copy)\
                .then_inc(kv_ready, 1)
            act.wait_ge(kv_ready, 1)
            act.dma_start(A["kcT"][DEC_B].rearrange("k p n -> p k n"), kT[:, :, :]).then_inc(kv_sent, 16)
            act.dma_start(A["vc"][DEC_B], v[:, :, :]).then_inc(kv_sent, 16)
            act.wait_ge(kv_sent, 32)

        @block.gpsimd
        def _(pool):
            nc.gpsimd.memset(wbd[:, :, :], 0.0).then_inc(zeroed, 1)
            pool.wait_ge(zeroed, 1)
            nc.gpsimd.memset(kT[:, :, :], 0.0).then_inc(zeroed, 1)
            nc.gpsimd.memset(v[:, :, :], 0.0).then_inc(zeroed, 1)

        @block.vector
        def _(dve):
            dve.wait_ge(rows_in, 16 * 16)
            dve.wait_ge(consts, 48)
            for half in range(2):
                w = pos_q[:, half, :, None, :].to_broadcast([P, STRIDE, 2, HD])
                nc.vector.tensor_tensor(weighted[half][:, :, :].rearrange("p s (g d) -> p s g d", d=HD),
                                        X[:, :, :].rearrange("p s (g d) -> p s g d", d=HD), w, ALU.mult)\
                    .then_inc(multiplied, 1)
            for half in range(2):
                dve.wait_ge(multiplied, half + 1)
                ins = nc.vector.reduce_sum(C[:, half, :], weighted[half][:, :, :].rearrange("p s c -> p c s"), axis=AX.X)
            ins.then_inc(C_ready, 1)

        @block.tensor
        def _(pe):
            mm = nc.tensor.matmul
            pe.wait_ge(wts, 64)
            pe.wait_ge(C_ready, 1)
            for q in range(4):
                r = rows(q)
                mm(ps_pool[q][:, 0:N], C[r, 0, :], ident[r, r], start=True, stop=False)
                ins = mm(ps_pool[q][:, 0:N], C[r, 1, :], shift[r, r], start=False, stop=True)
            ins.then_inc(pool_mm, 1)
            pe.wait_ge(pooled_ready, 1)
            for gp in range(2):
                mm(ps_k[:, gp * N:(gp + 1) * N], wbd[:, 0, :], pooled[:, gp, :], start=True, stop=True)
            for gp in range(2):
                ins = mm(ps_v[0:N, gp * P:(gp + 1) * P], pooled[:, 2 + gp, :], wbd[:, 1, :], start=True, stop=True)
            ins.then_inc(proj_mm, 1)


N_TILE = SEQ // P
G_KV = 4
REP = 4
N_CMP_PAD = 32


def attend_prompt(nc, A):
    UNITS = [(r, t) for r in range(REP) for t in range(N_TILE)]
    NU = len(UNITS)
    with ExitStack() as ctx:
        sb = lambda name, shape: ctx.enter_context(nc.sbuf_tensor(name, shape, F32))
        sem = nc.alloc_semaphore
        psum = lambda name: ctx.enter_context(nc.psum_tensor(name, [P, 512], F32))
        q = [sb(f"a_q{j}", [HD, REP, SEQ]) for j in range(2)]
        kT = [sb(f"a_kT{j}", [HD, 2, SEQ]) for j in range(2)]
        vv = [sb(f"a_v{j}", [P, 2, N_TILE, HD]) for j in range(2)]
        kcT = [sb(f"a_kcT{j}", [HD, N_CMP_PAD]) for j in range(2)]
        vc = [sb(f"a_vc{j}", [N_CMP_PAD, HD]) for j in range(2)]
        bias = [sb(f"a_bias{j}", [P, REP, SEQ]) for j in range(2)]
        cbias = [sb(f"a_cbias{j}", [P, NU, N_CMP_PAD]) for j in range(2)]
        gates = [sb(f"a_gates{j}", [P, N_TILE, 3, REP]) for j in range(2)]
        ident, cmask = sb("a_ident", [P, P]), sb("a_cmask", [P, N_TILE, N_CMP_PAD])
        S = [sb(f"a_S{j}", [P, 2, SEQ]) for j in range(2)]
        Pm = [sb(f"a_P{j}", [P, 2, SEQ]) for j in range(2)]
        PT = [sb(f"a_PT{j}", [P, 2, SEQ]) for j in range(2)]
        Sc, Pc = sb("a_Sc", [P, NU, N_CMP_PAD]), sb("a_Pc", [P, NU, N_CMP_PAD])
        PTc = [sb(f"a_PTc{j}", [N_CMP_PAD, P]) for j in range(2)]
        cmax, csum, coef_c = sb("a_cmax", [P, NU]), sb("a_csum", [P, NU]), sb("a_coef_c", [P, NU])
        mx, sums, coef = sb("a_mx", [P, 2, 2]), sb("a_sums", [P, 4, 2]), sb("a_coef", [P, 2, 2])
        acc = sb("a_acc", [P, HD])
        out = [sb(f"a_out{j}", [P, N_TILE, REP, HD]) for j in range(2)]
        s_bank = [[psum(f"s_{n}{j}") for n in ("sel", "win")] for j in range(2)]
        pt_bank = [psum("pt_sel"), psum("pt_win")]
        c_bank, o_bank = psum("c_bank"), psum("o_bank")

        consts, g_in = sem("a_consts"), [sem(f"a_in{j}") for j in range(2)]
        q_scaled, c_scores, c_sub, c_exp, c_ready, gate_done = (
            sem("a_" + n) for n in ("q_scaled", "c_scores", "c_sub", "c_exp", "c_ready", "gate_done"))
        scores, max_ready, exp_done, t_done, evA, evB, pv_done, out_done = (
            sem("a_" + n) for n in ("scores", "max_ready", "exp_done", "t_done", "evA", "evB", "pv_done", "out_done"))
        chain, sent, cmax_ready = sem("a_chain"), sem("a_sent"), sem("a_cmax_ready")
        freed = sem("a_freed")
        settled, settled_dve = sem("a_settled"), sem("a_settled_dve")
        load_samples, store_samples, samples_act, samples_act_end, samples_steps, samples_dve, samples_dve_end = \
            rwkv_samples(nc, A, ctx)
        block = ctx.enter_context(nc.Block())
        N_IN = 13

        def keys(t):
            return (t + 1) * P

        @block.sync
        def _(sp):
            sp.dma_start(ident[:, :], A["ident"]).then_inc(consts, 16)
            sp.dma_start(cmask[:, :, :], A["cmask"]).then_inc(consts, 16)
            load_samples(sp)
            with sp.Fori(0, 2) as i:
                for j in range(2):
                    g = i * 2 + j
                    sp.wait_ge(freed, g + 1)
                    rows = lambda base: A["uT"][bass.ds(g * HD + base, HD), 0:SEQ]
                    dma = lambda dst, src: sp.dma_start(dst, src).then_inc(g_in[j], 16)
                    dma(q[j][:, :, :], A["uT"][bass.ds(g * (REP * HD) + COL_Q, REP * HD), 0:SEQ]
                        .rearrange("(r d) n -> d r n", r=REP))
                    dma(kT[j][:, 0, :], rows(COL_S))
                    dma(kT[j][:, 1, :], rows(COL_W))
                    for k, col in enumerate((COL_S, COL_W)):
                        c0 = col + 2 * P - 48 * P
                        dma(vv[j][:, k, :, :], A["u_tok"][:, :, bass.ds(g * HD + c0, HD)])
                    dma(kcT[j][:, :], A["kcT"][DEC_B, i, j * HD:(j + 1) * HD, 0:N_CMP_PAD]
                        if isinstance(i, int) else
                        A["kcT"][DEC_B][bass.ds(i, 1)].rearrange("a p n -> (a p) n")[j * HD:(j + 1) * HD, 0:N_CMP_PAD])
                    dma(vc[j][:, :], A["vc"][DEC_B, 0:N_CMP_PAD, :, :].rearrange("p k n -> p (k n)")
                        [:, bass.ds(g * HD, HD)])
                    for t in range(N_TILE):
                        dma(gates[j][:, t, :, :], A["u_tok"][:, t, COL_GATE - 48 * P:COL_GATE - 48 * P + N_GATE]
                            .rearrange("p (b g r) -> g p b r", b=3, g=G_KV)[bass.ds(g, 1)]
                            .rearrange("a p b r -> (a p) b r"))
                    dma(bias[j][:, :, :], A["bias_p"][bass.ds(g, 1)].rearrange("a p r n -> (a p) r n"))
                    dma(cbias[j][:, :, :], A["cbias_p"][bass.ds(g, 1)].rearrange("a p u n -> (a p) u n"))
            store_samples(sp)

        @block.gpsimd
        def _(pool):
            samples_steps(pool)

        @block.scalar
        def _(act):
            f = nc.scalar.activation
            act.sem_inc(freed, 2)
            samples_act(act)
            with act.Fori(0, 2) as i:
                for j in range(2):
                    g = i * 2 + j
                    act.wait_ge(g_in[j], i * 16 * N_IN + 16 * N_IN)
                    f(q[j][:, :, :], q[j][:, :, :], ACT.Copy, scale=HD ** -0.5).then_inc(q_scaled, 1)
                    f(gates[j][:, :, :, :], gates[j][:, :, :, :], ACT.Sigmoid).then_inc(gate_done, 1)

                    def exps(u):
                        r, t = UNITS[u]
                        act.wait_ge(max_ready, g * NU + u + 1)
                        for k in range(2):
                            ins = f(Pm[u % 2][:, k, 0:keys(t)], S[u % 2][:, k, 0:keys(t)], ACT.Exp,
                                    bias=mx[:, u % 2, k:k + 1], accum_out=sums[:, u % 4, k:k + 1])
                        ins.then_inc(exp_done, 1)
                    act.wait_ge(c_sub, g + 1)
                    f(Pc[:, :, :], Sc[:, :, :], ACT.Exp).then_inc(c_exp, 1)
                    exps(0)
                    for u, (r, t) in enumerate(UNITS):
                        if u + 1 < NU:
                            exps(u + 1)
                        act.wait_ge(t_done, g * NU + u + 1)
                        f(PT[u % 2][:, 0, 0:keys(t)], pt_bank[0][:, 0:keys(t)], ACT.Copy)
                        f(PTc[u % 2][:, :], c_bank[0:N_CMP_PAD, 0:P], ACT.Copy).then_inc(evA, 1)
                    act.wait_ge(out_done, g * NU + NU)
                    act.dma_start(A["obN"][:, :, bass.ds(g * (REP * HD), REP * HD)],
                                  out[j][:, :, :, :].rearrange("p t r d -> p t (r d)")).then_inc(sent, 16)
                    act.wait_ge(sent, g * 16 + 16)
                    act.sem_inc(freed, 1)
            samples_act_end(act)

        @block.vector
        def _(dve):
            v = nc.vector
            link = same_engine(dve, chain)
            samples_dve(dve)
            dve.wait_ge(consts, 32)
            with dve.Fori(0, 2) as i:
                for j in range(2):
                    g = i * 2 + j

                    def maxes(u):
                        r, t = UNITS[u]
                        dve.wait_ge(scores, g * NU + u + 1)
                        dve.sem_inc(settled_dve, 1)
                        for k in range(2):
                            last = v.tensor_tensor_reduce(
                                out=S[u % 2][:, k, 0:keys(t)], in0=s_bank[u % 2][k][:, 0:keys(t)],
                                in1=bias[j][:, r, SEQ - keys(t):SEQ], scale=1.0, scalar=-3e38,
                                op0=ALU.add, op1=ALU.max, accum_out=mx[:, u % 2, k:k + 1])
                        link(last)
                        v.tensor_scalar(mx[:, u % 2, :], mx[:, u % 2, :], -1.0, None, ALU.mult).then_inc(max_ready, 1)
                    dve.wait_ge(c_scores, g + 1)
                    link(v.tensor_tensor(Sc[:, :, :], c_bank[:, :].rearrange("p (u n) -> p u n", n=N_CMP_PAD),
                                         cbias[j][:, :, :], ALU.add))
                    link(v.tensor_reduce(cmax[:, :], Sc[:, :, :], axis=AX.X, op=ALU.max))
                    v.tensor_tensor(Sc[:, :, :], Sc[:, :, :], cmax[:, :, None].to_broadcast([P, NU, N_CMP_PAD]),
                                    ALU.subtract).then_inc(c_sub, 1)
                    maxes(0)
                    dve.wait_ge(c_exp, g + 1)
                    for r in range(REP):
                        last = v.tensor_tensor(Pc[:, 4 * r:4 * r + 4, :], Pc[:, 4 * r:4 * r + 4, :], cmask[:, :, :],
                                               ALU.mult)
                    last.then_inc(c_ready, 1)
                    dve.wait_ge(c_ready, g + 1)
                    link(v.reduce_sum(csum[:, :], Pc[:, :, :], axis=AX.X))
                    link(v.tensor_scalar(csum[:, :], csum[:, :], 1e-30, None, ALU.max))
                    link(v.reciprocal(csum[:, :], csum[:, :]))
                    dve.wait_ge(gate_done, g + 1)
                    link(v.tensor_tensor(coef_c[:, :].rearrange("p (r t) -> p r t", t=N_TILE),
                                         csum[:, :].rearrange("p (r t) -> p r t", t=N_TILE),
                                         gates[j][:, :, 0, :].rearrange("p t r -> p r t"), ALU.mult))

                    def outs(u):
                        r, t = UNITS[u]
                        link(v.reciprocal(coef[:, u % 2, :], sums[:, u % 4, :]))
                        link(v.tensor_tensor(coef[:, u % 2, :], coef[:, u % 2, :], gates[j][:, t, 1:3, r], ALU.mult))
                        dve.wait_ge(pv_done, g * NU + u + 1)
                        o = lambda k: o_bank[:, k * HD:(k + 1) * HD]
                        dst = out[j][:, t, r, :]
                        link(v.tensor_scalar(acc[:, :], o(0), coef[:, u % 2, 0:1], None, ALU.mult))
                        link(v.scalar_tensor_tensor(out=acc[:, :], in0=o(1), scalar=coef[:, u % 2, 1:2], in1=acc[:, :],
                                                    op0=ALU.mult, op1=ALU.add))
                        v.scalar_tensor_tensor(out=dst, in0=o(2), scalar=coef_c[:, u:u + 1],
                                               in1=acc[:, :], op0=ALU.mult, op1=ALU.add).then_inc(out_done, 1)
                    for u, (r, t) in enumerate(UNITS):
                        if u + 1 < NU:
                            maxes(u + 1)
                        dve.wait_ge(t_done, g * NU + u + 1)
                        v.tensor_copy(PT[u % 2][:, 1, 0:keys(t)], pt_bank[1][:, 0:keys(t)]).then_inc(evB, 1)
                        if u:
                            outs(u - 1)
                    outs(NU - 1)
                link.restart()
            samples_dve_end(dve)

        @block.tensor
        def _(pe):
            mm = nc.tensor.matmul
            settle = lambda: pe.sem_inc(settled, 1)
            pe.wait_ge(consts, 32)
            with pe.Fori(0, 2) as i:
                for j in range(2):
                    g = i * 2 + j

                    def score(u):
                        r, t = UNITS[u]
                        if u >= 2:
                            pe.wait_ge(max_ready, g * NU + u - 1)
                            settle()
                        for k in range(2):
                            ins = mm(s_bank[u % 2][k][:, 0:keys(t)], q[j][:, r, t * P:(t + 1) * P],
                                     kT[j][:, k, 0:keys(t)], start=True, stop=True)
                        ins.then_inc(scores, 1)
                    pe.wait_ge(q_scaled, g + 1)
                    settle()
                    for u, (r, t) in enumerate(UNITS):
                        ins = mm(c_bank[:, u * N_CMP_PAD:(u + 1) * N_CMP_PAD], q[j][:, r, t * P:(t + 1) * P],
                                 kcT[j][:, :], start=True, stop=True)
                    ins.then_inc(c_scores, 1)
                    score(0)

                    def values(u):
                        r, t = UNITS[u]
                        pe.wait_ge(evA, g * NU + u + 1)
                        pe.wait_ge(evB, g * NU + u + 1)
                        if u:
                            pe.wait_ge(out_done, g * NU + u)
                        settle()
                        for k in range(2):
                            for b in range(t + 1):
                                mm(o_bank[:, k * HD:(k + 1) * HD], PT[u % 2][:, k, b * P:(b + 1) * P],
                                   vv[j][:, k, b, :], start=(b == 0), stop=(b == t))
                        mm(o_bank[:, 2 * HD:3 * HD], PTc[u % 2][:, :], vc[j][:, :], start=True, stop=True)\
                            .then_inc(pv_done, 1)
                    for u, (r, t) in enumerate(UNITS):
                        if u + 1 < NU:
                            score(u + 1)
                        pe.wait_ge(exp_done, g * NU + u + 1)
                        if u == 0:
                            pe.wait_ge(c_ready, g + 1)
                        else:
                            pe.wait_ge(evA, g * NU + u)
                            pe.wait_ge(evB, g * NU + u)
                        settle()
                        for k in range(2):
                            for b in range(t + 1):
                                nc.tensor.transpose(pt_bank[k][:, b * P:(b + 1) * P],
                                                    Pm[u % 2][:, k, b * P:(b + 1) * P], ident[:, :])
                        nc.tensor.transpose(c_bank[0:N_CMP_PAD, 0:P], Pc[:, u, :], ident[:, :]).then_inc(t_done, 1)
                        if u:
                            values(u - 1)
                    values(NU - 1)
                    pe.wait_ge(out_done, g * NU + NU)
                    settle()


S_SEL, S_SNEW, S_WIN, S_WNEW, S_CMP, S_END = 0, 2048, 2052, 2564, 2568, 2696
N_SELECT = 16


def attend_samples(nc, A):
    with ExitStack() as ctx:
        sb = lambda name, shape: ctx.enter_context(nc.sbuf_tensor(name, shape, F32))
        sem = nc.alloc_semaphore
        table = ctx.enter_context(nc.sbuf_tensor("d_table", [1, DEC_B * N_PAGES], I32))
        kvS = [[sb(f"d_kv{j}{b}", [P, N_PAGES, 4 * P]) for b in range(2)] for j in range(2)]
        kW, vW = ([sb(f"d_{n}{b}", [P, 2, WINDOW]) for b in range(2)] for n in ("kW", "vW"))
        kC, vC = ([sb(f"d_{n}{b}", [P, 2, P]) for b in range(2)] for n in ("kC", "vC"))
        vN = [sb(f"d_vN{b}", [DEC_T, 2, 2 * P]) for b in range(2)]
        q_raw, q_all = sb("d_q_raw", [P, 2, REP, NS]), sb("d_q_all", [P, DEC_B, 2, 32])
        q = sb("d_q", [P, 2, 2, 32])
        kN_all, kN = sb("d_kN_all", [P, 2, 2, NS]), sb("d_kN", [P, 2, 2, 2, DEC_T])
        bias, S, PT = sb("d_bias", [P, S_END]), sb("d_S", [P, S_END]), sb("d_PT", [P, N_PAGES, P])
        PTc, PTw, PTn = sb("d_PTc", [P, P]), sb("d_PTw", [P, 4, P]), sb("d_PTn", [DEC_T, 2, P])
        ident, gsum, overlap = sb("d_ident", [P, P]), sb("d_gsum", [P, P]), sb("d_overlap", [P, N_SEL])
        selc = sb("d_selc", [P, 2, N_SEL])
        lower = sb("d_lower", [P, N_SEL, N_SEL])
        gmask = sb("d_gmask", [P, G_KV])
        imp, score, rank, mb = (sb("d_" + n, [P, N_SEL]) for n in ("imp", "score", "rank", "mb"))
        gt, eq = sb("d_gt", [P, N_SEL, N_SEL]), sb("d_eq", [P, N_SEL, N_SEL])
        mx, nmx, sums, coef = sb("d_mx", [P, 3]), sb("d_nmx", [P, 3]), sb("d_sums", [P, 3]), sb("d_coef", [P, 3])
        gates = sb("d_gates", [P, 4, 3])
        tok_gates, own_head = sb("d_tok_gates", [NS, N_GATE]), sb("d_own_head", [P, 16])
        spread = PT[0:NS, 0:4, :]
        row_gates = eq[:, 0:12, 0:16]
        gates_now = sb("d_gates_now", [P, 3])
        acc, o = sb("d_acc", [P, G_KV, HD]), sb("d_o", [P, HD])
        psum = lambda name: ctx.enter_context(nc.psum_tensor(name, [P, 512], F32))
        sc = [psum("d_sc0"), psum("d_sc1")]
        small, pt, ob, oc, ps_imp = psum("d_small"), [psum("d_pt0"), psum("d_pt1")], psum("d_ob"), psum("d_oc"), psum("d_ps_imp")

        names = ("consts", "table_in", "q_in", "zeroed", "q_ready", "set_up", "small_done", "small_out", "win_sc",
                 "keys_used", "c_exp", "c_norm", "c_max", "ptc_done", "ptc_out", "imp_done", "imp_out", "imp2_done", "w_max", "w_exp",
                 "s_max", "s_exp", "o_done", "freed", "sent", "settled", "chain", "o_ready", "sel_sc", "sel_out",
                 "pt_done", "pt_out", "gates_ready", "gates_spread", "pv_c", "win_out", "ptn_done")
        s = {n: sem("d_" + n) for n in names}
        pages_in = [sem(f"d_pages_in{j}") for j in range(2)]
        keys_in, values_in = sem("d_keys_in"), sem("d_values_in")
        block = ctx.enter_context(nc.Block())
        GROUPS = [(kind, n) for kind in ("w", "s") for n in range(1 if kind == "w" else 4)]

        @block.sync
        def _(sp):
            sp.dma_start(table[:, :], A["page_table"]).then_inc(s["table_in"], 16)
            for dst, src in ((ident, "ident"), (gsum, "gsum"), (overlap, "overlap"), (selc, "selc"), (lower, "lower"),
                             (gmask, "gmask"), (bias, "bias_s")):
                sp.dma_start(dst[:], A[src]).then_inc(s["consts"], 16)
            for g2 in range(2):
                for gp in range(2):
                    row = COL_Q + (2 * gp + g2) * REP * HD
                    sp.dma_start(q_raw[g2 * HD:(g2 + 1) * HD, gp, :, :],
                                 A["uT"][row:row + REP * HD, SEQ:NT].rearrange("(r d) n -> d r n", r=REP))\
                        .then_inc(s["q_in"], 16)
            for k, col in enumerate((COL_S, COL_W)):
                sp.dma_start(kN_all[:, k, :, :], A["uT"][col:col + 2 * P, SEQ:NT].rearrange("(g p) n -> p g n", g=2))\
                    .then_inc(s["q_in"], 16)
            sp.dma_start(tok_gates[:, :], A["u_tail"][1:1 + NS, COL_GATE:COL_GATE + N_GATE]).then_inc(s["q_in"], 16)
            sp.dma_start(spread, A["spread"]).then_inc(s["q_in"], 16)
            sp.dma_start(own_head[:, :], A["own_head"]).then_inc(s["q_in"], 16)
            sp.wait_ge(s["table_in"], 16)
            with sp.Fori(0, 2) as i:
                for j in range(2):
                    bp = i * 2 + j
                    sp.wait_ge(s["freed"], bp + 2)
                    for b2 in range(2):
                        for p in range(N_PAGES):
                            page = sp.value_load(table[0:1, bass.ds(bp * (2 * N_PAGES) + b2 * N_PAGES + p, 1)],
                                                 min_val=0, max_val=N_POOL - 1)
                            sp.dma_start(kvS[j][b2][:, p, :], A["sel_kv"][bass.ds(page, 1)]
                                         .rearrange("a p n -> (a p) n")).then_inc(pages_in[j], 16)
                    sp.wait_ge(s["keys_used"], bp + 1)
                    for b2 in range(2):
                        one = lambda name: A[name][bass.ds(bp * 2 + b2, 1)]
                        for dst, src in ((kC[b2][:, :, :], one("kcT").rearrange("a k p n -> p (a k) n")),
                                         (kW[b2][:, :, :], one("win_k").rearrange("a k p n -> p (a k) n"))):
                            sp.dma_start(dst, src).then_inc(keys_in, 16)
                    sp.wait_ge(s["freed"], bp + 3)
                    for b2 in range(2):
                        b = bp * 2 + b2
                        one = lambda name: A[name][bass.ds(b, 1)]
                        for dst, src in ((vC[b2][:, :, :], one("vc").rearrange("a p k n -> (a p) k n")),
                                         (vW[b2][:, :, :].rearrange("p a (c n) -> p (a c) n", n=2 * P),
                                          one("win_v").rearrange("a p t n -> (a p) t n")),
                                         (vN[b2][:, :, :], A["u_tail"][bass.ds(b * DEC_T + 1, DEC_T), COL_S + 2 * P:COL_W + 4 * P]
                                          .rearrange("p (k n) -> p k n", n=2 * P)[:, 0:3:2, :])):
                            sp.dma_start(dst, src).then_inc(values_in, 16)

        @block.scalar
        def _(act):
            f = nc.scalar.activation
            act.sem_inc(s["freed"], 3)
            act.wait_ge(s["q_in"], 16 * 9)
            act.wait_ge(s["zeroed"], 1)
            for g2 in range(2):
                rows = slice(g2 * HD, (g2 + 1) * HD)
                for gp in range(2):
                    ins = f(q_all[rows, :, gp, g2 * 16:(g2 + 1) * 16].rearrange("p b (t r) -> p b t r", r=REP),
                            q_raw[rows, gp, :, :].rearrange("p r (b t) -> p b t r", t=DEC_T), ACT.Copy, scale=HD ** -0.5)
            ins.then_inc(s["q_ready"], 1)
            f(tok_gates[:, :], tok_gates[:, :], ACT.Sigmoid).then_inc(s["gates_ready"], 1)
            with act.Fori(0, 2) as i:
                for j in range(2):
                    bp = i * 2 + j
                    w = lambda name, n=1, k=1: act.wait_ge(s[name], bp * n + k)

                    def soft(name, a, b, k):
                        f(S[:, a:b], S[:, a:b], ACT.Exp, bias=nmx[:, k:k + 1], accum_out=sums[:, k:k + 1])\
                            .then_inc(s[name], 1)
                    w("c_max")
                    soft("c_exp", S_CMP, S_END, 2)
                    w("ptc_done")
                    f(PTc[:, :], pt[0][:, 0:P], ACT.Copy).then_inc(s["ptc_out"], 1)
                    w("imp_done")
                    f(imp[:, :], ps_imp[:, 0:N_SEL], ACT.Copy).then_inc(s["imp_out"], 1)
                    w("w_max")
                    soft("w_exp", S_WIN, S_CMP, 1)
                    w("pt_done", 5, 1)
                    f(PTw[:, :, :], pt[1][:, :].rearrange("p (k n) -> p k n", k=4), ACT.Copy).then_inc(s["pt_out"], 1)
                    w("s_max")
                    soft("s_exp", S_SEL, S_WIN, 0)
                    w("ptn_done")
                    f(PTn[:, :, :], ps_imp[0:DEC_T, 0:2 * P].rearrange("p (k n) -> p k n", k=2), ACT.Copy)\
                        .then_inc(s["pt_out"], 1)
                    for n in range(4):
                        w("pt_done", 5, n + 2)
                        f(PT[:, 4 * n:4 * n + 4, :], pt[n % 2][:, :].rearrange("p (k n) -> p k n", k=4), ACT.Copy)\
                            .then_inc(s["pt_out"], 1)
                    w("o_ready")
                    act.dma_start(A["obS"][bass.ds(bp, 1)].rearrange("a p n -> (a p) n"), o[:, :]).then_inc(s["sent"], 16)
                    w("sent", 16, 16)
                    act.sem_inc(s["freed"], 1)

        @block.vector
        def _(dve):
            v = nc.vector
            tt, ts, stt = v.tensor_tensor, v.tensor_scalar, v.scalar_tensor_tensor
            link = same_engine(dve, s["chain"])
            v.memset(q_all[:, :, :, :], 0.0).then_inc(s["zeroed"], 1)
            dve.wait_ge(s["consts"], 16 * 7)
            dve.sem_inc(s["keys_used"], 1)
            dve.wait_ge(s["q_ready"], 1)
            dve.wait_ge(s["gates_spread"], 1)
            link(tt(row_gates, small[:, 0:4 * N_GATE].rearrange("p (x h) -> p x h", h=16),
                    own_head[:, None, :].to_broadcast([P, 12, 16]), ALU.mult))
            link(v.reduce_sum(gates[:, :, :].rearrange("p b c -> p (b c)"), row_gates, axis=AX.X))
            link.restart()
            with dve.Fori(0, 2) as i:
                for j in range(2):
                    bp = i * 2 + j
                    w = lambda name, n=1, k=1: dve.wait_ge(s[name], bp * n + k)
                    w("freed", 1, 3)
                    v.tensor_copy(q[:, :, :, :], q_all[:, bass.ds(bp * 2, 2), :, :])
                    v.tensor_copy(gates_now[:, :], gates[:, bass.ds(bp, 1), :].rearrange("p a c -> p (a c)"))
                    for b2 in range(2):
                        last = v.tensor_copy(kN[:, b2, :, :, :], kN_all[:, :, :, bass.ds(bp * (2 * DEC_T) + b2 * DEC_T, DEC_T)])
                    last.then_inc(s["set_up"], 1)
                    w("small_done")
                    tt(S[:, S_CMP:S_END], small[:, 0:P], bias[:, S_CMP:S_END], ALU.add)
                    tt(S[:, S_SNEW:S_WIN], small[:, P:P + DEC_T], bias[:, S_SNEW:S_WIN], ALU.add)
                    link(tt(S[:, S_WNEW:S_CMP], small[:, P + DEC_T:P + 2 * DEC_T], bias[:, S_WNEW:S_CMP], ALU.add))

                    def neg_max(a, b, k, name):
                        link(v.reduce_max(mx[:, k:k + 1], S[:, a:b], axis=AX.X))
                        ts(nmx[:, k:k + 1], mx[:, k:k + 1], -1.0, None, ALU.mult).then_inc(s[name], 1)
                    neg_max(S_CMP, S_END, 2, "c_max")
                    for n in range(5):
                        w("sel_sc", 5, n + 1)
                        a = S_WIN if n == 0 else 512 * (n - 1)
                        tt(S[:, a:a + 512], sc[n % 2][:, :], bias[:, a:a + 512], ALU.add).then_inc(s["sel_out"], 1)
                        if n == 0:
                            w("sel_out", 5, 1)
                            neg_max(S_WIN, S_CMP, 1, "w_max")
                        if n == 1:
                            w("c_exp")
                            link(v.reciprocal(coef[:, 2:3], sums[:, 2:3]))
                            ts(S[:, S_CMP:S_END], S[:, S_CMP:S_END], coef[:, 2:3], None, ALU.mult).then_inc(s["c_norm"], 1)
                    w("sel_out", 5, 5)
                    dve.sem_inc(s["keys_used"], 1)
                    w("imp2_done")
                    link(tt(score[:, :], ps_imp[:, 64:64 + N_SEL], selc[:, 0, :], ALU.mult))
                    link(tt(score[:, :], score[:, :], selc[:, 1, :], ALU.add))
                    si = score[:, None, :].to_broadcast([P, N_SEL, N_SEL])
                    sj = score[:, :, None].to_broadcast([P, N_SEL, N_SEL])
                    tt(gt[:, :, :], si, sj, ALU.is_gt)
                    link(tt(eq[:, :, :], si, sj, ALU.is_equal))
                    link(tt(eq[:, :, :], eq[:, :, :], lower[:, :, :], ALU.mult))
                    link(tt(gt[:, :, :], gt[:, :, :], eq[:, :, :], ALU.add))
                    link(v.reduce_sum(rank[:, :], gt[:, :, :], axis=AX.X))
                    link(ts(mb[:, :], rank[:, :], N_SELECT - 0.5, NEG, ALU.is_gt, ALU.mult))
                    link(tt(S[:, 0:PAST].rearrange("p (j k) -> p j k", k=SEL_BLOCK),
                            S[:, 0:PAST].rearrange("p (j k) -> p j k", k=SEL_BLOCK),
                            mb[:, 0:N_SEL - 1, None].to_broadcast([P, N_SEL - 1, SEL_BLOCK]), ALU.add))
                    link(ts(S[:, S_SNEW:S_WIN], S[:, S_SNEW:S_WIN], mb[:, N_SEL - 1:N_SEL], None, ALU.add))
                    neg_max(S_SEL, S_WIN, 0, "s_max")
                    w("s_exp")
                    w("w_exp")
                    link(v.reciprocal(coef[:, 0:2], sums[:, 0:2]))
                    link(tt(coef[:, 0:2], coef[:, 0:2], gates_now[:, 1:3], ALU.mult))
                    w("o_done")
                    flat = acc[:, :, :].rearrange("p g d -> p (g d)")
                    link(ts(flat, ob[:, 0:2 * P], coef[:, 0:1], None, ALU.mult))
                    link(stt(out=flat, in0=ob[:, 2 * P:4 * P], scalar=coef[:, 1:2], in1=flat, op0=ALU.mult, op1=ALU.add))
                    link(stt(out=flat, in0=oc[:, 0:2 * P], scalar=gates_now[:, 0:1], in1=flat, op0=ALU.mult, op1=ALU.add))
                    link(tt(acc[:, :, :], acc[:, :, :], gmask[:, :, None].to_broadcast([P, G_KV, HD]), ALU.mult))
                    v.reduce_sum(o[:, :], acc[:, :, :].rearrange("p g d -> p d g"), axis=AX.X).then_inc(s["o_ready"], 1)
                link.restart()

        @block.tensor
        def _(pe):
            mm = nc.tensor.matmul
            pe.wait_ge(s["consts"], 16 * 7)
            pe.wait_ge(s["gates_ready"], 1)
            for bp in range(4):
                ins = mm(small[:, bp * N_GATE:(bp + 1) * N_GATE], spread[:, bp, :], tok_gates[:, :], start=True, stop=True)
            ins.then_inc(s["gates_spread"], 1)
            with pe.Fori(0, 2) as i:
                for j in range(2):
                    bp = i * 2 + j

                    def w(*conditions):
                        for name, n, k in conditions:
                            pe.wait_ge(s[name], bp * n + k)
                        pe.sem_inc(s["settled"], 1)
                    rows = lambda b2, gp: slice(b2 * HD + gp * 32, b2 * HD + gp * 32 + 32)
                    PAIRS = [(b2, gp) for b2 in range(2) for gp in range(2)]
                    pe.wait_ge(keys_in, bp * 64 + 64)
                    w(("set_up", 1, 1))
                    for b2, gp in PAIRS:
                        mm(small[rows(b2, gp), 0:P], q[:, b2, gp, :], kC[b2][:, gp, :], start=True, stop=True)
                        for k in range(2):
                            c = P + k * DEC_T
                            ins = mm(small[rows(b2, gp), c:c + DEC_T], q[:, b2, gp, :], kN[:, b2, k, gp, :],
                                     start=True, stop=True)
                    ins.then_inc(s["small_done"], 1)
                    for n in range(5):
                        if n >= 2:
                            w(("sel_out", 5, n - 1))
                        if n == 1:
                            pe.wait_ge(pages_in[j], i * (2 * N_PAGES * 16) + 2 * N_PAGES * 16)
                            pe.sem_inc(s["settled"], 1)
                        for b2, gp in PAIRS:
                            rhs = kW[b2][:, gp, :] if n == 0 else kvS[j][b2][:, 4 * (n - 1):4 * n, gp * P:(gp + 1) * P]
                            out = sc[n % 2][rows(b2, gp), :]
                            if n:
                                out = out.rearrange("p (a k) -> p a k", k=PAGE)
                            ins = mm(out, q[:, b2, gp, :], rhs, start=True, stop=True)
                        ins.then_inc(s["sel_sc"], 1)
                    w(("c_norm", 1, 1))
                    nc.tensor.transpose(pt[0][:, 0:P], S[:, S_CMP:S_END], ident[:, :]).then_inc(s["ptc_done"], 1)
                    w(("ptc_out", 1, 1))
                    mm(ps_imp[:, 0:N_SEL], PTc[:, :], overlap[:, :], start=True, stop=True).then_inc(s["imp_done"], 1)
                    w(("imp_out", 1, 1))
                    mm(ps_imp[:, 64:64 + N_SEL], gsum[:, :], imp[:, :], start=True, stop=True).then_inc(s["imp2_done"], 1)
                    halves = [slice(b2 * HD, (b2 + 1) * HD) for b2 in range(2)]
                    pe.wait_ge(values_in, bp * 96 + 96)
                    pe.sem_inc(s["settled"], 1)
                    for b2, h in enumerate(halves):
                        mm(oc[h, 0:2 * P], PTc[:, h], vC[b2][:, :, :].rearrange("p a n -> p (a n)"), start=True, stop=True)
                    w(("w_exp", 1, 1))
                    for n in range(4):
                        ins = nc.tensor.transpose(pt[1][:, n * P:(n + 1) * P], S[:, S_WIN + n * P:S_WIN + (n + 1) * P],
                                                  ident[:, :])
                    ins.then_inc(s["pt_done"], 1)
                    w(("s_exp", 1, 1))
                    for k, c in enumerate((S_SNEW, S_WNEW)):
                        ins = nc.tensor.transpose(ps_imp[0:DEC_T, k * P:(k + 1) * P], S[:, c:c + DEC_T], ident[:, :])
                    ins.then_inc(s["ptn_done"], 1)
                    for n in range(4):
                        w(("pt_out", 6, 1 if n < 2 else n + 1))
                        for k in range(4):
                            c = (4 * n + k) * P
                            ins = nc.tensor.transpose(pt[n % 2][:, k * P:(k + 1) * P], S[:, c:c + P], ident[:, :])
                        ins.then_inc(s["pt_done"], 1)
                    w(("pt_out", 6, 6))
                    for b2, h in enumerate(halves):
                        for kind, tiles, pts, vals in ((0, N_PAGES, PT, kvS[j][b2][:, :, 2 * P:4 * P]),
                                                       (1, 4, PTw, vW[b2][:, :, :].rearrange("p a (c n) -> p (a c) n", n=2 * P))):
                            out = ob[h, kind * 2 * P:(kind + 1) * 2 * P]
                            for n in range(tiles):
                                mm(out, pts[:, n, h], vals[:, n, :], start=(n == 0), stop=False)
                            ins = mm(out, PTn[:, kind, h], vN[b2][:, kind, :], start=False, stop=True)
                    ins.then_inc(s["o_done"], 1)


KW = A_WIDTH // P
N_OUT = D_MODEL // P


def merge_and_out(nc, A):
    with ExitStack() as ctx:
        sb = lambda name, shape, dt=F32: ctx.enter_context(nc.sbuf_tensor(name, shape, dt))
        sem = nc.alloc_semaphore
        o_lo = sb("m_o_lo", [P, KD, NT], F32R)
        w = [sb(f"m_w{j}", [P, KD, P]) for j in range(2)]
        w_hi, w_lo = ([sb(f"m_w_{n}{j}", [P, KD, P], F32R) for j in range(2)] for n in ("hi", "lo"))
        gates = [sb(f"m_gates{j}", [P, 2, NT]) for j in range(2)]
        prod = sb("m_prod", [P, 2, NT])
        xr, sq = (sb("m_" + n, [P, 2, NT]) for n in ("xr", "sq"))
        oa_s, ob_s = (t[0:NS, :, :].rearrange("p a n -> p (a n)")[:, 0:1024] for t in (xr, sq))
        ident, ones, g_out, eps = sb("m_ident", [P, P]), sb("m_ones", [P, P]), sb("m_g_out", [P, KD]), sb("m_eps", [P, 1])
        own = lambda stack, name, shape, dt: stack.enter_context(nc.sbuf_tensor(name, shape, dt))
        with ExitStack() as place:
            o_hi = own(place, "m_o_hi", [P, KD, NT], F32R)
            with ExitStack() as upper:
                buf = own(upper, "m_buf", [P, KD * NT], F32)
                o_raw = own(upper, "m_o_raw", [P, KD, NT], F32)
                gT = buf[:, 0:KW * NT].rearrange("p (k n) -> p k n", n=NT)
                ob_tok = buf[:, KW * NT:KW * NT + 4096].rearrange("p (t n) -> p t n", t=4)
                sg = o_raw[:, KW:KD, :]
            m_hi, m_lo = (own(place, "m_m_" + n, [P, KD, NT], F32R) for n in ("hi", "lo"))
        h = own(ctx, "m_h", [P, KD, NT], F32)
        ps = [[ctx.enter_context(nc.psum_tensor(f"m_ps{j}{k}", [P, 2, 512], F32)) for k in range(2)] for j in range(2)]
        sum_sq = ps[0][1]
        g_in, ob_in, oa_in, consts = sem("m_g_in"), sem("m_ob_in"), sem("m_oa_in"), sem("m_consts")
        sig, silu, tps, taken, o_hi_done, o_lo_done = (
            sem("m_" + n) for n in ("sig", "silu", "tps", "taken", "o_hi_done", "o_lo_done"))
        w_in, gates_in, x_in = ([sem(f"m_{n}{j}") for j in range(2)] for n in ("w_in", "gates_in", "x_in"))
        w_hi_done, w_lo_done, mm_done, multiplied, m_sum, m_hi_done, m_lo_done = (
            sem("m_" + n) for n in ("w_hi_done", "w_lo_done", "mm_done", "multiplied", "m_sum", "m_hi_done", "m_lo_done"))
        added, squared, summed, rooted, scaled, sent = (
            sem("m_" + n) for n in ("added", "squared", "summed", "rooted", "scaled", "sent"))
        chain, settled, ones_set = sem("m_chain"), sem("m_settled"), sem("m_ones_set")
        block = ctx.enter_context(nc.Block())
        two = lambda t: t.rearrange("p (a n) -> p a n", a=2)

        @block.sync
        def _(sp):
            def weights(c, j):
                src = A["w_mo"][bass.ds(c, 1)].rearrange("a p k n -> (a p) k n")
                sp.dma_start(w[j][:, :, :], src).then_inc(w_in[j], 16)

            def merge_gates(c, j):
                src = A["uT"][ROW_M:N_ROWS, :].rearrange("(k c p) n -> c p k n", k=2, p=P)[bass.ds(c, 1)]
                sp.dma_start(gates[j][:, :, :], src.rearrange("a p k n -> (a p) k n")).then_inc(gates_in[j], 16)

            def residual(n, j):
                sp.dma_start(xr[:, j, :], A["xT"][:, bass.ds(n, 1), :].rearrange("p a n -> p (a n)"))\
                    .then_inc(x_in[j], 16)
            sp.dma_start(ob_tok, A["obN"]).then_inc(ob_in, 16)
            sp.dma_start(o_raw[:, 0:KW, 0:SEQ], A["oaT"].rearrange("c p n -> p c n")).then_inc(oa_in, 16)
            for c in range(2):
                weights(c, c)
                merge_gates(c, c)
            with sp.Fori(1, 8) as i:
                for j in range(2):
                    c = i * 2 + j
                    sp.wait_ge(w_lo_done, c - 1)
                    weights(c, j)
                    sp.wait_ge(multiplied, c + 1)
                    merge_gates(c, j)
            for c in (N_OUT, N_OUT + 1):
                sp.wait_ge(w_lo_done, c - 1)
                weights(c, c % 2)
            for n in range(2):
                residual(n, n)
            with sp.Fori(9, 16) as i:
                for j in range(2):
                    c = i * 2 + j
                    sp.wait_ge(w_lo_done, c - 1)
                    weights(c, j)
                    sp.wait_ge(added, c - 1 - N_OUT)
                    residual(c - N_OUT, j)

        @block.gpsimd
        def _(pool):
            nc.gpsimd.memset(ones[:, :], 1.0).then_inc(ones_set, 1)
            for q in range(4):
                pool.wait_ge(scaled, 4 * q + 4)
                pool.dma_start(A["yT"][:, 4 * q:4 * q + 4, :], h[:, 4 * q:4 * q + 4, :]).then_inc(sent, 16)
            pool.wait_ge(sent, 64)

        @block.scalar
        def _(act):
            f = nc.scalar.activation
            act.dma_start(gT, A["uT"][COL_GB:COL_GB + 1024, :].rearrange("(c p) n -> p c n", p=P)).then_inc(g_in, 16)
            for dst, src in ((ident, "ident"), (g_out, "g_out")):
                act.dma_start(dst[:, :], A[src]).then_inc(consts, 16)
            act.dma_start(oa_s[:, :].rearrange("n (h d) -> n h d", h=16), A["oS"].rearrange("h n d -> n h d"))\
                .then_inc(ob_in, 16)
            for b in range(DEC_B):
                src = A["obS"][b // 2, (b % 2) * HD:(b % 2 + 1) * HD, :].rearrange("(g t r) d -> t g (r d)", g=G_KV, t=DEC_T)
                act.dma_start(ob_s[b * DEC_T:(b + 1) * DEC_T, :].rearrange("n (g x) -> n g x", g=G_KV), src)\
                    .then_inc(ob_in, 16)
            act.wait_ge(g_in, 16)
            f(sg, gT, ACT.Sigmoid).then_inc(sig, 1)

            def high_part(c, j):
                act.wait_ge(w_in[j], (c - j) * 8 + 16)
                act.wait_ge(mm_done, c)
                f(w_hi[j][:, :, :], w[j][:, :, :], ACT.Copy).then_inc(w_hi_done, 1)
            act.wait_ge(w_in[0], 16)
            f(w_hi[0][:, :, :], w[0][:, :, :], ACT.Copy).then_inc(w_hi_done, 1)
            for c in range(KW):
                act.wait_ge(taken, c + 1)
                f(o_hi[:, c, :], o_raw[:, c, :], ACT.Copy)
                f(o_hi[:, KW + c, :], o_raw[:, KW + c, :], ACT.Copy).then_inc(o_hi_done, 1)
            with act.Fori(0, 8) as i:
                for j in range(2):
                    c = i * 2 + j
                    high_part(c + 1, 1 - j)
                    act.wait_ge(m_sum, c + 1)
                    f(m_hi[:, bass.ds(c, 1), :].rearrange("p a n -> p (a n)"), prod[:, 0, :], ACT.Copy)\
                        .then_inc(m_hi_done, 1)

            def square(c, j):
                n = c - N_OUT
                act.wait_ge(added, n + 1)
                act.wait_ge(summed, n + 1)
                src = h[:, n, :] if isinstance(c, int) else h[:, bass.ds(n, 1), :].rearrange("p a n -> p (a n)")
                f(sq[:, j, :], src, ACT.Square).then_inc(squared, 1)
            with act.Fori(8, 15) as i:
                for j in range(2):
                    c = i * 2 + j
                    high_part(c + 1, 1 - j)
                    square(c, j)
            high_part(31, 1)
            square(30, 0)
            square(31, 1)
            act.wait_ge(summed, 2 + N_OUT)
            f(two(prod[:, 0, :]), sum_sq[:, :, 0:HALF], ACT.Sqrt, bias=eps[:, 0:1], scale=1.0 / D_MODEL).then_inc(rooted, 1)

        @block.vector
        def _(dve):
            v = nc.vector
            link = same_engine(dve, chain)
            link(v.memset(eps[:, :], RMS_EPS))
            dve.sem_inc(multiplied, 2)

            def low_part(c, j):
                dve.wait_ge(w_hi_done, c + 1)
                v.tensor_tensor(w_lo[j][:, :, :], w[j][:, :, :], w_hi[j][:, :, :].bitcast(F32), ALU.subtract)\
                    .then_inc(w_lo_done, 1)
            dve.wait_ge(sig, 1)
            v.tensor_tensor(gT, gT, sg, ALU.mult).then_inc(silu, 1)
            low_part(0, 0)
            dve.wait_ge(silu, 1)
            dve.wait_ge(oa_in, 16)

            def o_low(c):
                dve.wait_ge(o_hi_done, c + 1)
                for k in (c, KW + c):
                    ins = v.tensor_tensor(o_lo[:, k, :], o_raw[:, k, :], o_hi[:, k, :].bitcast(F32), ALU.subtract)
                ins.then_inc(o_lo_done, 1)
            for c in range(KW):
                dve.wait_ge(tps, c + 1)
                p = ps[c % 2]
                v.tensor_tensor(o_raw[:, KW + c, 0:SEQ], p[0][:, 0, :], gT[:, c, 0:SEQ], ALU.mult)
                v.tensor_tensor(o_raw[:, KW + c, SEQ:NT], p[1][:, 0, 0:NS], gT[:, c, SEQ:NT], ALU.mult)
                v.tensor_copy(o_raw[:, c, SEQ:NT], p[1][:, 0, NS:2 * NS]).then_inc(taken, 1)
                if c:
                    o_low(c - 1)
            o_low(KW - 1)
            dve.wait_ge(o_lo_done, KW)
            link.restart()
            with dve.Fori(0, 8) as i:
                for j in range(2):
                    c = i * 2 + j
                    low_part(c + 1, 1 - j)
                    dve.wait_ge(mm_done, c + 2)
                    dve.wait_ge(gates_in[j], i * 16 + 16)
                    for k in range(2):
                        ins = v.tensor_tensor(two(prod[:, k, :]), ps[j][k][:, :, 0:HALF], two(gates[j][:, k, :]), ALU.mult)
                    ins.then_inc(multiplied, 1)
                    dve.wait_ge(multiplied, c + 3)
                    v.tensor_tensor(prod[:, 0, :], prod[:, 0, :], prod[:, 1, :], ALU.add).then_inc(m_sum, 1)
                    dve.wait_ge(m_hi_done, c + 1)
                    one = lambda t: t[:, bass.ds(c, 1), :].rearrange("p a n -> p (a n)")
                    v.tensor_tensor(one(m_lo), prod[:, 0, :], one(m_hi).bitcast(F32), ALU.subtract).then_inc(m_lo_done, 1)
                    dve.wait_ge(m_lo_done, c + 1)

            def add_residual(c, j):
                n = c - N_OUT
                dve.wait_ge(mm_done, c + 2)
                dve.wait_ge(x_in[j], (n - j) * 8 + 16)
                dst = h[:, n, :] if isinstance(c, int) else h[:, bass.ds(n, 1), :].rearrange("p a n -> p (a n)")
                v.tensor_tensor(two(dst), ps[j][0][:, :, 0:HALF], two(xr[:, j, :]), ALU.add).then_inc(added, 1)
            with dve.Fori(8, 15) as i:
                for j in range(2):
                    c = i * 2 + j
                    low_part(c + 1, 1 - j)
                    add_residual(c, j)
            low_part(31, 1)
            add_residual(30, 0)
            add_residual(31, 1)
            dve.wait_ge(rooted, 1)
            link(v.reciprocal(prod[:, 1, :], prod[:, 0, :]))
            dve.wait_ge(consts, 32)
            dve.wait_ge(squared, N_OUT)
            for k in range(N_OUT):
                v.scalar_tensor_tensor(out=h[:, k, :], in0=h[:, k, :], scalar=g_out[:, k:k + 1], in1=prod[:, 1, :],
                                       op0=ALU.mult, op1=ALU.mult).then_inc(scaled, 1)

        @block.tensor
        def _(pe):
            mm = nc.tensor.matmul
            pe.sem_inc(mm_done, 1)
            pe.sem_inc(summed, 2)
            pe.wait_ge(consts, 32)
            pe.wait_ge(ob_in, 16 * 10)
            for c in range(KW):
                if c >= 2:
                    pe.wait_ge(taken, c - 1)
                p = ps[c % 2]
                cols = slice(c * P, (c + 1) * P)
                for t in range(4):
                    nc.tensor.transpose(p[0][:, 0, t * P:(t + 1) * P], ob_tok[:, t, cols], ident[:, :])
                mm(p[1][:, 0, 0:NS], ob_s[:, cols], ident[0:NS, 0:NS], start=True, stop=True)
                mm(p[1][:, 0, NS:2 * NS], oa_s[:, cols], ident[0:NS, 0:NS], start=True, stop=True).then_inc(tps, 1)
            pe.wait_ge(o_lo_done, KW)

            def product(out, j, tiles, x_hi, x_lo):
                parts = ((w_hi[j], x_hi), (w_hi[j], x_lo), (w_lo[j], x_hi))
                for k in tiles:
                    for n, (a, x) in enumerate(parts):
                        for half in range(2):
                            ins = mm(out[:, half, 0:HALF], a[:, k, :], x[:, k, half * HALF:(half + 1) * HALF],
                                     start=(k == tiles[0] and n == 0), stop=(k == tiles[-1] and n == 2))
                return ins
            with pe.Fori(0, 8) as i:
                for j in range(2):
                    c = i * 2 + j
                    pe.wait_ge(w_lo_done, c + 1)
                    pe.wait_ge(multiplied, c + 1)
                    pe.sem_inc(settled, 1)
                    product(ps[j][0], j, range(KW), o_hi, o_lo)
                    product(ps[j][1], j, range(KW, KD), o_hi, o_lo).then_inc(mm_done, 1)
            pe.wait_ge(m_lo_done, N_OUT)
            pe.wait_ge(ones_set, 1)

            def square_sum(n, j):
                pe.wait_ge(squared, n + 1)
                pe.sem_inc(settled, 1)
                for half in range(2):
                    ins = mm(sum_sq[:, half, 0:HALF], ones[:, :], sq[:, j, half * HALF:(half + 1) * HALF],
                             start=(isinstance(n, int) and n == 0), stop=(isinstance(n, int) and n == N_OUT - 1))
                ins.then_inc(summed, 1)

            def y_chunk(c, j):
                pe.wait_ge(w_lo_done, c + 1)
                if isinstance(c, int) and c < N_OUT + 2:
                    pe.wait_ge(multiplied, 2 + N_OUT)
                else:
                    pe.wait_ge(added, c - 1 - N_OUT)
                pe.sem_inc(settled, 1)
                product(ps[j][0], j, range(KD), m_hi, m_lo).then_inc(mm_done, 1)
            y_chunk(16, 0)
            y_chunk(17, 1)
            square_sum(0, 0)
            with pe.Fori(9, 16) as i:
                for j in range(2):
                    c = i * 2 + j
                    y_chunk(c, j)
                    square_sum(c - N_OUT - 1, 1 - j)
            square_sum(N_OUT - 1, 1)



def program(nc, A):
    for phase in (project, rwkv, compress_prompt, attend_prompt, attend_samples, merge_and_out):
        before = nc.snapshot_sems()
        phase(nc, A)
        nc.clear_and_free_semaphores(nc.allocated_since(before))
        nc.all_engine_barrier()


def laid_out(i):
    w = i["w_in"][0].reshape(KD, P, -1).transpose(1, 0, 2)

    def groups(a, b):
        return w[:, :, a:b].reshape(P, KD, (b - a) // GRP, GRP).transpose(2, 0, 1, 3)
    x = np.concatenate([i["x_prompt"].reshape(SEQ, D_MODEL), i["x_sample"].reshape(NS, D_MODEL)])
    per_channel = lambda v: v.reshape(-1, P).T
    out = {
        "x": x,
        "xT": x.T.reshape(KD, P, NT).transpose(1, 0, 2),
        "g_in": per_channel(i["norm_in"][0]),
        "w_main": groups(0, 30 * GRP),
        "w_tail": w[:, :, 30 * GRP:COL_GATE + N_GATE],
        "w_merge": groups(COL_GATE + N_GATE, COL_GATE + N_GATE + 2 * D_MODEL),
        "par": np.concatenate([i["mu_shift"][0][:4 * A_WIDTH].reshape(4, 8, P).transpose(1, 2, 0)]
                              + [i[n][0].reshape(8, P, 1) for n in ("w0", "a0", "k_k", "k_a", "r_k", "gn_w", "gn_b")]
                              + [np.zeros((8, P, 1), np.float32)], axis=2),
        "wup": np.concatenate([i["w_up"][0], i["a_up"][0]]).reshape(P, 8, P).transpose(1, 0, 2),
        "lora_mu": i["mu_shift"][0][4 * A_WIDTH:].reshape(P, 1),
        "shift": i["state_shift"][0][:, :4 * A_WIDTH].reshape(DEC_B, 4, 8, P).transpose(2, 3, 1, 0),
        "lora_shift": i["state_shift"][0][:, 4 * A_WIDTH:].T,
        "stab": np.stack([np.repeat(i[n][0].reshape(16, HD), DEC_B, axis=0)
                          for n in ("k_k", "k_a", "r_k", "gn_w", "gn_b")], axis=1),
        "state": i["state_rwkv"][0].transpose(1, 0, 2, 3).reshape(P, HD, HD),
        "cmp_rows": i["cache_cmp_kv"][0].reshape(N_POOL, 8, STRIDE, 4, P).transpose(0, 3, 1, 2, 4)
        .reshape(N_POOL, 4, 8, STRIDE * P),
        "pos_w": np.broadcast_to(np.stack([i["cmp_pos_k"][0].reshape(2, STRIDE, HD),
                                           i["cmp_pos_v"][0].reshape(2, STRIDE, HD)]).reshape(1, 4, STRIDE, HD),
                                 (P, 4, STRIDE, HD)),
        "pos_q": np.repeat(np.stack([i["cmp_pos_k"][0], i["cmp_pos_k"][0], i["cmp_pos_v"][0], i["cmp_pos_v"][0]])
                           .reshape(4, 2, STRIDE, HD), P // 4, axis=0),
        "w_cmp_k": i["w_cmp_k"][0], "w_cmp_v": i["w_cmp_v"][0],
        "page_table": i["page_table"].reshape(1, DEC_B * N_PAGES),
        "sel_kv": np.concatenate([
            i["cache_sel_kv"][0][:, :, 0].reshape(N_POOL, PAGE, 2, P).transpose(0, 3, 2, 1).reshape(N_POOL, P, 2 * P),
            i["cache_sel_kv"][0][:, :, 1].reshape(N_POOL, PAGE, 2 * P)], axis=2),
        "win_k": i["cache_win_kv"][0][:, :, 0].reshape(DEC_B, WINDOW, 2, P).transpose(0, 2, 3, 1),
        "win_v": i["cache_win_kv"][0][:, :, 1].reshape(DEC_B, 4, P, 2 * P).transpose(0, 2, 1, 3),
        "w_mo": np.concatenate([
            np.concatenate([i["w_pa"][0], i["w_pb"][0]]).reshape(16, P, 16, P).transpose(2, 1, 0, 3),
            i["w_o"][0].reshape(16, P, 16, P).transpose(2, 1, 0, 3)]),
        "g_out": per_channel(i["norm_out"][0] if i["norm_out"].ndim > 1 else i["norm_out"]),
        "win_in": i["cache_win_kv"][0].reshape(DEC_B, WINDOW, KVW),
    }
    return out


def constants():
    f = lambda a: np.asarray(a, np.float32)
    s, t = np.arange(CH)[:, None], np.arange(CH)[None, :]
    same16 = s // 16 == t // 16
    two = lambda m: np.concatenate([m, m])
    head = np.arange(P) // HD
    rmask = np.concatenate([
        np.broadcast_to(np.arange(SEQ) % CH != 0, (P, SEQ)),
        np.concatenate([two(s < t), two(s <= t)], axis=1),
        two((s < t) & same16), two((s < t) & ~same16), two((s > t) & same16), two(s == t), two(s == t)], axis=1)
    slope = np.exp2(-8.0 * np.arange(1, 17, dtype=np.float32) / 16).astype(np.float32).reshape(4, 4)
    q, key = np.arange(P)[:, None], np.arange(SEQ)[None, :]
    dist = q + SEQ - P - key
    bias_p = np.where(dist[None, :, None, :] >= 0, -slope[:, None, :, None] * f(dist)[None, :, None, :], NEG)
    tok = (np.arange(4)[:, None] * P + np.arange(P)[None, :])[:, :, None]
    n = np.arange(32)[None, None, :]
    cdist = tok - (n * STRIDE + 2 * STRIDE - 1)
    cmp_ok = (cdist >= 0) & (n < 31)
    cbias_p = np.where(cmp_ok[None, :, :, None, :], -slope[:, None, None, :, None] * f(cdist)[None, :, :, None, :], NEG)
    cbias_p = cbias_p.transpose(0, 2, 3, 1, 4).reshape(4, P, 16, 32)
    row = np.arange(P)
    rg, rt, rr = row // 16 % 4, row // 4 % 4, row % 4
    pos = PAST + rt[:, None]

    def alibi(key, seen):
        d = pos - key[None, :]
        return np.where(seen(d), -slope[rg, rr][:, None] * f(d), NEG)
    new = PAST + np.arange(DEC_T)
    causal = lambda d: d >= 0
    window = lambda d: (d >= 0) & (d <= WINDOW)
    n128 = np.arange(P)
    bias_s = np.concatenate([alibi(np.arange(PAST), causal), alibi(new, causal),
                             alibi(PAST - WINDOW + np.arange(WINDOW), window), alibi(new, window),
                             np.where(n128 < 127, alibi(n128 * STRIDE + 2 * STRIDE - 1, causal), NEG)], axis=1)
    same_group = (row[:, None] // 4) == (row[None, :] // 4)
    cs, bs = n128[:, None] * STRIDE, np.arange(N_SEL)[None, :] * SEL_BLOCK
    overlap = np.clip(np.minimum(cs + 2 * STRIDE, bs + SEL_BLOCK) - np.maximum(cs, bs), 0, None) / (2 * STRIDE)
    forced = np.isin(np.arange(N_SEL), (0, N_SEL - 2, N_SEL - 1))
    selc = np.broadcast_to(np.stack([~forced, forced * 1e4]), (P, 2, N_SEL))
    jj = np.arange(N_SEL)
    same_head = f(head[:, None] == head[None, :])
    return {
        "ident": np.eye(P, dtype=np.float32),
        "headsum": same_head, "headmean": same_head / HD, "rmask": f(rmask),
        "bias_p": f(bias_p), "cbias_p": f(cbias_p), "cmask": f(np.broadcast_to(cmp_ok.transpose(1, 0, 2), (P, 4, 32))),
        "bias_s": f(bias_s), "gsum": f(same_group), "overlap": f(overlap), "selc": f(selc),
        "lower": f(np.broadcast_to(jj[None, None, :] < jj[None, :, None], (P, N_SEL, N_SEL))),
        "spread": f(np.arange(NS)[:, None, None] == (np.arange(4)[None, :, None] * 2 + (row // HD)[None, None, :]) * 4
                    + rt[None, None, :]),
        "own_head": f((rg * 4 + rr)[:, None] == np.arange(16)[None, :]),
        "gmask": f(rg[:, None] == np.arange(4)[None, :]),
        "shift1": np.eye(P, k=-1, dtype=np.float32),
    }


_SCRATCH = [("uT", (N_ROWS, NT)), ("u_tail", (33, 62 * P)), ("u_tok", (P, 4, 14 * P)),
            ("smp", (16, NS, 6 * HD)), ("oaT", (8, P, SEQ)),
            ("oS", (16, NS, HD)), ("obN", (P, 4, 1024)), ("obS", (4, P, HD)), ("kcT", (DEC_B + 1, 2, P, P)), ("vc", (DEC_B + 1, P, 2, P))]


_OUTS = [
    ("yT", (P, KD, NT)),
    ("p_cmp", (SEQ, KVW)), ("p_sel", (SEQ, KVW)), ("p_win", (SEQ, KVW)),
    ("p_rwkv", (16, HD, HD)), ("p_shift", (1, A_COLS)),
    ("s_cmp", (NS, KVW)), ("s_sel", (NS, KVW)), ("s_win", (DEC_B, WINDOW, KVW)),
    ("s_rwkv", (P, HD, HD)), ("s_shift", (DEC_B, A_COLS)),
]
_RESULTS = ["y_prompt", "y_sample"] + [n for n, _ in _OUTS[1:]]
_SHAPES = [
    (1, SEQ, D_MODEL), (DEC_B, DEC_T, D_MODEL),
    (1, 1, SEQ, 2, 4, HD), (1, 1, SEQ, 2, 4, HD), (1, 1, SEQ, 2, 4, HD), (1, 1, 16, HD, HD), (1, 1, A_COLS),
    (1, DEC_B, DEC_T, 2, 4, HD), (1, DEC_B, DEC_T, 2, 4, HD), (1, DEC_B, WINDOW, 2, 4, HD),
    (1, DEC_B, 16, HD, HD), (1, DEC_B, A_COLS),
]


def kernel(**inputs):
    import concourse.bacc as bacc
    from concourse.bass_utils import run_bass_kernel_spmd

    arrays = laid_out({k: np.asarray(v) for k, v in inputs.items()})
    arrays.update(constants())
    nc = bacc.Bacc("TRN2", target_bir_lowering=False, num_devices=1)
    A = {}
    for name, a in arrays.items():
        arrays[name] = a = np.ascontiguousarray(a)
        A[name] = nc.dram_tensor(f"in_{name}", a.shape, mybir.dt.from_np(a.dtype), kind="ExternalInput").ap()
    for name, shape in _OUTS:
        A[name] = nc.dram_tensor(f"out_{name}", shape, F32, kind="ExternalOutput").ap()
    for name, shape in _SCRATCH:
        A[name] = nc.dram_tensor(f"tmp_{name}", shape, F32, kind="Internal").ap()
    program(nc, A)
    r = run_bass_kernel_spmd(nc, [{f"in_{n}": a for n, a in arrays.items()}], core_ids=[0])
    out = {n: np.asarray(r.results[0][f"out_{n}"]) for n, _ in _OUTS}
    out["s_rwkv"] = out["s_rwkv"].reshape(16, DEC_B, HD, HD).transpose(1, 0, 2, 3)
    y = out["yT"].transpose(2, 1, 0).reshape(NT, D_MODEL)
    out["y_prompt"], out["y_sample"] = y[:SEQ], y[SEQ:]
    return tuple(out[n].reshape(s) for n, s in zip(_RESULTS, _SHAPES))
```
